# Optimizing a Trainium2 kernel written in Bass

```python
import jax, jax.numpy as jnp
from jax import lax
import numpy as np

D_MODEL = 1024
BATCH = 1
SEQ = 256
DEPTH = 2

CHUNK = 64
N_EVEN = (DEPTH + 1) // 2
N_ODD = DEPTH // 2
POOL_WINDOWS = (2, 4, 8, 16)
N_POOL_GROUPS = 4
POOL_WIDTH = D_MODEL // 2
POOL_GROUP = POOL_WIDTH // N_POOL_GROUPS
SB_HEAD_DIM = 64
SB_HEADS = (D_MODEL // 2) // SB_HEAD_DIM
SB_WIDTH = SB_HEADS * SB_HEAD_DIM
SB_BLOCK = 128
IN_WIDTH = POOL_WIDTH + 3 * SB_WIDTH
MIX_WIDTH = POOL_WIDTH + SB_WIDTH
RW_HEAD = 64
RW_HEADS = D_MODEL // RW_HEAD
W_LORA = 64
A_LORA = 64
G_LORA = 160
GN_EPS = 64e-5
N_EXPERTS = 64
TOP_K = 8
N_GROUPS = 8
TOPK_GROUPS = 4
EXPERT_FF = 256
SHARED_FF = 256
ROUTED_SCALE = 2.5
MOE_BLOCK = 128
DN_ALPHA = (2.0 * DEPTH) ** 0.25
DN_BETA = (8.0 * DEPTH) ** -0.25
LN_EPS = 1e-5

kernel_name = 'hybrid_pool_stickbreak_rwkv7_moe'

def _layer_norm(x, g, b):
    xf = x.astype(jnp.float32)
    mu = jnp.mean(xf, axis=-1, keepdims=True)
    var = jnp.mean(jnp.square(xf - mu), axis=-1, keepdims=True)
    return ((xf - mu) * lax.rsqrt(var + LN_EPS) * g + b).astype(x.dtype)

def _pool_mixer(u, pool_w, pool_scale):
    b, s, _ = u.shape
    uf = u.astype(jnp.float32).reshape(b, s, N_POOL_GROUPS, POOL_GROUP)
    csum = jnp.concatenate([jnp.zeros((b, 1, N_POOL_GROUPS, POOL_GROUP), jnp.float32),
                            jnp.cumsum(uf, axis=1)], axis=1)
    t = jnp.arange(s)
    means = []
    for g, win in enumerate(POOL_WINDOWS):
        lo = jnp.maximum(t + 1 - win, 0)
        cnt = (t + 1 - lo).astype(jnp.float32)
        window_sum = csum[:, 1:, g] - jnp.take(csum[:, :, g], lo, axis=1)
        means.append(window_sum / cnt[None, :, None])
    pooled = jnp.stack(means, axis=2)
    diff = (pooled - uf).astype(u.dtype)
    y = jnp.einsum('bsgc,gcd->bsgd', diff, pool_w)
    return y.reshape(b, s, POOL_WIDTH) * pool_scale

def _stick_breaking(q, k, v):
    b, h, s, dh = q.shape
    nb = s // SB_BLOCK
    qb = q.astype(jnp.float32).reshape(b, h, nb, SB_BLOCK, dh).transpose(2, 0, 1, 3, 4)
    kf = k.astype(jnp.float32)
    vf = v.astype(jnp.float32)
    key_pos = jnp.arange(s)
    scale = dh ** -0.5

    def block(args):
        qi, bi = args
        z = jnp.einsum('bhqd,bhkd->bhqk', qi, kf) * scale
        q_pos = bi * SB_BLOCK + jnp.arange(SB_BLOCK)
        past = key_pos[None, :] < q_pos[:, None]
        log_fail = jnp.where(past, -jax.nn.softplus(z), 0.0)
        between = lax.cumsum(log_fail, axis=3, reverse=True) - log_fail
        w = jnp.where(past, jnp.exp(jax.nn.log_sigmoid(z) + between), 0.0)
        return jnp.einsum('bhqk,bhkd->bhqd', w, vf)

    o = lax.map(block, (qb, jnp.arange(nb)))
    return o.transpose(1, 2, 0, 3, 4).reshape(b, h, s, dh).astype(q.dtype)

def _even_mixer(x, w_in, pool_w, pool_scale, w_out):
    b, s, _ = x.shape
    hcat = x @ w_in
    u, q, k, v = jnp.split(hcat, [POOL_WIDTH, POOL_WIDTH + SB_WIDTH, POOL_WIDTH + 2 * SB_WIDTH], axis=-1)
    y_pool = _pool_mixer(u, pool_w, pool_scale)
    to_heads = lambda t: t.reshape(b, s, SB_HEADS, SB_HEAD_DIM).transpose(0, 2, 1, 3)
    y_sb = _stick_breaking(to_heads(q), to_heads(k), to_heads(v))
    y_sb = y_sb.transpose(0, 2, 1, 3).reshape(b, s, SB_WIDTH)
    return jnp.concatenate([y_pool, y_sb], axis=-1) @ w_out

def _rwkv7_mixer(x, mu, w_r, w_k, w_v, w_w1, w_w2, w0, a1, a2, a0, g1, g2,
                 k_k, k_a, r_k, lnx_g, lnx_b, w_o):
    b, s, d = x.shape
    hh, n = RW_HEADS, RW_HEAD
    xx = jnp.pad(x, ((0, 0), (1, 0), (0, 0)))[:, :-1] - x
    xr, xw, xk, xv, xa, xg = [x + xx * mu[i] for i in range(6)]
    r = xr @ w_r
    w_log = -jax.nn.softplus(-(w0 + jnp.tanh(xw @ w_w1) @ w_w2)) - 0.5
    k = xk @ w_k
    v = xv @ w_v
    a = jax.nn.sigmoid(a0 + (xa @ a1) @ a2)
    g = jax.nn.sigmoid(xg @ g1) @ g2
    heads = lambda t: t.astype(jnp.float32).reshape(b, s, hh, n)
    kk = heads(k * k_k)
    kk = kk / jnp.maximum(jnp.sqrt(jnp.sum(jnp.square(kk), axis=-1, keepdims=True)), 1e-12)
    k = k * (1.0 + (a - 1.0) * k_a)
    rh, kh, vh, ah = heads(r), heads(k), heads(v), heads(a)
    decay = jnp.exp(-jnp.exp(heads(w_log)))

    def step(state, inp):
        r_t, d_t, k_t, v_t, kk_t, a_t = inp
        sa = jnp.einsum('bhvk,bhk->bhv', state, kk_t)
        state = (state * d_t[:, :, None, :] - sa[..., None] * (kk_t * a_t)[:, :, None, :]
                 + v_t[..., None] * k_t[:, :, None, :])
        return state, jnp.einsum('bhvk,bhk->bhv', state, r_t)

    seq_major = lambda t: jnp.swapaxes(t, 0, 1)
    inputs = (seq_major(rh), seq_major(decay), seq_major(kh), seq_major(vh), seq_major(kk), seq_major(ah))
    _, y = lax.scan(step, jnp.zeros((b, hh, n, n), jnp.float32), inputs)
    y = jnp.swapaxes(y, 0, 1)
    ym = jnp.mean(y, axis=-1, keepdims=True)
    yv = jnp.mean(jnp.square(y - ym), axis=-1, keepdims=True)
    y = ((y - ym) * lax.rsqrt(yv + GN_EPS)).reshape(b, s, d) * lnx_g + lnx_b
    bonus = jnp.sum(rh * kh * r_k, axis=-1, keepdims=True) * vh
    y = (y + bonus.reshape(b, s, d)).astype(x.dtype)
    return (y * g) @ w_o

def _swiglu(h, wg, wu, wd):
    return (jax.nn.silu(h @ wg) * (h @ wu)) @ wd

def _routed_experts(xf, idx, gates, w_gate, w_up, w_down):
    n, d = xf.shape
    n_assign = n * TOP_K
    n_blocks = -(-n_assign // MOE_BLOCK) + N_EXPERTS
    n_slots = n_blocks * MOE_BLOCK
    e_flat = idx.reshape(-1)
    tok_flat = jnp.repeat(jnp.arange(n, dtype=jnp.int32), TOP_K)
    g_flat = gates.reshape(-1)
    order = jnp.argsort(e_flat)
    e_sorted = e_flat[order]
    counts = jnp.zeros((N_EXPERTS,), jnp.int32).at[e_flat].add(1)
    padded = (counts + MOE_BLOCK - 1) // MOE_BLOCK * MOE_BLOCK
    start = jnp.cumsum(counts) - counts
    pad_end = jnp.cumsum(padded)
    pad_start = pad_end - padded
    dest = pad_start[e_sorted] + (jnp.arange(n_assign, dtype=jnp.int32) - start[e_sorted])
    slot_tok = jnp.full((n_slots,), n, jnp.int32).at[dest].set(tok_flat[order])
    slot_gate = jnp.zeros((n_slots,), jnp.float32).at[dest].set(g_flat[order])
    block_start = jnp.arange(n_blocks, dtype=jnp.int32) * MOE_BLOCK
    block_expert = jnp.minimum(jnp.searchsorted(pad_end, block_start, side='right'), N_EXPERTS - 1)
    x_pad = jnp.concatenate([xf, jnp.zeros((1, d), xf.dtype)], axis=0)
    xs = x_pad[slot_tok].reshape(n_blocks, MOE_BLOCK, d)

    def expert_block(args):
        xb, e = args
        return _swiglu(xb, w_gate[e], w_up[e], w_down[e])

    ys = lax.map(expert_block, (xs, block_expert)).reshape(n_slots, d)
    ys = ys.astype(jnp.float32) * slot_gate[:, None]
    out = jnp.zeros((n + 1, d), jnp.float32).at[slot_tok].add(ys)[:n]
    return out.astype(xf.dtype)

def _moe(x, w_router, e_bias, w_gate, w_up, w_down, ws_gate, ws_up, ws_down):
    b, s, d = x.shape
    xf = x.reshape(b * s, d)
    n = xf.shape[0]
    scores = jax.nn.sigmoid((xf @ w_router).astype(jnp.float32))
    biased = scores + e_bias
    grp_score = jnp.sum(lax.top_k(biased.reshape(n, N_GROUPS, N_EXPERTS // N_GROUPS), 2)[0], axis=-1)
    _, top_grp = lax.top_k(grp_score, TOPK_GROUPS)
    grp_mask = jnp.any(top_grp[:, :, None] == jnp.arange(N_GROUPS)[None, None, :], axis=1)
    expert_mask = jnp.repeat(grp_mask, N_EXPERTS // N_GROUPS, axis=1)
    _, idx = lax.top_k(jnp.where(expert_mask, biased, -jnp.inf), TOP_K)
    sel = jnp.take_along_axis(scores, idx, axis=1)
    gates = sel / jnp.sum(sel, axis=-1, keepdims=True) * ROUTED_SCALE
    routed = _routed_experts(xf, idx, gates, w_gate, w_up, w_down)
    shared = _swiglu(xf, ws_gate, ws_up, ws_down)
    return (routed + shared).reshape(b, s, d)

def setup_inputs(seed: int = 0) -> dict:
    key = jax.random.key(seed)
    ks = iter(jax.random.split(key, 48))
    f32 = jnp.float32
    nrm = lambda shape, sc: sc * jax.random.normal(next(ks), shape, f32)
    uni = lambda shape, lo, hi: jax.random.uniform(next(ks), shape, f32, lo, hi)
    D = D_MODEL
    return {
        'x': nrm((BATCH, SEQ, D), 1.0),
        'ln_mix_g': 1.0 + nrm((DEPTH, D), 0.05),
        'ln_mix_b': nrm((DEPTH, D), 0.01),
        'ln_ffn_g': 1.0 + nrm((DEPTH, D), 0.05),
        'ln_ffn_b': nrm((DEPTH, D), 0.01),
        'ab_w_in': nrm((N_EVEN, D, IN_WIDTH), D ** -0.5),
        'ab_pool_w': nrm((N_EVEN, N_POOL_GROUPS, POOL_GROUP, POOL_GROUP), POOL_GROUP ** -0.5),
        'ab_pool_scale': 1.0 + nrm((N_EVEN, POOL_WIDTH), 0.1),
        'ab_w_out': nrm((N_EVEN, MIX_WIDTH, D), DN_BETA * MIX_WIDTH ** -0.5),
        'rw_mu': uni((N_ODD, 6, D), 0.0, 1.0),
        'rw_w_r': nrm((N_ODD, D, D), D ** -0.5),
        'rw_w_k': nrm((N_ODD, D, D), D ** -0.5),
        'rw_w_v': nrm((N_ODD, D, D), D ** -0.5),
        'rw_w_w1': nrm((N_ODD, D, W_LORA), D ** -0.5),
        'rw_w_w2': nrm((N_ODD, W_LORA, D), 0.5 * W_LORA ** -0.5),
        'rw_w0': uni((N_ODD, D), -6.0, -1.0),
        'rw_a1': nrm((N_ODD, D, A_LORA), D ** -0.5),
        'rw_a2': nrm((N_ODD, A_LORA, D), 0.5 * A_LORA ** -0.5),
        'rw_a0': nrm((N_ODD, D), 0.5),
        'rw_g1': nrm((N_ODD, D, G_LORA), D ** -0.5),
        'rw_g2': nrm((N_ODD, G_LORA, D), G_LORA ** -0.5),
        'rw_k_k': 0.85 + nrm((N_ODD, D), 0.05),
        'rw_k_a': 1.0 + nrm((N_ODD, D), 0.05),
        'rw_r_k': nrm((N_ODD, RW_HEADS, RW_HEAD), 0.1),
        'rw_lnx_g': 1.0 + nrm((N_ODD, D), 0.05),
        'rw_lnx_b': nrm((N_ODD, D), 0.01),
        'rw_w_o': nrm((N_ODD, D, D), DN_BETA * D ** -0.5),
        'moe_w_router': nrm((DEPTH, D, N_EXPERTS), D ** -0.5),
        'moe_e_bias': nrm((DEPTH, N_EXPERTS), 0.01),
        'moe_w_gate': nrm((DEPTH, N_EXPERTS, D, EXPERT_FF), D ** -0.5),
        'moe_w_up': nrm((DEPTH, N_EXPERTS, D, EXPERT_FF), D ** -0.5),
        'moe_w_down': nrm((DEPTH, N_EXPERTS, EXPERT_FF, D), DN_BETA * EXPERT_FF ** -0.5),
        'moe_ws_gate': nrm((DEPTH, D, SHARED_FF), D ** -0.5),
        'moe_ws_up': nrm((DEPTH, D, SHARED_FF), D ** -0.5),
        'moe_ws_down': nrm((DEPTH, SHARED_FF, D), DN_BETA * SHARED_FF ** -0.5),
    }

def reference(x, ln_mix_g, ln_mix_b, ln_ffn_g, ln_ffn_b,
              ab_w_in, ab_pool_w, ab_pool_scale, ab_w_out,
              rw_mu, rw_w_r, rw_w_k, rw_w_v, rw_w_w1, rw_w_w2, rw_w0, rw_a1, rw_a2, rw_a0,
              rw_g1, rw_g2, rw_k_k, rw_k_a, rw_r_k, rw_lnx_g, rw_lnx_b, rw_w_o,
              moe_w_router, moe_e_bias, moe_w_gate, moe_w_up, moe_w_down,
              moe_ws_gate, moe_ws_up, moe_ws_down):
    for layer in range(DEPTH):
        i = layer // 2
        if layer % 2 == 0:
            mix = _even_mixer(x, ab_w_in[i], ab_pool_w[i], ab_pool_scale[i], ab_w_out[i])
        else:
            mix = _rwkv7_mixer(x, rw_mu[i], rw_w_r[i], rw_w_k[i], rw_w_v[i], rw_w_w1[i], rw_w_w2[i],
                               rw_w0[i], rw_a1[i], rw_a2[i], rw_a0[i], rw_g1[i], rw_g2[i],
                               rw_k_k[i], rw_k_a[i], rw_r_k[i], rw_lnx_g[i], rw_lnx_b[i], rw_w_o[i])
        x = _layer_norm(DN_ALPHA * x + mix, ln_mix_g[layer], ln_mix_b[layer])
        ff = _moe(x, moe_w_router[layer], moe_e_bias[layer], moe_w_gate[layer], moe_w_up[layer],
                  moe_w_down[layer], moe_ws_gate[layer], moe_ws_up[layer], moe_ws_down[layer])
        x = _layer_norm(DN_ALPHA * x + ff, ln_ffn_g[layer], ln_ffn_b[layer])
    return x


_drawn_inputs = setup_inputs


def setup_inputs(seed=0):
    import zlib

    import numpy as np

    out = dict(_drawn_inputs(seed))
    spreads = {}
    factors = {'rw_w_w1': 3.828, 'rw_w_w2': 3.507, 'rw_k_k': 3.101, 'rw_lnx_b': 7.701}
    for name, (base, spread) in spreads.items():
        noise = np.random.default_rng([zlib.crc32(name.encode()), seed]).standard_normal(out[name].shape)
        drawn = base * np.exp(spread * noise) if base else spread * noise
        out[name] = __import__('jax').numpy.asarray(drawn.astype(out[name].dtype))
    for name, factor in factors.items():
        out[name] = (out[name] * factor).astype(out[name].dtype)
    return out
```

```python
import math
from contextlib import ExitStack

import numpy as np

import concourse.bass as bass
from concourse import mybir

P = 128
D = 1024
T = 256
TT = T // P
KT = D // P
E = 64
FF = 256
FT = FF // P
NG = 8
GE = E // NG
TOPG = 4
B = 64
NR = T // B - 1
NOV = T * 8 // B
PAIRS = E // 2
H0 = 8
HD = 64
CH = 64
NCH = T // CH
ALPHA = 4.0 ** 0.25
LN_EPS = 1e-5
GN_EPS = 64e-5
CDEC = math.exp(-0.5)
BIG = 1.0e30
CB = 256
STOP = 4

F32 = mybir.dt.float32
I32 = mybir.dt.int32
BF16 = mybir.dt.bfloat16
ALU = mybir.AluOpType
ACT = mybir.ActivationFunctionType
AX = mybir.AxisListType.X
ds = bass.ds


class Link:

    def __init__(self, eng, sem):
        self.eng, self.sem, self.base, self.n = eng, sem, 0, 0

    def __call__(self, ins):
        ins.then_inc(self.sem, 1)
        self.n += 1

    def sync(self):
        self.eng.wait_ge(self.sem, self.base + self.n)

    def enter(self, i, first, per):
        self.start, self.per = self.base + self.n, per
        self.base, self.n = self.start + (i - first) * per, 0

    def leave(self, count):
        assert self.n == self.per, (self.n, self.per)
        self.base, self.n = self.start + count * self.per, 0


def program(nc, a):
    ctx = ExitStack()
    with ctx:
        def sb(name, shape, dt=F32):
            return ctx.enter_context(nc.sbuf_tensor(name, shape, dt))

        def sem(name):
            return ctx.enter_context(nc.semaphore(name))

        X = sb("X", [P, TT, D])
        xT = sb("xT", [P, KT, T])
        GB = sb("GB", [P, 2, D])
        RING = sb("RING", [P, 3, 6144])
        WR = sb("WR", [P, 2, KT, E])
        EB = sb("EB", [P, 2, E])
        ident = sb("ident", [P, P])
        ones = sb("ones", [P, P])
        before = sb("before", [P, P])
        bones = sb("bones", [P, P])
        iotab = sb("iotab", [P, B])
        tri8 = sb("tri8", [P, NG, NG])
        MK = sb("MK", [P, 2, P])
        LM = sb("LM", [P, 6, P])
        m01 = sb("m01", [P, T])
        MU = sb("MU", [P, 6, KT])
        VEC = sb("VEC", [P, 8, KT])
        V_W0, V_A0, V_KK, V_KA, V_RK, V_LG, V_LB, V_1KA = range(8)
        thr = sb("thr", [P, NR])
        rbase = sb("rbase", [P, NR])
        iotap = sb("iotap", [P, NOV])
        ecol = sb("ecol", [P, 1])
        ioi = sb("ioi", [P, T + 1], I32)
        elist = sb("elist", [1, NOV], I32)
        stat = sb("stat", [P, 2, 6])
        mv = sb("mv", [P, 4])
        cnti = sb("cnti", [1, 4], I32)
        AFL = 24960
        AR = sb("AR", [P, AFL])
        PS = ctx.enter_context(nc.psum_tensor("PS", [P, 8, 512], F32))

        class Area:
            def __init__(self, buf, at=0, end=None):
                self.buf, self.at, self.end = buf, at, end

            def __call__(self, *shape):
                n = int(np.prod(shape))
                v = self.buf[:, self.at:self.at + n]
                self.at += n
                assert self.at <= self.end, (self.at, self.end)
                if len(shape) == 1:
                    return v
                names = "abcd"[:len(shape)]
                return v.rearrange(f"p ({' '.join(names)}) -> p {' '.join(names)}",
                                   **{c: s for c, s in zip(names, shape)})

        flat = RING[:, :, :].rearrange("p s f -> p (s f)")
        am = Area(AR, 0, AFL)
        odd = am(2, 6144)

        def wslot(s):
            w = RING[:, s + 1, :] if s < 2 else odd[:, s - 2, :]
            return (w[:, 0:2048].rearrange("p (k f) -> p k f", k=KT),
                    w[:, 2048:4096].rearrange("p (k f) -> p k f", k=KT),
                    w[:, 4096:6144].rearrange("p (k f) -> p k f", k=FT))

        SCO = am(TT, E)
        BIA = am(TT, E)
        top2 = am(TT * NG, 8)
        grp = am(TT, NG)
        cmpa = am(TT, NG, NG)
        cmpb = am(TT, NG, NG)
        gcnt = am(TT, NG)
        gpen = am(TT, NG)
        MSK = am(TT, E)
        REP = am(TT, E)
        top8 = am(TT, 8)
        SEL = am(TT, E)
        gsum = am(TT)
        RKX = am(TT, E + NOV)
        GX = am(TT, E + NOV)
        HS = am(FT, T)
        HSs = am(FT, T)
        XB = am(3 * TT * D // 2).bitcast(BF16).rearrange("p (n t d) -> p n t d", n=3, t=TT)
        XR = am(TT * D)
        SEL1 = am(2 * TT * B).bitcast(BF16).rearrange("p (u t s b) -> p u t s b", u=2, t=TT, s=2)
        SELG = am(2, TT, 2, B)
        XG = am(KT, 2 * B)
        SIL = am(FF)
        HH = am(FF)
        HT = am(FT, 2 * B)
        GT = am(TT, P)
        Y = am(D)
        F1 = am(3, NR)
        OH = am(NR, NOV)
        OS = am(2, NOV)
        TR4 = am(4, P)
        F2 = am(E)
        CNT = am(E)
        cntf = am(2)
        ax = Area(AR, 0, AFL)
        WB = ax(2, 2048)
        mix0 = ax.at
        a0_ = Area(AR, mix0, AFL)
        UQK = a0_(12, T)
        V0 = a0_(TT, 512)
        CAT = a0_(KT, T)
        ZM = a0_(H0, T)
        BET = a0_(H0, T)
        FFT = a0_(H0, T + 1)
        IPR = a0_(H0, T + 1)
        Z1 = a0_(H0, T + 1)
        WT = a0_(2 * H0, P)
        MQ = a0_(TT, T)
        a0b = Area(flat, 12288, 18432)
        PW = a0b(4, P)
        PSC = a0b(4)
        WS1 = a0b(4, T)
        WS2 = a0b(4, T)
        ICN = a0b(4, T)
        DIF = a0b(4, T)
        a1_ = Area(AR, mix0, AFL)
        RT = a1_(KT, T)
        KTT = a1_(KT, T)
        V1 = a1_(TT, D)
        AT = a1_(KT, T)
        GTT = a1_(KT, T)
        SG = a1_(KT, T)
        g2b = a1_(D)
        l1x = a1_.at
        XX = a1_(KT, T)
        XM = a1_(2, KT, T)
        a1s = Area(flat, 12288, 18432)
        w1 = a1s(KT, 64)
        a1w = a1s(KT, 64)
        g1 = a1s(KT, 160)
        w2 = a1s(D)
        a2 = a1s(D)
        g2a = a1s(D)
        LH = a1_(4, T)
        ap_ = Area(AR, l1x, l1x + 6144)
        KR = ap_(TT, 2, P)
        BI = ap_(T)
        KI = ap_(T)
        BKT = ap_(2, TT, P)
        VT = ap_(T)
        VP = ap_(TT, P)
        R1 = ap_(TT, P)
        UU = ap_(TT, P)
        SS = ap_(NCH, P)
        SD = ap_(P)
        XI = ap_(4, P)
        DG = ap_(4, P)
        DT = ap_(4, P)
        YY = ap_(T)
        YC = ap_(T)
        YQ = ap_(T)
        BON = ap_(T)
        aq_ = Area(flat, 12288, 18432)
        MP = aq_(2, TT, 2, P)
        NQ = aq_(2, TT, 2, P)
        E1 = aq_(T)
        E2 = aq_(T)
        E3 = aq_(T)
        LC = aq_(T)
        LCX = aq_(T)
        KKR = aq_(T)
        SQ = aq_(T)
        KK = aq_(T)
        KM = aq_(T)
        TMP = aq_(T)
        LVL = Area(AR, AFL - 512, AFL)(4, P)

        s_const = sem("constants_ready")
        s_g2d = sem("gpsimd_steps")
        s_dve = sem("vector_steps")
        s_act = sem("scalar_steps")
        s_vec = sem("vectors_loaded")
        s_x = sem("x_loaded")
        s_gb = sem("ln_params_loaded")
        s_ln = sem("ln_done")
        s_var = sem("ln_variance_ready")
        s_std = sem("ln_deviation_ready")
        s_tr = sem("x_transposed")
        s_xT = sem("xT_ready")
        s_wl = [sem(f"mixer_chunk_loaded{b}") for b in range(2)]
        s_wf = sem("mixer_chunk_used")
        s_pj = sem("projection_done")
        s_pe = sem("projection_copied")
        s_res = sem("residual_done")
        s_out = sem("out_stored")

        def dve_transpose_copy(v, st):
            for n in range(4):
                if n % 2 == 0:
                    v.wait_ge(s_tr, 4 * st + n + 1)
                    nc.vector.tensor_copy(xT[:, 4 * (n % 2):4 * (n % 2) + 4, P * (n // 2):P * (n // 2) + P],
                                          PS[:, 4 + n, :].rearrange("p (k t) -> p k t", k=4)).then_inc(s_xT, 1)

        def act_transpose_copy(s, st):
            for n in range(4):
                if n % 2 == 1:
                    s.wait_ge(s_tr, 4 * st + n + 1)
                    nc.scalar.copy(xT[:, 4 * (n % 2):4 * (n % 2) + 4, P * (n // 2):P * (n // 2) + P],
                                   PS[:, 4 + n, :].rearrange("p (k t) -> p k t", k=4)).then_inc(s_xT, 1)

        def pe_transpose(pe, st):
            if st == 0:
                pe.wait_ge(s_x, 16)
                pe.wait_ge(s_const, 1)
            else:
                pe.wait_ge(s_ln, TT * st)
            for n in range(4):
                for k in range(4):
                    ins = nc.tensor.transpose(PS[:, 4 + n, k * P:(k + 1) * P],
                                              X[:, n // 2, (4 * (n % 2) + k)::KT], ident[:, :])
                ins.then_inc(s_tr, 1)

        def layer_norm(v, link, st):
            v.wait_ge(s_res, st + 1)
            v.wait_ge(s_gb, 32 * (st + 1))
            for t in range(TT):
                for h in range(2):
                    link(nc.vector.scalar_tensor_tensor(out=X[:, t, 512 * h:512 * h + 512],
                                                        in0=X[:, t, 512 * h:512 * h + 512], scalar=ALPHA,
                                                        in1=PS[:, 2 * t + h, :], op0=ALU.mult, op1=ALU.add))
                link.sync()
                for h in range(2):
                    link(nc.vector.bn_stats(stat[:, h, :], X[:, t, 512 * h:512 * h + 512]))
                link.sync()
                link(nc.vector.bn_aggr(mv[:, 0:2], stat[:, :, :]))
                link.sync()
                nc.vector.tensor_scalar(mv[:, 3:4], mv[:, 1:2], LN_EPS, None, ALU.add).then_inc(s_var, 1)
                v.wait_ge(s_std, TT * st + t + 1)
                link(nc.vector.reciprocal(mv[:, 2:3], mv[:, 3:4]))
                link.sync()
                link(nc.vector.tensor_scalar(X[:, t, :], X[:, t, :], mv[:, 0:1], mv[:, 2:3], ALU.subtract, ALU.mult))
                link.sync()
                link(nc.vector.tensor_tensor(X[:, t, :], X[:, t, :], GB[:, 0, :], ALU.mult))
                link.sync()
                nc.vector.tensor_tensor(X[:, t, :], X[:, t, :], GB[:, 1, :], ALU.add).then_inc(s_ln, 1)

        def act_ln(s, st):
            for t in range(TT):
                s.wait_ge(s_var, TT * st + t + 1)
                nc.scalar.activation(mv[:, 3:4], mv[:, 3:4], ACT.Sqrt).then_inc(s_std, 1)

        def load_ln(sp, st):
            g, b = (a["ln_mix_g"], a["ln_mix_b"]) if st % 2 == 0 else (a["ln_ffn_g"], a["ln_ffn_b"])
            l = st // 2
            if st:
                sp.wait_ge(s_ln, TT * st)
            sp.dma_start(GB[:, 0, :], g[l:l + 1, :].to_broadcast([P, D])).then_inc(s_gb, 16)
            sp.dma_start(GB[:, 1, :], b[l:l + 1, :].to_broadcast([P, D])).then_inc(s_gb, 16)

        def chunk(i):
            return WB[:, i % 2, :].rearrange("p (k c) -> p k c", k=KT)

        def load_chunk(sp, src, b, c):
            sp.dma_start(chunk(b), src[:, :, ds(c * CB, CB)]).then_inc(s_wl[b], 16)

        def stream(sp, src, n0, tile0, count):
            lead = 1 if n0 == 0 else 0
            for b in range(2 * lead):
                load_chunk(sp, src, b, b)
            with sp.Fori(lead, count // 2) as i:
                for b in range(2):
                    sp.wait_ge(s_pj, 4 * i + (tile0 + 2 * (n0 + b) - 2))
                    load_chunk(sp, src, b, 2 * i + b)

        def stream_out(sp, src, l, n0, tile0):
            for c in range(4):
                if c < 2:
                    sp.wait_ge(s_pj, tile0 + 2 * (n0 + c) - 2)
                else:
                    sp.wait_ge(s_wf, 4 * l + c - 1)
                load_chunk(sp, src, c % 2, c)

        def project_channels(pe, x, base, chunks, tile0):
            with pe.Fori(0, chunks // 2) as i:
                for b in range(2):
                    pe.wait_ge(s_wl[b], 16 * i + 16 * (base // 2 + 1))
                    for c in range(2):
                        pe.wait_ge(s_pe, 4 * i + (tile0 + 2 * b + c + 1))
                        for k in range(KT):
                            ins = nc.tensor.matmul(PS[:, 4 + 2 * b + c, 0:T], chunk(b)[:, k, c * P:(c + 1) * P],
                                                   x[:, k, :], start=(k == 0), stop=(k == KT - 1))
                        ins.then_inc(s_pj, 1)

        def project_tokens(pe, x, base, chunks, tile0):
            with pe.Fori(0, chunks // 2) as i:
                for b in range(2):
                    pe.wait_ge(s_wl[b], 16 * i + 16 * (base // 2 + 1))
                    for t in range(TT):
                        pe.wait_ge(s_pe, 4 * i + (tile0 + 2 * b + t + 1))
                        for k in range(KT):
                            ins = nc.tensor.matmul(PS[:, 4 + 2 * b + t, 0:CB], x[:, k, t * P:(t + 1) * P],
                                                   chunk(b)[:, k, :], start=(k == 0), stop=(k == KT - 1))
                        ins.then_inc(s_pj, 1)

        def out_project(pe, x, base, l):
            for c in range(4):
                g = base + c
                pe.wait_ge(s_wl[g % 2], 16 * (g // 2 + 1))
                for t in range(TT):
                    for k in range(KT):
                        ins = nc.tensor.matmul(PS[:, 2 * t + c // 2, (c % 2) * CB:(c % 2) * CB + CB],
                                               x[:, k, t * P:(t + 1) * P], chunk(g)[:, k, :],
                                               start=(k == 0), stop=(k == KT - 1))
                ins.then_inc(s_wf, 1)
            pe.wait_ge(s_wf, 4 * l + 4)
            pe.sem_inc(s_res, 1)

        def copy_tiles(s, dst, tile0, iters):
            with s.Fori(0, iters) as i:
                for n in range(4):
                    s.wait_ge(s_pj, 4 * i + (tile0 + n + 1))
                    nc.scalar.copy(dst[:, ds(4 * i + n, 1), :], PS[:, 4 + n:5 + n, 0:T]).then_inc(s_pe, 1)

        def constants(g):
            link = Link(g, s_g2d)
            L.append(link)

            def keep(dst, pattern, base, mult, op, fill=0.0):
                link(nc.gpsimd.affine_select(out=dst, in_=dst, compare_op=op, fill=fill, base=base,
                                             pattern=pattern, channel_multiplier=mult))

            link(nc.gpsimd.memset(ident[:, :], 0.0))
            link.sync()
            keep(ident[:, :], [[-1, P]], 0, 1, ALU.not_equal, 1.0)
            link.sync()
            g.sem_inc(s_const, 1)
            for dst, val in ((ones[:, :], 1.0), (before[:, :], 1.0), (bones[:, :], 0.0),
                             (tri8[:, :, :], 1.0), (MK[:, :, :], 1.0), (LM[:, :, :], 1.0), (m01[:, :], 1.0),
                             (Z1[:, :, :], 0.0), (FFT[:, :, T:T + 1], 0.0), (MQ[:, :, :], 0.0)):
                link(nc.gpsimd.memset(dst, val))
            link(nc.gpsimd.iota(ioi[:, 0:T], pattern=[[1, T]], base=0, channel_multiplier=0))
            link(nc.gpsimd.iota(ioi[:, T:T + 1], pattern=[[1, 1]], base=0, channel_multiplier=1))
            link.sync()

            keep(before[:, :], [[1, P]], 0, -1, ALU.is_gt)
            keep(tri8[:, :, :], [[1, NG], [-1, NG]], 0, 0, ALU.is_gt)
            keep(MK[:, 0, :], [[1, P]], 0, -1, ALU.is_gt)
            keep(MK[:, 1, :], [[1, P]], 0, -1, ALU.is_ge)
            for q in range(TT):
                keep(MQ[:, q, :], [[-1, T]], q * P, 1, ALU.is_gt, -BIG)
            link.sync()
            for c in range(2):
                link(nc.gpsimd.memset(bones[c * HD:(c + 1) * HD, c * HD:(c + 1) * HD], 1.0))
                link.sync()
            for c in range(NCH):
                link(nc.gpsimd.memset(m01[:, c * CH:c * CH + 1], 0.0))
            link(nc.gpsimd.memset(Z1[:, :, T:T + 1], 1.0))
            link.sync()
            link(nc.gpsimd.memset(MK[0:CH, :, CH:P], 0.0))
            link.sync()
            for lv in range(6):
                w = 1 << lv
                nb = P // (2 * w)
                v = LM[:, lv, :].rearrange("p (n t) -> p n t", t=2 * w)
                lo, hi = v[:, :, 0:w], v[:, :, w:2 * w]
                link(nc.gpsimd.memset(lo, 0.0))
                for pattern, base, mult in (([[-2 * w, nb], [0, w]], 0, 1), ([[2 * w, nb], [0, w]], w - 1, -1)):
                    keep(hi, pattern, base, mult, ALU.is_ge)
                    link.sync()
            for g_, win in enumerate((2, 4, 8, 16)):
                link(nc.gpsimd.tensor_scalar(ICN[:, g_, :], ioi[:, 0:T], 1.0, float(win), ALU.add, ALU.min))
            link(nc.gpsimd.tensor_copy(iotab[:, :], ioi[:, 0:B]))
            link(nc.gpsimd.tensor_copy(iotap[:, :], ioi[:, 0:NOV]))
            link(nc.gpsimd.tensor_copy(ecol[:, :], ioi[:, T:T + 1]))
            link(nc.gpsimd.tensor_scalar(thr[:, :], ioi[:, 1:NR + 1], float(B), None, ALU.mult))
            link(nc.gpsimd.tensor_scalar(rbase[:, :], ioi[:, 1:NR + 1], -float(B), 1.0, ALU.mult, ALU.add))
            link.sync()
            g.sem_inc(s_const, 1)

        L = []

        s_pw = sem("pool_weights_loaded")
        s_dif = sem("pool_differences_ready")
        s_yp = sem("pool_product_done")
        s_cat = sem("mixed_heads_ready")
        s_z = sem("scores_done")
        s_zm = sem("masked_scores_ready")
        s_sig = sem("sigmoids_ready")
        s_w = sem("stick_weights_ready")
        s_wt = sem("stick_weights_transposed")
        s_wtc = sem("stick_weights_copied")
        s_o = sem("heads_done")
        s_l0c = sem("layer0_constants_ready")
        L0CH = 8 + 4
        w_in = a["ab_w_in"][0].rearrange("(p k) c -> p k c", k=KT)
        w_out = a["ab_w_out"][0].rearrange("(k p) c -> p k c", p=P)

        def sp_mix0(sp):
            sp.dma_start(X[:, :, :], a["x"][0].rearrange("(t p) d -> p t d", p=P)).then_inc(s_x, 16)
            stream(sp, w_in, 0, 0, 8)
            sp.dma_start(PW[:, :, :], a["ab_pool_w"][0].rearrange("g c d -> c g d")).then_inc(s_pw, 16)
            with nc.allow_non_contiguous_dma(reason="a few short vectors"):
                sp.dma_start(PSC[:, :], a["ab_pool_scale"][0].rearrange("(g p) -> p g", p=P)).then_inc(s_pw, 16)
            load_ln(sp, 0)
            sp.dma_start(WR[:, :, :, :], a["moe_w_router"].rearrange("l (p k) e -> p l k e", k=KT)).then_inc(s_vec, 16)
            sp.dma_start(EB[:, :, :].rearrange("p l e -> p (l e)"),
                         a["moe_e_bias"].rearrange("(o l) e -> o (l e)", o=1).to_broadcast([P, 2 * E])).then_inc(s_vec, 16)
            with nc.allow_non_contiguous_dma(reason="a few short vectors"):
                sp.dma_start(MU[:, :, :], a["rw_mu"][0].rearrange("m (p k) -> p m k", k=KT)).then_inc(s_vec, 16)
                for n, name in enumerate(["rw_w0", "rw_a0", "rw_k_k", "rw_k_a", "rw_r_k", "rw_lnx_g", "rw_lnx_b"]):
                    v = a[name][0] if name != "rw_r_k" else a[name][0].rearrange("h n -> (h n)")
                    sp.dma_start(VEC[:, n, :], v.rearrange("(k p) -> p k", p=P)).then_inc(s_vec, 16)
            stream_out(sp, w_out, 0, 8, 0)

        def gp_mix0(g):
            link_g = L[0]
            g.wait_ge(s_l0c, 1)
            g.wait_ge(s_pe, 4 + 4)
            src, w = UQK[:, 0:4, :], 1
            for lv, dst in enumerate([WS1, WS2, WS1, WS2]):
                link_g(nc.gpsimd.tensor_tensor(dst[:, lv:4, w:T], src[:, lv:4, w:T], src[:, lv:4, 0:T - w], ALU.add))
                link_g(nc.gpsimd.tensor_copy(dst[:, lv:4, 0:w], src[:, lv:4, 0:w]))
                link_g.sync()
                link_g(nc.gpsimd.tensor_tensor(DIF[:, lv, :], dst[:, lv, :], ICN[:, lv, :], ALU.mult))
                link_g.sync()
                nc.gpsimd.tensor_tensor(DIF[:, lv, :], DIF[:, lv, :], UQK[:, lv, :], ALU.subtract).then_inc(s_dif, 1)
                src, w = dst, 2 * w

        def pe_mix0(pe):
            pe_transpose(pe, 0)
            pe.wait_ge(s_xT, 4)
            project_channels(pe, xT, 0, 6, 0)
            project_tokens(pe, xT, 6, 2, 12)
            pe.wait_ge(s_pw, 32)
            pe.wait_ge(s_dif, 4)
            for g in range(4):
                ins = nc.tensor.matmul(PS[:, g // 2, (g % 2) * T:(g % 2) * T + T], PW[:, g, :], DIF[:, g, :],
                                       start=True, stop=True)
            ins.then_inc(s_yp, 1)
            pe.wait_ge(s_pe, 4 + 16)
            for q in range(TT):
                if q:
                    pe.wait_ge(s_cat, 4 + 1)
                for h in range(H0):
                    r = HD * (h % 2)
                    n = 4 * (h % 2) + h // 2
                    ins = nc.tensor.matmul(PS[:, 4 + n // 2, (n % 2) * T:(n % 2) * T + T],
                                           UQK[r:r + HD, 4 + h // 2, q * P:(q + 1) * P],
                                           UQK[r:r + HD, 8 + h // 2, :], start=True, stop=True)
                ins.then_inc(s_z, 1)
                pe.wait_ge(s_w, q + 1)
                if q == 0:
                    pe.wait_ge(s_cat, 4)
                for n in range(H0):
                    for k in range(TT):
                        m = 2 * n + k
                        ins = nc.tensor.transpose(PS[:, m // 4, (m % 4) * P:(m % 4) * P + P],
                                                  BET[:, n, k * P:(k + 1) * P], ident[:, :])
                ins.then_inc(s_wt, 1)
                pe.wait_ge(s_wtc, q + 1)
                for h in range(H0):
                    n = 4 * (h % 2) + h // 2
                    r = HD * (h % 2)
                    for k in range(TT):
                        ins = nc.tensor.matmul(PS[r:r + HD, 4, (h // 2) * P:(h // 2) * P + P],
                                               V0[:, k, h * HD:(h + 1) * HD], WT[:, 2 * n + k, :],
                                               start=(k == 0), stop=(k == TT - 1))
                ins.then_inc(s_o, 1)
            pe.wait_ge(s_cat, 4 + 2)
            out_project(pe, CAT, 8, 0)

        def act_mix0(s):
            s.sem_inc(s_pe, 4)
            act_transpose_copy(s, 0)
            s.wait_ge(s_xT, 4)
            copy_tiles(s, UQK, 0, 3)
            for n in range(4):
                s.wait_ge(s_pj, 12 + n + 1)
                nc.scalar.copy(V0[:, n % 2, (n // 2) * CB:(n // 2) * CB + CB], PS[:, 4 + n, 0:CB]).then_inc(s_pe, 1)
            s.wait_ge(s_yp, 1)
            for g in range(4):
                nc.scalar.activation(CAT[:, g, :], PS[:, g // 2, (g % 2) * T:(g % 2) * T + T], ACT.Copy,
                                     scale=PSC[:, g:g + 1]).then_inc(s_cat, 1)
            for q in range(TT):
                s.wait_ge(s_zm, 4 * (q + 1))
                if q:
                    s.wait_ge(s_wt, q)
                nc.scalar.activation(FFT[:, :, 0:T], ZM[:, :, :], ACT.Sigmoid, scale=-1.0).then_inc(s_sig, 1)
                nc.scalar.activation(BET[:, :, :], ZM[:, :, :], ACT.Sigmoid).then_inc(s_sig, 1)
                s.wait_ge(s_wt, q + 1)
                for n in range(4):
                    ins = nc.scalar.copy(WT[:, 4 * n:4 * n + 4, :], PS[:, n, :].rearrange("p (m q) -> p m q", m=4))
                ins.then_inc(s_wtc, 1)
                s.wait_ge(s_o, q + 1)
                nc.scalar.copy(CAT[:, 4:8, q * P:(q + 1) * P],
                               PS[:, 4, :].rearrange("p (m q) -> p m q", m=4)).then_inc(s_cat, 1)

        def dve_mix0(v, link):
            v.wait_ge(s_const, 2)
            nc.vector.reciprocal(ICN[:, :, :], ICN[:, :, :]).then_inc(s_l0c, 1)
            dve_transpose_copy(v, 0)
            for q in range(TT):
                v.wait_ge(s_z, q + 1)
                if q:
                    v.wait_ge(s_sig, 2 * q)
                for n in range(4):
                    nc.vector.scalar_tensor_tensor(
                        out=ZM[:, 2 * n:2 * n + 2, :], in0=PS[:, 4 + n, :].rearrange("p (h k) -> p h k", h=2),
                        scalar=HD ** -0.5, in1=MQ[:, q:q + 1, :].to_broadcast([P, 2, T]),
                        op0=ALU.mult, op1=ALU.add).then_inc(s_zm, 1)
                v.wait_ge(s_sig, 2 * q + 1)
                fl = lambda m: m.rearrange("p h k -> p (h k)")[:, ::-1]
                link(nc.vector.tensor_tensor_scan(out=fl(IPR), data0=fl(FFT), data1=fl(Z1), initial=1.0,
                                                  op0=ALU.mult, op1=ALU.add))
                link.sync()
                v.wait_ge(s_sig, 2 * q + 2)
                nc.vector.tensor_tensor(BET[:, :, :], BET[:, :, :], IPR[:, :, 1:T + 1], ALU.mult).then_inc(s_w, 1)

        s_lw = sem("lora_weights_loaded")
        s_xx = sem("shift_difference_ready")
        s_xm = sem("mixed_input_ready")
        s_lh = sem("lora_hidden_done")
        s_lhc = sem("lora_hidden_ready")
        s_sq = sem("key_squares_ready")
        s_hs = sem("head_sum_done")
        s_hsc = sem("head_sum_read")
        s_lc = sem("log_decay_ready")
        s_ex = sem("decays_ready")
        s_kr = sem("chunk_operands_ready")
        s_vp = sem("pair_values_ready")
        s_bkt = sem("token_major_done")
        s_bkc = sem("token_major_copied")
        s_gm = sem("grams_done")
        s_gmm = sem("grams_masked")
        s_lv = sem("level_operand_ready")
        s_xi = sem("level_product_done")
        s_xc = sem("level_product_copied")
        s_dd = sem("level_update_done")
        s_dg = sem("inverse_updated")
        s_r1 = sem("local_rhs_done")
        s_r = sem("rhs_ready")
        s_r2 = sem("state_rhs_done")
        s_u = sem("solution_done")
        s_uc = sem("solution_ready")
        s_sd = sem("state_increment_done")
        s_st = sem("state_ready")
        s_y = sem("y_done")
        s_yc = sem("y_ready")
        s_ym = sem("y_moment_done")
        s_yr = sem("y_moment_read")
        s_pair = sem("pair_finished")
        s_ms = sem("mean_square_ready")
        s_rt = sem("root_ready")
        L1F = 12
        NPAIR = KT

        def sp_mix1(sp):
            sp.wait_ge(s_ln, 2 * TT)
            for n, (dst, src) in enumerate([
                    (w1, a["rw_w_w1"][0].rearrange("(p k) c -> p k c", k=KT)),
                    (a1w, a["rw_a1"][0].rearrange("(p k) c -> p k c", k=KT)),
                    (g1, a["rw_g1"][0].rearrange("(p k) c -> p k c", k=KT)),
                    (w2[0:64, :], a["rw_w_w2"][0]), (a2[0:64, :], a["rw_a2"][0]),
                    (g2a, a["rw_g2"][0][0:P, :]), (g2b[0:32, :], a["rw_g2"][0][P:160, :])]):
                sp.dma_start(dst, src).then_inc(s_lw, 16)
            load_ln(sp, 2)
            for m, name in enumerate(["rw_w_r", "rw_w_k", "rw_w_v"]):
                stream(sp, a[name][0].rearrange("(p k) c -> p k c", k=KT), 4 * m, 16, 4)
            stream_out(sp, a["rw_w_o"][0].rearrange("(k p) c -> p k c", p=P), 1, 12, 16)

        ORDER = [0, 2, 3, 1, 4, 5]

        def dve_mix1(v, link):
            dve_transpose_copy(v, 2)
            v.wait_ge(s_xT, 12)
            v.wait_ge(s_vec, 16 * 10)
            link(nc.vector.tensor_tensor(XX[:, :, 1:T], xT[:, :, 0:T - 1], xT[:, :, 1:T], ALU.subtract))
            link(nc.vector.tensor_scalar(XX[:, :, 0:1], xT[:, :, 0:1], -1.0, None, ALU.mult))
            link(nc.vector.tensor_scalar(VEC[:, V_1KA, :], VEC[:, V_KA, :], -1.0, 1.0, ALU.mult, ALU.add))
            link.sync()
            for n, m in enumerate(ORDER):
                if 2 <= n <= 4:
                    v.wait_ge(s_pj, 16 + 8 * (n - 1))
                if n == 5:
                    v.wait_ge(s_lh, 1)
                for k in range(KT):
                    ins = nc.vector.scalar_tensor_tensor(out=XM[:, n % 2, k, :], in0=XX[:, k, :],
                                                         scalar=MU[:, m, k:k + 1], in1=xT[:, k, :],
                                                         op0=ALU.mult, op1=ALU.add)
                ins.then_inc(s_xm, 1)
            v.wait_ge(s_lh, 4)
            v.wait_ge(s_xm, 6)
            link(nc.vector.memset(SS[:, :, :], 0.0))
            v.wait_ge(s_pe, 4 + 16 + 16 + 8 + 24)
            link.sync()
            PER = 41
            with v.Fori(0, NPAIR) as j:
                link.enter(j, 0, PER)
                jj = lambda m: m[:, ds(j, 1), :].rearrange("p o t -> p (o t)")
                vec = lambda n: VEC[:, n, ds(j, 1)]
                v.wait_ge(s_pair, j + 1)
                link(nc.vector.tensor_tensor_scan(out=LC, data0=m01[:, :], data1=jj(SG), initial=0.0,
                                                  op0=ALU.mult, op1=ALU.add))
                link(nc.vector.tensor_scalar(KKR, jj(KTT), vec(V_KK), None, ALU.mult))
                link.sync()
                nc.vector.tensor_tensor(LCX, LC, jj(SG), ALU.subtract).then_inc(s_lc, 1)
                nc.vector.tensor_tensor(SQ, KKR, KKR, ALU.mult).then_inc(s_sq, 1)
                link(nc.vector.tensor_scalar(KM, jj(AT), vec(V_KA), vec(V_1KA), ALU.mult, ALU.add))
                link.sync()
                link(nc.vector.tensor_tensor(KM, KM, jj(KTT), ALU.mult))
                link.sync()
                v.wait_ge(s_hs, 2 * j + 1)
                nc.vector.tensor_scalar(TMP, PS[:, 4, 0:T], 1e-24, None, ALU.max).then_inc(s_ms, 1)
                v.wait_ge(s_rt, 2 * j + 1)
                link(nc.vector.reciprocal(TMP, TMP))
                link.sync()
                link(nc.vector.tensor_tensor(KK, KKR, TMP, ALU.mult))
                link.sync()
                link(nc.vector.scalar_tensor_tensor(out=SQ, in0=KM, scalar=vec(V_RK), in1=jj(RT),
                                                    op0=ALU.mult, op1=ALU.mult))
                link.sync()
                v.sem_inc(s_sq, 1)
                v.wait_ge(s_ex, 3 * j + 3)
                link(nc.vector.tensor_tensor(BI, KK, jj(AT), ALU.mult))
                link.sync()
                nc.vector.tensor_tensor(BI, BI, E3, ALU.mult).then_inc(s_kr, 1)
                nc.vector.tensor_tensor(KI, KM, E3, ALU.mult).then_inc(s_kr, 1)
                tiles = lambda m: m.rearrange("p (a t) -> p a t", a=TT)
                nc.vector.tensor_tensor(KR[:, :, 0, :], tiles(KK), tiles(E2), ALU.mult).then_inc(s_kr, 1)
                nc.vector.tensor_tensor(KR[:, :, 1, :], jj(RT).rearrange("p (a t) -> p a t", a=TT), tiles(E1),
                                        ALU.mult).then_inc(s_kr, 1)
                v.wait_ge(s_gm, j + 1)
                for o, dst in enumerate([MP, NQ]):
                    for h in range(2):
                        nc.vector.tensor_tensor(
                            dst[:, h, :, :, :].rearrange("p a m t -> p a (m t)"),
                            PS[:, 2 * o + h, :].rearrange("p (a f) -> p a f", a=TT),
                            MK[:, :, :].rearrange("p (o m) t -> p o (m t)", o=1).to_broadcast([P, TT, 2 * P]),
                            ALU.mult).then_inc(s_gmm, 1)
                v.wait_ge(s_gmm, 4 * j + 2)
                quad = lambda m: m[:, :, :, 0, :].rearrange("p h a t -> p (h a) t")
                bc = lambda m: m.to_broadcast([P, 4, P])
                link(nc.vector.tensor_tensor(LVL, quad(MP), bc(LM[:, 0:1, :]), ALU.mult))
                link.sync()
                nc.vector.tensor_tensor(DT[:, :, :], bc(ident[:, :].rearrange("p (o t) -> p o t", o=1)), LVL,
                                        ALU.subtract).then_inc(s_dg, 1)
                v.wait_ge(s_dd, 6 * j + 1)
                link(nc.vector.tensor_copy(DG[:, :, :], PS[:, 5, :].rearrange("p (m t) -> p m t", m=4)))
                for lv in range(1, 6):
                    if lv > 1:
                        v.wait_ge(s_xi, 5 * j + lv - 1)
                    link(nc.vector.tensor_tensor(LVL, quad(MP), bc(LM[:, lv:lv + 1, :]), ALU.mult))
                    link.sync()
                    v.sem_inc(s_lv, 1)
                    v.wait_ge(s_dd, 6 * j + lv + 1)
                    link(nc.vector.tensor_tensor(DG[:, :, :], DG[:, :, :], PS[:, 5, :].rearrange("p (m t) -> p m t", m=4),
                                                 ALU.subtract))
                    link(nc.vector.tensor_tensor(DT[:, :, :], DT[:, :, :], PS[:, 6, :].rearrange("p (m t) -> p m t", m=4),
                                                 ALU.subtract))
                    link.sync()
                    v.sem_inc(s_dg, 1)
                v.wait_ge(s_r1, j + 1)
                link(nc.vector.tensor_copy(R1[:, :, :], PS[:, 7, 0:2 * P].rearrange("p (a c) -> p a c", a=TT)))
                link.sync()
                v.sem_inc(s_r, 1)
                for c in range(NCH):
                    t, p0 = c // 2, CH * (c % 2)
                    if c:
                        v.wait_ge(s_r2, 3 * j + c)
                        link(nc.vector.tensor_tensor(R1[p0:p0 + CH, t, :], R1[p0:p0 + CH, t, :],
                                                     PS[p0:p0 + CH, 0, 0:P], ALU.add))
                        link.sync()
                        v.sem_inc(s_r, 1)
                    if c < NCH - 1:
                        dc = E1[:, CH * c + CH - 1:CH * c + CH]
                        link(nc.vector.tensor_scalar(SD, SS[:, c, :], dc, None, ALU.mult))
                    v.wait_ge(s_u, 4 * j + c + 1)
                    nc.vector.tensor_scalar(UU[p0:p0 + CH, t, :], PS[p0:p0 + CH, 1, 0:P], -1.0, None,
                                            ALU.mult).then_inc(s_uc, 1)
                    if c < NCH - 1:
                        link.sync()
                        v.wait_ge(s_sd, 3 * j + c + 1)
                        for h in range(2):
                            q = slice(HD * h, HD * h + HD)
                            ins = nc.vector.scalar_tensor_tensor(
                                out=SS[q, c + 1, q], in0=PS[q, 2, q], scalar=dc[q, :], in1=SD[q, q],
                                op0=ALU.mult, op1=ALU.add)
                            if h == 0:
                                link(ins)
                            else:
                                ins.then_inc(s_st, 1)
                v.wait_ge(s_y, j + 1)
                nc.vector.tensor_copy(YY, PS[:, 3, 0:T]).then_inc(s_yc, 1)
                v.wait_ge(s_ym, 2 * j + 1)
                link(nc.vector.scalar_tensor_tensor(out=YC, in0=PS[:, 0, 0:T], scalar=-1.0 / HD, in1=YY,
                                                    op0=ALU.mult, op1=ALU.add))
                link.sync()
                nc.vector.tensor_tensor(YQ, YC, YC, ALU.mult).then_inc(s_yr, 1)
                v.wait_ge(s_ym, 2 * j + 2)
                nc.vector.tensor_scalar(TMP, PS[:, 1, 0:T], 1.0 / HD, GN_EPS, ALU.mult, ALU.add).then_inc(s_ms, 1)
                v.wait_ge(s_rt, 2 * j + 2)
                link(nc.vector.reciprocal(TMP, TMP))
                link.sync()
                link(nc.vector.tensor_tensor(YC, YC, TMP, ALU.mult))
                link.sync()
                link(nc.vector.tensor_scalar(YC, YC, vec(V_LG), vec(V_LB), ALU.mult, ALU.add))
                link.sync()
                v.wait_ge(s_hsc, 2 * j + 2)
                link(nc.vector.tensor_tensor(YC, YC, BON, ALU.add))
                link.sync()
                link(nc.vector.tensor_tensor(jj(RT), YC, jj(GTT), ALU.mult))
                link.sync()
                v.sem_inc(s_pair, 1)
            link.leave(NPAIR)

        def act_mix1(s):
            act_transpose_copy(s, 2)
            s.wait_ge(s_xT, 12)
            copy_tiles(s, RT, 16, 2)
            copy_tiles(s, KTT, 24, 2)
            with s.Fori(0, 2) as i:
                for n in range(4):
                    s.wait_ge(s_pj, 4 * i + (32 + n + 1))
                    nc.scalar.copy(V1[:, n % 2, ds((2 * i + n // 2) * CB, CB)], PS[:, 4 + n, 0:CB]).then_inc(s_pe, 1)
            s.wait_ge(s_lh, 1)
            nc.scalar.activation(LH[0:64, 0, :], PS[0:64, 0, 0:T], ACT.Tanh).then_inc(s_lhc, 1)
            s.wait_ge(s_lh, 2)
            nc.scalar.copy(LH[0:64, 1, :], PS[0:64, 1, 0:T]).then_inc(s_lhc, 1)
            s.wait_ge(s_lh, 4)
            nc.scalar.activation(LH[:, 2, :], PS[:, 2, 0:T], ACT.Sigmoid).then_inc(s_lhc, 1)
            nc.scalar.activation(LH[0:32, 3, :], PS[0:32, 3, 0:T], ACT.Sigmoid).then_inc(s_lhc, 1)
            for m in range(3):
                dst = (SG, AT, GTT)[m]
                with s.Fori(0, 2) as i:
                    for n in range(4):
                        s.wait_ge(s_pj, 4 * i + (40 + 8 * m + n + 1))
                        o = dst[:, ds(4 * i + n, 1), :].rearrange("p o t -> p (o t)")
                        if m < 2:
                            ins = nc.scalar.activation(o, PS[:, 4 + n, 0:T], ACT.Sigmoid,
                                                       bias=VEC[:, V_W0 + m, ds(4 * i + n, 1)])
                        else:
                            ins = nc.scalar.copy(o, PS[:, 4 + n, 0:T])
                        ins.then_inc(s_pe, 1)
            s.wait_ge(s_pe, 4 + 16 + 24 + 24)
            s.sem_inc(s_pair, 1)
            with s.Fori(0, NPAIR) as j:
                s.wait_ge(s_pair, j + 1)
                s.wait_ge(s_lc, j + 1)
                nc.scalar.activation(E1, LC, ACT.Exp, scale=-CDEC).then_inc(s_ex, 1)
                nc.scalar.activation(E2, LCX, ACT.Exp, scale=-CDEC).then_inc(s_ex, 1)
                nc.scalar.activation(E3, LC, ACT.Exp, scale=CDEC).then_inc(s_ex, 1)
                nc.scalar.copy(VP[:, :, :], V1[:, :, ds(P * j, P)]).then_inc(s_vp, 1)
                s.wait_ge(s_ms, 2 * j + 1)
                nc.scalar.activation(TMP, TMP, ACT.Sqrt).then_inc(s_rt, 1)
                s.wait_ge(s_bkt, 2 * j + 1)
                nc.scalar.copy(BKT[:, :, :, :].rearrange("p m a t -> p (m a t)"), PS[:, 6, :]).then_inc(s_bkc, 1)
                s.wait_ge(s_bkt, 2 * j + 2)
                nc.scalar.copy(VT, PS[:, 7, 0:T]).then_inc(s_bkc, 1)
                s.wait_ge(s_hs, 2 * j + 2)
                s.wait_ge(s_bkc, 2 * j + 2)
                nc.scalar.copy(BON, PS[:, 4, 0:T]).then_inc(s_hsc, 1)
                for lv in range(1, 6):
                    s.wait_ge(s_xi, 5 * j + lv)
                    nc.scalar.copy(XI[:, :, :], PS[:, 4, :].rearrange("p (m t) -> p m t", m=4)).then_inc(s_xc, 1)
                s.wait_ge(s_ms, 2 * j + 2)
                nc.scalar.activation(TMP, TMP, ACT.Sqrt).then_inc(s_rt, 1)

        def gp_mix1(g):
            with g.Fori(0, NPAIR) as j:
                g.wait_ge(s_hsc, 2 * j + 1)
                nc.gpsimd.tensor_tensor(BON, BON, VT, ALU.mult).then_inc(s_hsc, 1)

        def pe_mix1(pe):
            pe_transpose(pe, 2)
            pe.wait_ge(s_xT, 12)
            for n in range(2):
                pe.wait_ge(s_xm, n + 1)
                project_channels(pe, XM[:, n, :, :], L1F + 4 * n, 4, 16 + 8 * n)
            pe.wait_ge(s_xm, 3)
            project_tokens(pe, XM[:, 0, :, :], L1F + 8, 4, 32)
            pe.wait_ge(s_lw, 16 * 7)
            for n, (x, w, c0, m, bank) in enumerate([(1, w1, 0, 64, 0), (0, a1w, 0, 64, 1),
                                                     (1, g1, 0, P, 2), (1, g1, P, 32, 3)]):
                pe.wait_ge(s_xm, min(4 + n, 6))
                for k in range(KT):
                    ins = nc.tensor.matmul(PS[0:m, bank, 0:T], w[:, k, c0:c0 + m], XM[:, x, k, :],
                                           start=(k == 0), stop=(k == KT - 1))
                ins.then_inc(s_lh, 1)
            for m in range(3):
                pe.wait_ge(s_lhc, (1, 2, 4)[m])
                for n in range(KT):
                    pe.wait_ge(s_pe, 40 + 8 * m + n + 1)
                    cs = slice(n * P, (n + 1) * P)
                    if m < 2:
                        nc.tensor.matmul(PS[:, 4 + n % 4, 0:T], (w2, a2)[m][0:64, cs], LH[0:64, m, :],
                                         start=True, stop=True).then_inc(s_pj, 1)
                    else:
                        nc.tensor.matmul(PS[:, 4 + n % 4, 0:T], g2a[:, cs], LH[:, 2, :], start=True, stop=False)
                        nc.tensor.matmul(PS[:, 4 + n % 4, 0:T], g2b[0:32, cs], LH[0:32, 3, :],
                                         start=False, stop=True).then_inc(s_pj, 1)
            pe.wait_ge(s_pe, 4 + 16 + 24 + 24)
            with pe.Fori(0, NPAIR) as j:
                pe.wait_ge(s_pair, j + 1)
                pe.wait_ge(s_sq, 2 * j + 1)
                nc.tensor.matmul(PS[:, 4, 0:T], bones[:, :], SQ, start=True, stop=True).then_inc(s_hs, 1)
                pe.wait_ge(s_sq, 2 * j + 2)
                nc.tensor.matmul(PS[:, 4, 0:T], bones[:, :], SQ, start=True, stop=True).then_inc(s_hs, 1)
                pe.wait_ge(s_kr, 4 * j + 4)
                for m, src in enumerate([BI, KI]):
                    for t in range(TT):
                        o = (2 * m + t) * P
                        ins = nc.tensor.transpose(PS[:, 6, o:o + P], src[:, t * P:(t + 1) * P], ident[:, :])
                ins.then_inc(s_bkt, 1)
                pe.wait_ge(s_vp, j + 1)
                for t in range(TT):
                    ins = nc.tensor.transpose(PS[:, 7, t * P:(t + 1) * P], VP[:, t, :], ident[:, :])
                ins.then_inc(s_bkt, 1)
                for m, src in enumerate([BI, KI]):
                    for h in range(2):
                        r = slice(HD * h, HD * h + HD)
                        for t in range(TT):
                            ins = nc.tensor.matmul(PS[:, 2 * m + h, t * 2 * P:(t + 1) * 2 * P], src[r, t * P:(t + 1) * P],
                                                   KR[r, t, :, :].rearrange("p m t -> p (m t)"), start=True, stop=True)
                ins.then_inc(s_gm, 1)
                pe.wait_ge(s_dg, 6 * j + 1)
                for q in range(4):
                    ins = nc.tensor.transpose(PS[:, 5, q * P:(q + 1) * P], DT[:, q, :], ident[:, :])
                ins.then_inc(s_dd, 1)
                pe.wait_ge(s_hsc, 2 * j + 1)
                pe.wait_ge(s_bkc, 2 * j + 2)
                pe.wait_ge(s_gmm, 4 * j + 4)
                for t in range(TT):
                    for h in range(2):
                        o = t * P + h * HD
                        ins = nc.tensor.matmul(PS[:, 7, o:o + HD], NQ[:, h, t, 0, :], VP[:, t, h * HD:h * HD + HD],
                                               start=True, stop=True)
                ins.then_inc(s_r1, 1)
                for lv in range(1, 6):
                    pe.wait_ge(s_lv, 5 * j + lv)
                    for q in range(4):
                        ins = nc.tensor.matmul(PS[:, 4, q * P:(q + 1) * P], LVL[:, q, :], DG[:, q, :], start=True, stop=True)
                    ins.then_inc(s_xi, 1)
                    pe.wait_ge(s_xc, 5 * j + lv)
                    for q in range(4):
                        nc.tensor.matmul(PS[:, 5, q * P:(q + 1) * P], DT[:, q, :], XI[:, q, :], start=True, stop=True)
                    for q in range(4):
                        ins = nc.tensor.matmul(PS[:, 6, q * P:(q + 1) * P], XI[:, q, :], DT[:, q, :], start=True, stop=True)
                    ins.then_inc(s_dd, 1)
                pe.wait_ge(s_dg, 6 * j + 6)
                for c in range(NCH):
                    t, p0 = c // 2, CH * (c % 2)
                    rows = slice(p0, p0 + CH)
                    if c:
                        pe.wait_ge(s_st, 3 * j + c)
                        nc.tensor.matmul(PS[rows, 0, 0:P], KR[:, t, 0, rows], SS[:, c, :], start=True,
                                         stop=True).then_inc(s_r2, 1)
                    pe.wait_ge(s_r, 4 * j + c + 1)
                    for h in range(2):
                        hc = slice(h * HD, h * HD + HD)
                        ins = nc.tensor.matmul(PS[:, 1, hc], DT[rows, 2 * h + t, :], R1[rows, t, hc],
                                               start=True, stop=True)
                    ins.then_inc(s_u, 1)
                    pe.wait_ge(s_uc, 4 * j + c + 1)
                    if c < NCH - 1:
                        nc.tensor.matmul(PS[:, 2, 0:P], BKT[rows, 0, t, :], UU[rows, t, :], start=True, stop=False)
                        nc.tensor.matmul(PS[:, 2, 0:P], BKT[rows, 1, t, :], VP[rows, t, :], start=False,
                                         stop=True).then_inc(s_sd, 1)
                for t in range(TT):
                    for c in range(2):
                        nc.tensor.matmul(PS[:, 3, t * P + c * CH:t * P + (c + 1) * CH], SS[:, 2 * t + c, :],
                                         KR[:, t, 1, c * CH:(c + 1) * CH], start=(c == 0), stop=False,
                                         skip_group_check=True)
                    for h in range(2):
                        hc = slice(h * HD, h * HD + HD)
                        nc.tensor.matmul(PS[hc, 3, t * P:(t + 1) * P], VP[:, t, hc], NQ[:, h, t, 1, :],
                                         start=False, stop=False, skip_group_check=True)
                        ins = nc.tensor.matmul(PS[hc, 3, t * P:(t + 1) * P], UU[:, t, hc], MP[:, h, t, 1, :],
                                               start=False, stop=True, skip_group_check=True)
                ins.then_inc(s_y, 1)
                pe.wait_ge(s_yc, j + 1)
                nc.tensor.matmul(PS[:, 0, 0:T], bones[:, :], YY, start=True, stop=True).then_inc(s_ym, 1)
                pe.wait_ge(s_yr, j + 1)
                nc.tensor.matmul(PS[:, 1, 0:T], bones[:, :], YQ, start=True, stop=True).then_inc(s_ym, 1)
            pe.wait_ge(s_pair, NPAIR + 1)
            out_project(pe, RT, L1F + 12, 1)

        def moe_sems(l):
            names = ["logits_done", "scores_ready", "mask_ready", "rank_done", "rank_ready", "count_ready",
                     "shared_loaded", "shared_gate_up", "shared_silu", "shared_hidden", "onehot_ready",
                     "gathered0", "gathered1", "gathered0_copied", "gathered1_copied", "gate_up_done",
                     "silu_ready", "hidden_ready", "turned", "hidden_copied", "gates_copied", "x_part", "x_rest", "down0", "down1",
                     "down0_copied", "down1_copied", "scattered",
                     "over_pe", "over_dve", "over_act", "over_loaded", "over_free", "over_link", "over_list"]
            return {n: sem(f"l{l}_{n}") for n in names} | {
                "gu_w": [sem(f"l{l}_gate_up_loaded{s}") for s in range(4)],
                "dn_w": [sem(f"l{l}_down_loaded{s}") for s in range(4)]}

        def moe_view(l):
            q = moe_sems(l)
            st = 2 * l + 1
            wg, wu, wd = a["moe_w_gate"][l], a["moe_w_up"][l], a["moe_w_down"][l]
            gate_src = lambda w, e: w[ds(e, 1), :, :].rearrange("o (p k) f -> p (o k) f", k=KT)
            down_src = lambda w, e: w[ds(e, 1), :, :].rearrange("o (k p) d -> p (o k) d", p=P)

            def gate_and_up(slot):
                w = RING[:, slot + 1, :] if slot < 2 else odd[:, slot - 2, :]
                return w[:, 0:4096].rearrange("p (m k f) -> p k m f", m=2, k=KT)

            def load_gate_up(sp, e, slot):
                g, u, d = wslot(slot)
                sp.dma_start(g, gate_src(wg, e)).then_inc(q["gu_w"][slot], 16)
                sp.dma_start(u, gate_src(wu, e)).then_inc(q["gu_w"][slot], 16)

            def load_down(sp, e, slot):
                sp.dma_start(wslot(slot)[2], down_src(wd, e)).then_inc(q["dn_w"][slot], 16)

            def load_expert(sp, e, slot):
                load_gate_up(sp, e, slot)
                load_down(sp, e, slot)

            def prefetch(sp):
                if l:
                    sp.wait_ge(s_res, 2)
                g, u, d = wslot(-1)
                sp.dma_start(g, a["moe_ws_gate"][l].rearrange("(p k) f -> p k f", k=KT)).then_inc(q["shared_loaded"], 16)
                sp.dma_start(u, a["moe_ws_up"][l].rearrange("(p k) f -> p k f", k=KT)).then_inc(q["shared_loaded"], 16)
                sp.dma_start(d, a["moe_ws_down"][l].rearrange("(k p) d -> p k d", p=P)).then_inc(q["shared_loaded"], 16)
                load_expert(sp, 0, 0)

            def loads(sp):
                sp.wait_ge(s_ln, TT * st)
                for e in range(1, 4):
                    load_expert(sp, e, e)
                load_ln(sp, st)
                with sp.Fori(1, PAIRS // 2) as i:
                    for half in range(2):
                        sp.wait_ge(q["gate_up_done"], 2 * i + (half - 1))
                        for s in range(2):
                            load_gate_up(sp, 4 * i + 2 * half + s, 2 * half + s)
                        sp.wait_ge(q["down1"], 2 * i + (half - 1))
                        for s in range(2):
                            load_down(sp, 4 * i + 2 * half + s, 2 * half + s)
                sp.wait_ge(q["count_ready"], 1)
                most = nc.sync.value_load(cnti[0:1, 2 * l:2 * l + 1], min_val=0, max_val=T)
                with sp.If(most > B):
                    sp.wait_ge(q["over_list"], 1)
                    rounds = nc.sync.value_load(cnti[0:1, 2 * l + 1:2 * l + 2], min_val=1, max_val=NOV // 2)
                    with sp.Fori(0, rounds) as i:
                        sp.wait_ge(q["over_free"], i + 1)
                        for s in range(2):
                            e = nc.sync.value_load(elist[0:1, ds(2 * i + s, 1)], min_val=0, max_val=E - 1)
                            g, u, d = wslot(s)
                            sp.dma_start(g, gate_src(wg, e)).then_inc(q["over_loaded"], 16)
                            sp.dma_start(u, gate_src(wu, e)).then_inc(q["over_loaded"], 16)
                            sp.dma_start(d, down_src(wd, e)).then_inc(q["over_loaded"], 16)

            def gather(pe, half, sel):
                for k in range(4):
                    for t in range(TT):
                        for n in range(3):
                            ins = nc.tensor.matmul(PS[:, 6 + half, k * 2 * B:(k + 1) * 2 * B],
                                                   XB[:, n, t, 4 * half + k::KT], sel[:, t, :, :].rearrange("p s b -> p (s b)"),
                                                   start=(t == 0 and n == 0), stop=(t == TT - 1 and n == 2))
                return ins

            def gate_up(pe, slots):
                for k in range(KT):
                    for s in range(2):
                        ins = nc.tensor.matmul(PS[s * B:(s + 1) * B, 4, :], XG[:, k, s * B:(s + 1) * B],
                                               gate_and_up(slots[s])[:, k, :, :], start=(k == 0), stop=(k == KT - 1))
                return ins

            def turn(pe, buf):
                for f in range(FT):
                    nc.tensor.transpose(PS[:, 4, f * 2 * B:(f + 1) * 2 * B], HH[0:2 * B, f * P:(f + 1) * P],
                                        ident[0:2 * B, 0:2 * B])
                for t in range(TT):
                    ins = nc.tensor.transpose(PS[0:2 * B, 4, T + t * P:T + (t + 1) * P],
                                              SELG[:, buf, t, :, :].rearrange("p s b -> p (s b)"), ident[:, :])
                return ins

            def down(pe, slots, h, bank):
                for f in range(FT):
                    for s in range(2):
                        ins = nc.tensor.matmul(PS[s * B:(s + 1) * B, bank, :], HT[:, f, s * B:(s + 1) * B],
                                               wslot(slots[s])[2][:, f, h * 512:(h + 1) * 512],
                                               start=(f == 0), stop=(f == FT - 1))
                return ins

            def scatter(pe):
                for t in range(TT):
                    for h in range(2):
                        ins = nc.tensor.matmul(PS[:, 2 * t + h, :], GT[0:2 * B, t, :],
                                               Y[0:2 * B, h * 512:(h + 1) * 512], start=False, stop=True,
                                               skip_group_check=True)
                return ins

            def pe_pair(pe, i, half, first, last, use):
                slots = (2 * half, 2 * half + 1)
                for n in range(2):
                    pe.wait_ge(q[f"gathered{n}_copied"], i + 1)
                for s in slots:
                    pe.wait_ge(q["gu_w"][s], 32 * use + 32)
                if not first:
                    pe.wait_ge(q["hidden_copied"], i)
                    pe.wait_ge(q["gates_copied"], i)
                gate_up(pe, slots).then_inc(q["gate_up_done"], 1)
                if not first:
                    pe.wait_ge(q["down0_copied"], i)
                    pe.wait_ge(q["down1_copied"], i)
                    scatter(pe).then_inc(q["scattered"], 1)
                pe.wait_ge(q["hidden_ready"], i + 1)
                turn(pe, half).then_inc(q["turned"], 1)
                if not last:
                    pe.wait_ge(q["onehot_ready"], i + 2)
                    gather(pe, 0, SEL1[:, 1 - half]).then_inc(q["gathered0"], 1)
                for s in slots:
                    pe.wait_ge(q["dn_w"][s], 16 * use + 16)
                pe.wait_ge(q["hidden_copied"], i + 1)
                down(pe, slots, 0, 5).then_inc(q["down0"], 1)
                if not last:
                    gather(pe, 1, SEL1[:, 1 - half]).then_inc(q["gathered1"], 1)
                pe.wait_ge(q["down0_copied"], i + 1)
                down(pe, slots, 1, 5).then_inc(q["down1"], 1)

            def pe_moe(pe):
                pe_transpose(pe, st)
                pe.wait_ge(s_xT, 4 * (st + 1))
                pe.wait_ge(s_vec, 16 * 10)
                for t in range(TT):
                    for k in range(KT):
                        ins = nc.tensor.matmul(PS[:, 4, t * E:(t + 1) * E], xT[:, k, t * P:(t + 1) * P], WR[:, l, k, :],
                                               start=(k == 0), stop=(k == KT - 1))
                ins.then_inc(q["logits_done"], 1)
                pe.wait_ge(q["shared_loaded"], 48)
                g, u, d = wslot(-1)
                for m, w in enumerate((g, u)):
                    for f in range(FT):
                        for k in range(KT):
                            ins = nc.tensor.matmul(PS[:, 5 + m, f * T:(f + 1) * T], w[:, k, f * P:(f + 1) * P], xT[:, k, :],
                                                   start=(k == 0), stop=(k == KT - 1))
                ins.then_inc(q["shared_gate_up"], 1)
                pe.wait_ge(q["mask_ready"], 1)
                nc.tensor.matmul(PS[:, 4, 0:E], before[:, :], MSK[:, 0, :], start=True, stop=True)
                nc.tensor.matmul(PS[:, 4, E:2 * E], ones[:, :], MSK[:, 0, :], start=True, stop=False)
                nc.tensor.matmul(PS[:, 4, E:2 * E], before[:, :], MSK[:, 1, :], start=False, stop=True)
                nc.tensor.matmul(PS[:, 4, 2 * E:3 * E], ones[:, :], MSK[:, 0, :], start=True, stop=False)
                nc.tensor.matmul(PS[:, 4, 2 * E:3 * E], ones[:, :], MSK[:, 1, :], start=False,
                                 stop=True).then_inc(q["rank_done"], 1)
                pe.wait_ge(q["shared_hidden"], 1)
                for t in range(TT):
                    for h in range(2):
                        for f in range(FT):
                            ins = nc.tensor.matmul(PS[:, 2 * t + h, :], HS[:, f, t * P:(t + 1) * P],
                                                   d[:, f, h * 512:(h + 1) * 512], start=(f == 0), stop=(f == FT - 1))
                pe.wait_ge(q["onehot_ready"], 1)
                pe.wait_ge(q["x_part"], 3)
                gather(pe, 0, SEL1[:, 0]).then_inc(q["gathered0"], 1)
                gather(pe, 1, SEL1[:, 0]).then_inc(q["gathered1"], 1)
                pe.wait_ge(q["rank_ready"], 1)
                pe_pair(pe, 0, 0, True, False, 0)
                pe_pair(pe, 1, 1, False, False, 0)
                with pe.Fori(1, PAIRS // 2 - 1) as i:
                    pe_pair(pe, 2 * i, 0, False, False, i)
                    pe_pair(pe, 2 * i + 1, 1, False, False, i)
                pe_pair(pe, PAIRS - 2, 0, False, False, PAIRS // 2 - 1)
                pe_pair(pe, PAIRS - 1, 1, False, True, PAIRS // 2 - 1)
                for h in range(2):
                    pe.wait_ge(q[f"down{h}_copied"], PAIRS)
                pe.wait_ge(q["gates_copied"], PAIRS)
                scatter(pe).then_inc(q["scattered"], 1)
                pe.wait_ge(q["count_ready"], 1)
                most = nc.tensor.value_load(cnti[0:1, 2 * l:2 * l + 1], min_val=0, max_val=T)
                with pe.If(most > B):
                    pe_over(pe)
                pe.wait_ge(q["scattered"], PAIRS)
                pe.sem_inc(s_res, 1)

            def pe_over(pe):
                pe.wait_ge(q["over_dve"], 1)
                nc.tensor.matmul(PS[0:E, 4, 0:NR], before[0:E, 0:E], F1[0:E, 0, :], start=True, stop=False)
                nc.tensor.matmul(PS[0:E, 4, 0:NR], ones[0:E, 0:E], F1[0:E, 1, :], start=False,
                                 stop=True).then_inc(q["over_pe"], 1)
                pe.wait_ge(q["over_dve"], 2)
                nc.tensor.matmul(PS[0:1, 5, 0:NOV], ecol[0:E, :], OS[0:E, 0, :], start=True, stop=True)
                nc.tensor.matmul(PS[0:1, 5, NOV:2 * NOV], ones[0:E, 0:1], OS[0:E, 0, :], start=True, stop=True)
                for t in range(TT):
                    nc.tensor.transpose(PS[0:E, 6, t * P:(t + 1) * P], RKX[:, t, 0:E], ident[:, :])
                    ins = nc.tensor.transpose(PS[0:E, 6, (2 + t) * P:(3 + t) * P], GX[:, t, 0:E], ident[:, :])
                ins.then_inc(q["over_pe"], 1)
                pe.wait_ge(q["over_dve"], 3)
                for t in range(TT):
                    o = t * NOV
                    nc.tensor.matmul(PS[:, 7, o:o + NOV], TR4[0:E, t, :], OS[0:E, 0, :], start=True, stop=False)
                    nc.tensor.matmul(PS[:, 7, o:o + NOV], ones[0:E, :], OS[0:E, 1, :], start=False, stop=True)
                    ins = nc.tensor.matmul(PS[:, 7, (2 + t) * NOV:(3 + t) * NOV], TR4[0:E, 2 + t, :], OS[0:E, 0, :],
                                           start=True, stop=True)
                ins.then_inc(q["over_pe"], 1)
                pe.wait_ge(q["over_list"], 1)
                rounds = nc.tensor.value_load(cnti[0:1, 2 * l + 1:2 * l + 2], min_val=1, max_val=NOV // 2)
                pe.sem_inc(q["over_free"], 1)
                with pe.Fori(0, rounds) as i:
                    pe.wait_ge(q["over_dve"], 5 * i + 5)
                    gather(pe, 0, SEL1[:, 0])
                    gather(pe, 1, SEL1[:, 0]).then_inc(q["over_pe"], 1)
                    pe.wait_ge(q["over_dve"], 5 * i + 6)
                    pe.wait_ge(q["over_loaded"], 96 * i + 96)
                    gate_up(pe, (0, 1)).then_inc(q["over_pe"], 1)
                    pe.wait_ge(q["over_dve"], 5 * i + 7)
                    turn(pe, 0).then_inc(q["over_pe"], 1)
                    pe.wait_ge(q["over_dve"], 5 * i + 8)
                    for h in range(2):
                        ins = down(pe, (0, 1), h, 5 + h)
                    ins.then_inc(q["over_pe"], 1)
                    pe.wait_ge(q["over_dve"], 5 * i + 9)
                    scatter(pe).then_inc(q["over_pe"], 1)
                    pe.wait_ge(q["over_pe"], 5 * i + 8)
                    pe.sem_inc(q["over_free"], 1)

            def silu(sem_):
                nc.scalar.activation(SIL[0:2 * B, :], PS[0:2 * B, 4, 0:FF], ACT.Silu).then_inc(sem_, 1)

            def copy_gathered(eng_copy, half):
                return eng_copy(XG[:, 4 * half:4 * half + 4, :].rearrange("p k b -> p (k b)"), PS[:, 6 + half, 0:8 * B])

            def act_pair(s, i, half, last):
                s.wait_ge(q["gate_up_done"], i + 1)
                silu(q["silu_ready"])
                s.wait_ge(q["hidden_copied"], i + 1)
                nc.scalar.copy(GT[0:2 * B, :, :].rearrange("p t b -> p (t b)"),
                               PS[0:2 * B, 4, T:2 * T]).then_inc(q["gates_copied"], 1)
                s.wait_ge(q["down0"], i + 1)
                nc.scalar.copy(Y[0:2 * B, 0:512], PS[0:2 * B, 5, :]).then_inc(q["down0_copied"], 1)
                if not last:
                    s.wait_ge(q["gathered1"], i + 2)
                    copy_gathered(nc.scalar.copy, 1).then_inc(q["gathered1_copied"], 1)

            def act_moe(s):
                s.wait_ge(s_ln, TT * st)
                part = lambda n: XB[:, n, :, :].rearrange("p t d -> p (t d)")
                nc.scalar.copy(part(0), X[:, :, :].rearrange("p t d -> p (t d)")).then_inc(q["x_part"], 1)
                act_transpose_copy(s, st)
                s.wait_ge(q["logits_done"], 1)
                nc.scalar.activation(SCO[:, :, :].rearrange("p t e -> p (t e)"), PS[:, 4, 0:TT * E],
                                     ACT.Sigmoid).then_inc(q["scores_ready"], 1)
                for n in range(2):
                    s.wait_ge(q["x_rest"], n + 1)
                    nc.scalar.copy(part(n + 1), XR).then_inc(q["x_part"], 1)
                s.wait_ge(q["shared_gate_up"], 1)
                nc.scalar.activation(HSs[:, :, :].rearrange("p f t -> p (f t)"), PS[:, 5, :],
                                     ACT.Silu).then_inc(q["shared_silu"], 1)
                s.wait_ge(q["gathered1"], 1)
                copy_gathered(nc.scalar.copy, 1).then_inc(q["gathered1_copied"], 1)
                act_pair(s, 0, 0, False)
                act_pair(s, 1, 1, False)
                with s.Fori(1, PAIRS // 2 - 1) as i:
                    act_pair(s, 2 * i, 0, False)
                    act_pair(s, 2 * i + 1, 1, False)
                act_pair(s, PAIRS - 2, 0, False)
                act_pair(s, PAIRS - 1, 1, True)
                s.wait_ge(q["count_ready"], 1)
                most = nc.scalar.value_load(cnti[0:1, 2 * l:2 * l + 1], min_val=0, max_val=T)
                with s.If(most > B):
                    s.wait_ge(q["over_list"], 1)
                    rounds = nc.scalar.value_load(cnti[0:1, 2 * l + 1:2 * l + 2], min_val=1, max_val=NOV // 2)
                    with s.Fori(0, rounds) as i:
                        s.wait_ge(q["over_pe"], 5 * i + 5)
                        silu(q["over_act"])

            def onehot(v, link, i, buf, sem_, width=E):
                spread = lambda m: m[:, :, ds(2 * i, 2)].rearrange("p t (s o) -> p t s o", o=1).to_broadcast([P, TT, 2, B])
                io = iotab[:, :].rearrange("p (t s b) -> p t s b", t=1, s=1).to_broadcast([P, TT, 2, B])
                link(nc.vector.tensor_tensor(SEL1[:, buf], spread(RKX), io, ALU.is_equal))
                link.sync()
                nc.vector.tensor_tensor(SELG[:, buf], SEL1[:, buf], spread(GX), ALU.mult).then_inc(sem_, 1)

            def hidden(sem_):
                nc.vector.tensor_tensor(HH[0:2 * B, :], SIL[0:2 * B, :], PS[0:2 * B, 4, FF:2 * FF],
                                        ALU.mult).then_inc(sem_, 1)

            def copy_hidden():
                return nc.vector.tensor_copy(HT[:, :, :].rearrange("p f b -> p (f b)"), PS[:, 4, 0:FT * 2 * B])

            def dve_pair(v, link, i, half, more, last):
                v.wait_ge(q["silu_ready"], i + 1)
                hidden(q["hidden_ready"])
                v.wait_ge(q["turned"], i + 1)
                copy_hidden().then_inc(q["hidden_copied"], 1)
                if not last:
                    v.wait_ge(q["gathered0"], i + 2)
                    copy_gathered(nc.vector.tensor_copy, 0).then_inc(q["gathered0_copied"], 1)
                if more:
                    onehot(v, link, i + 2, half, q["onehot_ready"])
                v.wait_ge(q["down1"], i + 1)
                nc.vector.tensor_copy(Y[0:2 * B, 512:1024], PS[0:2 * B, 5, :]).then_inc(q["down1_copied"], 1)

            def dve_route(v, link):
                pair = lambda m: m[:, :, :].rearrange("p t e -> p (t e)")
                byg = lambda m: m[:, :, :].rearrange("p t (g e) -> p (t g) e", e=GE)
                v.wait_ge(q["scores_ready"], 1)
                link(nc.vector.tensor_tensor(BIA[:, :, :], SCO[:, :, :], EB[:, l:l + 1, :].to_broadcast([P, TT, E]),
                                             ALU.add))
                link.sync()
                for n in range(TT * NG):
                    link(nc.vector.max(top2[:, n, :], byg(BIA)[:, n, :]))
                link.sync()
                tg = grp[:, :, :].rearrange("p t g -> p (t g)")
                link(nc.vector.tensor_tensor(tg, top2[:, :, 0], top2[:, :, 1], ALU.add))
                link.sync()
                mine = grp[:, :, :].rearrange("p t (g o) -> p t g o", o=1).to_broadcast([P, TT, NG, NG])
                other = grp[:, :, :].rearrange("p t (o g) -> p t o g", o=1).to_broadcast([P, TT, NG, NG])
                tri = tri8[:, :, :].rearrange("p (o g) h -> p o g h", o=1).to_broadcast([P, TT, NG, NG])
                link(nc.vector.tensor_tensor(cmpa[:, :, :, :], other, mine, ALU.is_gt))
                link(nc.vector.tensor_tensor(cmpb[:, :, :, :], other, mine, ALU.is_equal))
                link.sync()
                link(nc.vector.tensor_tensor(cmpb[:, :, :, :], cmpb[:, :, :, :], tri, ALU.mult))
                link.sync()
                link(nc.vector.tensor_tensor(cmpa[:, :, :, :], cmpa[:, :, :, :], cmpb[:, :, :, :], ALU.add))
                link.sync()
                link(nc.vector.tensor_reduce(gcnt[:, :, :], cmpa[:, :, :, :], AX, ALU.add))
                link.sync()
                link(nc.vector.tensor_scalar(gcnt[:, :, :], gcnt[:, :, :], TOPG - 0.5, None, ALU.is_lt))
                link.sync()
                link(nc.vector.tensor_scalar(gpen[:, :, :], gcnt[:, :, :], BIG, -BIG, ALU.mult, ALU.add))
                wide = lambda m: m[:, :, :].rearrange("p t (g o) -> p (t g) o", o=1).to_broadcast([P, TT * NG, GE])
                link(nc.vector.tensor_tensor(byg(BIA), byg(BIA), wide(gcnt), ALU.mult))
                link.sync()
                link(nc.vector.tensor_tensor(byg(BIA), byg(BIA), wide(gpen), ALU.add))
                link.sync()
                for t in range(TT):
                    link(nc.vector.max(top8[:, t, :], BIA[:, t, :]))
                link.sync()
                for t in range(TT):
                    link(nc.vector.match_replace(REP[:, t, :], top8[:, t, :], BIA[:, t, :], -3.0 * BIG))
                link.sync()
                nc.vector.tensor_tensor(MSK[:, :, :], REP[:, :, :], BIA[:, :, :], ALU.not_equal).then_inc(q["mask_ready"], 1)
                v.wait_ge(q["mask_ready"], 1)
                link(nc.vector.tensor_tensor(SEL[:, :, :], SCO[:, :, :], MSK[:, :, :], ALU.mult))
                link.sync()
                link(nc.vector.tensor_reduce(gsum[:, :], SEL[:, :, :], AX, ALU.add))
                link.sync()
                link(nc.vector.reciprocal(gsum[:, :], gsum[:, :]))
                link.sync()
                for t in range(TT):
                    link(nc.vector.tensor_scalar(GX[:, t, 0:E], SEL[:, t, :], gsum[:, t:t + 1], 2.5, ALU.mult, ALU.mult))
                v.wait_ge(q["rank_done"], 1)
                link(nc.vector.scalar_tensor_tensor(out=RKX[:, :, 0:E],
                                                    in0=PS[:, 4, 0:TT * E].rearrange("p (t e) -> p t e", t=TT), scalar=1.0,
                                                    in1=MSK[:, :, :], op0=ALU.add, op1=ALU.mult))
                link(nc.vector.tensor_reduce(cntf[0:1, 0:1], PS[0:1, 4, 2 * E:3 * E], AX, ALU.max))
                link(nc.vector.tensor_copy(CNT[:, :], PS[:, 4, 2 * E:3 * E]))
                link.sync()
                link(nc.vector.tensor_scalar(RKX[:, :, 0:E], RKX[:, :, 0:E], -1.0, None, ALU.add))
                link(nc.vector.tensor_copy(cnti[0:1, 2 * l:2 * l + 1], cntf[0:1, 0:1]))
                link.sync()
                v.sem_inc(q["rank_ready"], 1)
                v.sem_inc(q["count_ready"], 1)
                onehot(v, link, 0, 0, q["onehot_ready"])
                onehot(v, link, 1, 1, q["onehot_ready"])

            def dve_moe(v, link):
                dve_transpose_copy(v, st)
                dve_route(v, link)
                v.wait_ge(q["shared_silu"], 1)
                nc.vector.tensor_tensor(HS[:, :, :].rearrange("p f t -> p (f t)"),
                                        HSs[:, :, :].rearrange("p f t -> p (f t)"), PS[:, 6, :],
                                        ALU.mult).then_inc(q["shared_hidden"], 1)
                v.wait_ge(q["gathered0"], 1)
                copy_gathered(nc.vector.tensor_copy, 0).then_inc(q["gathered0_copied"], 1)
                dve_pair(v, link, 0, 0, True, False)
                dve_pair(v, link, 1, 1, True, False)
                with v.Fori(1, PAIRS // 2 - 1) as i:
                    link.enter(i, 1, 2)
                    dve_pair(v, link, 2 * i, 0, True, False)
                    dve_pair(v, link, 2 * i + 1, 1, True, False)
                link.leave(PAIRS // 2 - 2)
                dve_pair(v, link, PAIRS - 2, 0, False, False)
                dve_pair(v, link, PAIRS - 1, 1, False, True)
                most = nc.vector.value_load(cnti[0:1, 2 * l:2 * l + 1], min_val=0, max_val=T)
                with v.If(most > B):
                    dve_over(v, Link(v, q["over_link"]))

            def dve_over(v, link):
                v.wait_ge(q["scattered"], PAIRS)
                link(nc.vector.tensor_tensor(F2[0:E, :], ident[0:E, 0:E], CNT[0:E, :], ALU.mult))
                link.sync()
                link(nc.vector.tensor_reduce(cntf[0:E, 1:2], F2[0:E, :], AX, ALU.add))
                link.sync()
                link(nc.vector.tensor_scalar(F1[0:E, 0, :], thr[0:E, :], cntf[0:E, 1:2], None, ALU.is_lt))
                link(nc.vector.memset(F1[0:E, 1, 0:1], 0.0))
                link.sync()
                for r in range(1, NR):
                    link(nc.vector.tensor_tensor(F1[0:E, 1, r:r + 1], F1[0:E, 1, r - 1:r], F1[0:E, 0, r - 1:r], ALU.add))
                    link.sync()
                v.sem_inc(q["over_dve"], 1)
                v.wait_ge(q["over_pe"], 1)
                link(nc.vector.tensor_copy(F1[0:E, 2, :], PS[0:E, 4, 0:NR]))
                link.sync()
                wide = lambda m: m.rearrange("p (r o) -> p r o", o=1).to_broadcast([E, NR, NOV])
                link(nc.vector.tensor_tensor(OH[0:E, :, :],
                                             iotap[0:E, :].rearrange("p (o n) -> p o n", o=1).to_broadcast([E, NR, NOV]),
                                             wide(F1[0:E, 2, :]), ALU.is_equal))
                link.sync()
                link(nc.vector.tensor_tensor(OH[0:E, :, :], OH[0:E, :, :], wide(F1[0:E, 0, :]), ALU.mult))
                link.sync()
                link(nc.vector.tensor_reduce(OS[0:E, 0, :], OH[0:E, :, :].rearrange("p r n -> p n r"), AX, ALU.add))
                link.sync()
                link(nc.vector.tensor_tensor(OH[0:E, :, :], OH[0:E, :, :], wide(rbase[0:E, :]), ALU.mult))
                link.sync()
                link(nc.vector.tensor_reduce(OS[0:E, 1, :], OH[0:E, :, :].rearrange("p r n -> p n r"), AX, ALU.add))
                link.sync()
                v.sem_inc(q["over_dve"], 1)
                v.wait_ge(q["over_pe"], 2)
                link(nc.vector.tensor_copy(elist[0:1, :], PS[0:1, 5, 0:NOV]))
                link(nc.vector.tensor_reduce(cntf[0:1, 0:1], PS[0:1, 5, NOV:2 * NOV:2], AX, ALU.add))
                link(nc.vector.tensor_copy(TR4[0:E, :, :].rearrange("p m t -> p (m t)"), PS[0:E, 6, :]))
                link.sync()
                link(nc.vector.tensor_copy(cnti[0:1, 2 * l + 1:2 * l + 2], cntf[0:1, 0:1]))
                link.sync()
                v.sem_inc(q["over_dve"], 1)
                v.wait_ge(q["over_pe"], 3)
                link(nc.vector.tensor_scalar(RKX[:, :, E:E + NOV],
                                             PS[:, 7, 0:2 * NOV].rearrange("p (t n) -> p t n", t=TT), -1.0, None, ALU.add))
                link(nc.vector.tensor_copy(GX[:, :, E:E + NOV],
                                           PS[:, 7, 2 * NOV:4 * NOV].rearrange("p (t n) -> p t n", t=TT)))
                link.sync()
                v.sem_inc(q["over_dve"], 1)
                v.sem_inc(q["over_list"], 1)
                rounds = nc.vector.value_load(cnti[0:1, 2 * l + 1:2 * l + 2], min_val=1, max_val=NOV // 2)
                with v.Fori(0, rounds) as i:
                    link.enter(i, 0, 4)
                    v.wait_ge(q["over_free"], i + 1)
                    onehot(v, link, i + PAIRS, 0, q["over_dve"])
                    v.wait_ge(q["over_pe"], 5 * i + 4)
                    link(copy_gathered(nc.vector.tensor_copy, 0))
                    copy_gathered(nc.vector.tensor_copy, 1).then_inc(q["over_dve"], 1)
                    v.wait_ge(q["over_act"], i + 1)
                    hidden(q["over_dve"])
                    v.wait_ge(q["over_pe"], 5 * i + 6)
                    link(copy_hidden())
                    nc.vector.tensor_copy(GT[0:2 * B, :, :].rearrange("p t b -> p (t b)"),
                                          PS[0:2 * B, 4, T:2 * T]).then_inc(q["over_dve"], 1)
                    v.wait_ge(q["over_pe"], 5 * i + 7)
                    link(nc.vector.tensor_copy(Y[0:2 * B, 0:512], PS[0:2 * B, 5, :]))
                    nc.vector.tensor_copy(Y[0:2 * B, 512:1024], PS[0:2 * B, 6, :]).then_inc(q["over_dve"], 1)
                link.leave(NOV // 2)

            def gp_moe(g):
                part = lambda n: XB[:, n, :, :].rearrange("p t d -> p (t d)")
                for n in range(2):
                    g.wait_ge(q["x_part"], n + 1)
                    src = X[:, :, :].rearrange("p t d -> p (t d)") if n == 0 else XR
                    if n:
                        g.wait_ge(q["x_rest"], 1)
                    nc.gpsimd.tensor_tensor(XR, src, part(n), ALU.subtract).then_inc(q["x_rest"], 1)

            return dict(prefetch=prefetch, loads=loads, pe=pe_moe, gp=gp_moe, act=act_moe, dve=dve_moe)

        moe = [moe_view(l) for l in range(2)]
        out_t = a["out"][0].rearrange("(t p) d -> p t d", p=P)

        with nc.Block() as block:
            @block.sync
            def _(sp):
                sp_mix0(sp)
                if STOP > 1:
                    moe[0]["prefetch"](sp)
                    moe[0]["loads"](sp)
                if STOP > 2:
                    sp_mix1(sp)
                if STOP > 3:
                    moe[1]["prefetch"](sp)
                    moe[1]["loads"](sp)
                sp.wait_ge(s_ln, TT * STOP)
                sp.dma_start(out_t, X[:, :, :]).then_inc(s_out, 16)
                sp.wait_ge(s_out, 16)

            @block.gpsimd
            def _(g):
                constants(g)
                gp_mix0(g)
                if STOP > 1:
                    moe[0]["gp"](g)
                if STOP > 2:
                    gp_mix1(g)
                if STOP > 3:
                    moe[1]["gp"](g)

            @block.scalar
            def _(s):
                act_mix0(s)
                act_ln(s, 0)
                if STOP > 1:
                    moe[0]["act"](s)
                    act_ln(s, 1)
                if STOP > 2:
                    act_mix1(s)
                    act_ln(s, 2)
                if STOP > 3:
                    moe[1]["act"](s)
                    act_ln(s, 3)

            @block.vector
            def _(v):
                link = Link(v, s_dve)
                dve_mix0(v, link)
                layer_norm(v, link, 0)
                if STOP > 1:
                    moe[0]["dve"](v, link)
                    layer_norm(v, link, 1)
                if STOP > 2:
                    dve_mix1(v, link)
                    layer_norm(v, link, 2)
                if STOP > 3:
                    moe[1]["dve"](v, link)
                    layer_norm(v, link, 3)

            @block.tensor
            def _(pe):
                pe_mix0(pe)
                if STOP > 1:
                    moe[0]["pe"](pe)
                if STOP > 2:
                    pe_mix1(pe)
                if STOP > 3:
                    moe[1]["pe"](pe)


_INS = ["x", "ln_mix_g", "ln_mix_b", "ln_ffn_g", "ln_ffn_b", "ab_w_in", "ab_pool_w", "ab_pool_scale", "ab_w_out",
        "rw_mu", "rw_w_r", "rw_w_k", "rw_w_v", "rw_w_w1", "rw_w_w2", "rw_w0", "rw_a1", "rw_a2", "rw_a0",
        "rw_g1", "rw_g2", "rw_k_k", "rw_k_a", "rw_r_k", "rw_lnx_g", "rw_lnx_b", "rw_w_o",
        "moe_w_router", "moe_e_bias", "moe_w_gate", "moe_w_up", "moe_w_down",
        "moe_ws_gate", "moe_ws_up", "moe_ws_down"]


def kernel(**inputs):
    import numpy as _np
    import concourse.bacc as _bacc
    from concourse import mybir as _mybir
    from concourse.bass_utils import run_bass_kernel_spmd as _run

    nc = _bacc.Bacc("TRN2", target_bir_lowering=False, num_devices=1)
    arrays, args = {}, {}
    for name in _INS:
        v = _np.ascontiguousarray(inputs[name])
        arrays[f"in_{name}"] = v
        args[name] = nc.dram_tensor(f"in_{name}", v.shape, _mybir.dt.from_np(v.dtype), kind="ExternalInput").ap()
    args["out"] = nc.dram_tensor("out_x", (1, T, D), F32, kind="ExternalOutput").ap()
    program(nc, args)
    r = _run(nc, [arrays], core_ids=[0])
    return r.results[0]["out_x"]
```

```python
import math
from contextlib import ExitStack

import numpy as np

import concourse.bass as bass
from concourse import mybir

P = 128
D = 1024
T = 256
TT = T // P
KT = D // P
E = 64
FF = 256
FT = FF // P
NG = 8
GE = E // NG
TOPG = 4
B = 64
NR = T // B - 1
NOV = T * 8 // B
PAIRS = E // 2
H0 = 8
HD = 64
CH = 64
NCH = T // CH
ALPHA = 4.0 ** 0.25
LN_EPS = 1e-5
GN_EPS = 64e-5
CDEC = math.exp(-0.5)
BIG = 1.0e30
LEVELS = 5
CB = 256
STOP = 4

F32 = mybir.dt.float32
I32 = mybir.dt.int32
BF16 = mybir.dt.bfloat16
ALU = mybir.AluOpType
ACT = mybir.ActivationFunctionType
AX = mybir.AxisListType.X
ds = bass.ds


class Link:

    def __init__(self, eng, sem):
        self.eng, self.sem, self.base, self.n = eng, sem, 0, 0

    def __call__(self, ins):
        ins.then_inc(self.sem, 1)
        self.n += 1

    def sync(self):
        self.eng.wait_ge(self.sem, self.base + self.n)

    def enter(self, i, first, per):
        self.start, self.per = self.base + self.n, per
        self.base, self.n = self.start + (i - first) * per, 0

    def leave(self, count):
        assert self.n == self.per, (self.n, self.per)
        self.base, self.n = self.start + count * self.per, 0


def program(nc, a):
    ctx = ExitStack()
    with ctx:
        def sb(name, shape, dt=F32):
            return ctx.enter_context(nc.sbuf_tensor(name, shape, dt))

        def sem(name):
            return ctx.enter_context(nc.semaphore(name))

        X = sb("X", [P, TT, D])
        xT = sb("xT", [P, KT, T])
        GB = sb("GB", [P, 2, D])
        RING = sb("RING", [P, 3, 6144])
        WR = sb("WR", [P, 2, KT, E])
        EB = sb("EB", [P, 2, E])
        ident = sb("ident", [P, P])
        ones = sb("ones", [P, P])
        before = sb("before", [P, P])
        bones = sb("bones", [P, P])
        iotab = sb("iotab", [P, B])
        tri8 = sb("tri8", [P, NG, NG])
        MK = sb("MK", [P, 2, P])
        LM = sb("LM", [P, 6, P])
        m01 = sb("m01", [P, T])
        MU = sb("MU", [P, 6, KT])
        VEC = sb("VEC", [P, 8, KT])
        V_W0, V_A0, V_KK, V_KA, V_RK, V_LG, V_LB, V_1KA = range(8)
        thr = sb("thr", [P, NR])
        rbase = sb("rbase", [P, NR])
        iotap = sb("iotap", [P, NOV])
        ecol = sb("ecol", [P, 1])
        ioi = sb("ioi", [P, T + 1], I32)
        elist = sb("elist", [1, NOV], I32)
        stat = sb("stat", [P, 2, 6])
        mv = sb("mv", [P, 4])
        cnti = sb("cnti", [1, 4], I32)
        AFL = 24960
        AR = sb("AR", [P, AFL])
        PS = ctx.enter_context(nc.psum_tensor("PS", [P, 8, 512], F32))

        class Area:
            def __init__(self, buf, at=0, end=None):
                self.buf, self.at, self.end = buf, at, end

            def __call__(self, *shape):
                n = int(np.prod(shape))
                v = self.buf[:, self.at:self.at + n]
                self.at += n
                assert self.at <= self.end, (self.at, self.end)
                if len(shape) == 1:
                    return v
                names = "abcd"[:len(shape)]
                return v.rearrange(f"p ({' '.join(names)}) -> p {' '.join(names)}",
                                   **{c: s for c, s in zip(names, shape)})

        flat = RING[:, :, :].rearrange("p s f -> p (s f)")
        am = Area(AR, 0, AFL)
        odd = am(2, 6144)

        def wslot(s):
            w = RING[:, s + 1, :] if s < 2 else odd[:, s - 2, :]
            return (w[:, 0:2048].rearrange("p (k f) -> p k f", k=KT),
                    w[:, 2048:4096].rearrange("p (k f) -> p k f", k=KT),
                    w[:, 4096:6144].rearrange("p (k f) -> p k f", k=FT))

        SCO = am(TT, E)
        BIA = am(TT, E)
        top2 = am(TT * NG, 8)
        grp = am(TT, NG)
        cmpa = am(TT, NG, NG)
        cmpb = am(TT, NG, NG)
        gcnt = am(TT, NG)
        gpen = am(TT, NG)
        MSK = am(TT, E)
        REP = am(TT, E)
        top8 = am(TT, 8)
        SEL = am(TT, E)
        gsum = am(TT)
        RKX = am(TT, E + NOV)
        GX = am(TT, E + NOV)
        HS = am(FT, T)
        HSs = am(FT, T)
        XB = am(3 * TT * D // 2).bitcast(BF16).rearrange("p (n t d) -> p n t d", n=3, t=TT)
        XR = am(TT * D)
        SEL1 = am(2 * TT * B).bitcast(BF16).rearrange("p (u t s b) -> p u t s b", u=2, t=TT, s=2)
        SELG = am(2, TT, 2, B)
        XG = am(KT, 2 * B)
        SIL = am(FF)
        HH = am(FF)
        HT = am(FT, 2 * B)
        GT = am(TT, P)
        Y = am(D)
        F1 = am(3, NR)
        OH = am(NR, NOV)
        OS = am(2, NOV)
        TR4 = am(4, P)
        F2 = am(E)
        CNT = am(E)
        cntf = am(2)
        ax = Area(AR, 0, AFL)
        WB = ax(2, 2048)
        mix0 = ax.at
        a0_ = Area(AR, mix0, AFL)
        UQK = a0_(12, T)
        V0 = a0_(TT, 512)
        CAT = a0_(KT, T)
        ZM = a0_(H0, T)
        BET = a0_(H0, T)
        FFT = a0_(H0, T + 1)
        IPR = a0_(H0, T + 1)
        Z1 = a0_(H0, T + 1)
        WT = a0_(2 * H0, P)
        MQ = a0_(TT, T)
        a0b = Area(flat, 12288, 18432)
        PW = a0b(4, P)
        PSC = a0b(4)
        WS1 = a0b(4, T)
        WS2 = a0b(4, T)
        ICN = a0b(4, T)
        DIF = a0b(4, T)
        a1_ = Area(AR, mix0, AFL)
        RT = a1_(KT, T)
        KTT = a1_(KT, T)
        V1 = a1_(TT, D)
        AT = a1_(KT, T)
        GTT = a1_(KT, T)
        SG = a1_(KT, T)
        g2b = a1_(D)
        l1x = a1_.at
        XX = a1_(KT, T)
        XM = a1_(2, KT, T)
        a1s = Area(flat, 12288, 18432)
        w1 = a1s(KT, 64)
        a1w = a1s(KT, 64)
        g1 = a1s(KT, 160)
        w2 = a1s(D)
        a2 = a1s(D)
        g2a = a1s(D)
        LH = a1_(4, T)
        class Pair:
            def __init__(self, area_a, area_b):
                take = lambda *shape: (area_a if area_a.at + int(np.prod(shape)) <= area_a.end else area_b)(*shape)
                self.MP = take(2, TT, 2, P)
                self.NQ = take(2, TT, 2, P)
                self.KR = take(TT, 2, P)
                self.BKT = take(2, TT, P)
                self.SS = take(NCH, P)
                self.LVL = take(2, 4, P)
                inv = take(3, 4, P)
                self.XI, self.DG, self.DT = inv[:, 0], inv[:, 1], inv[:, 2]
                early = inv.rearrange("p a b (c d) -> p (a b c d)", d=P)
                (self.LC, self.LCX, self.KKR, self.KK, self.KM, self.E3) = [early[:, n * T:(n + 1) * T] for n in range(6)]
                self.BI, self.KI = take(T), take(T)
                self.YY, self.YC = self.BI, self.KI
                self.VT = take(T)
                self.VP = take(TT, P)
                self.R1 = take(TT, P)
                self.UU = take(TT, P)
                self.SD = take(P)
                self.BON = take(T)
                self.E1, self.E2, self.SQ, self.TMP = take(T), take(T), take(T), take(T)
                self.YQ = self.E2

        area_a = Area(AR, l1x, AFL)
        area_b = Area(flat, 6144, 18432)
        pairs = [Pair(area_a, area_b) for _ in range(2)]

        s_const = sem("constants_ready")
        s_g2d = sem("gpsimd_steps")
        s_dve = sem("vector_steps")
        s_act = sem("scalar_steps")
        s_vec = sem("vectors_loaded")
        s_x = sem("x_loaded")
        s_gb = sem("ln_params_loaded")
        s_ln = sem("ln_done")
        s_var = sem("ln_variance_ready")
        s_std = sem("ln_deviation_ready")
        s_tr = sem("x_transposed")
        s_xT = sem("xT_ready")
        s_wl = [sem(f"mixer_chunk_loaded{b}") for b in range(2)]
        s_wf = sem("mixer_chunk_used")
        s_pj = sem("projection_done")
        s_pe = sem("projection_copied")
        s_res = sem("residual_done")
        s_out = sem("out_stored")

        def dve_transpose_copy(v, st):
            for n in range(4):
                if n % 2 == 0:
                    v.wait_ge(s_tr, 4 * st + n + 1)
                    nc.vector.tensor_copy(xT[:, 4 * (n % 2):4 * (n % 2) + 4, P * (n // 2):P * (n // 2) + P],
                                          PS[:, 4 + n, :].rearrange("p (k t) -> p k t", k=4)).then_inc(s_xT, 1)

        def act_transpose_copy(s, st):
            for n in range(4):
                if n % 2 == 1:
                    s.wait_ge(s_tr, 4 * st + n + 1)
                    nc.scalar.copy(xT[:, 4 * (n % 2):4 * (n % 2) + 4, P * (n // 2):P * (n // 2) + P],
                                   PS[:, 4 + n, :].rearrange("p (k t) -> p k t", k=4)).then_inc(s_xT, 1)

        def pe_transpose(pe, st):
            if st == 0:
                pe.wait_ge(s_x, 16)
                pe.wait_ge(s_const, 1)
            else:
                pe.wait_ge(s_ln, TT * st)
            for n in range(4):
                for k in range(4):
                    ins = nc.tensor.transpose(PS[:, 4 + n, k * P:(k + 1) * P],
                                              X[:, n // 2, (4 * (n % 2) + k)::KT], ident[:, :])
                ins.then_inc(s_tr, 1)

        def layer_norm(v, link, st):
            v.wait_ge(s_res, st + 1)
            v.wait_ge(s_gb, 32 * (st + 1))
            for t in range(TT):
                for h in range(2):
                    link(nc.vector.scalar_tensor_tensor(out=X[:, t, 512 * h:512 * h + 512],
                                                        in0=X[:, t, 512 * h:512 * h + 512], scalar=ALPHA,
                                                        in1=PS[:, 2 * t + h, :], op0=ALU.mult, op1=ALU.add))
                link.sync()
                for h in range(2):
                    link(nc.vector.bn_stats(stat[:, h, :], X[:, t, 512 * h:512 * h + 512]))
                link.sync()
                link(nc.vector.bn_aggr(mv[:, 0:2], stat[:, :, :]))
                link.sync()
                nc.vector.tensor_scalar(mv[:, 3:4], mv[:, 1:2], LN_EPS, None, ALU.add).then_inc(s_var, 1)
                v.wait_ge(s_std, TT * st + t + 1)
                link(nc.vector.reciprocal(mv[:, 2:3], mv[:, 3:4]))
                link.sync()
                link(nc.vector.tensor_scalar(X[:, t, :], X[:, t, :], mv[:, 0:1], mv[:, 2:3], ALU.subtract, ALU.mult))
                link.sync()
                link(nc.vector.tensor_tensor(X[:, t, :], X[:, t, :], GB[:, 0, :], ALU.mult))
                link.sync()
                nc.vector.tensor_tensor(X[:, t, :], X[:, t, :], GB[:, 1, :], ALU.add).then_inc(s_ln, 1)

        def act_ln(s, st):
            for t in range(TT):
                s.wait_ge(s_var, TT * st + t + 1)
                nc.scalar.activation(mv[:, 3:4], mv[:, 3:4], ACT.Sqrt).then_inc(s_std, 1)

        def load_ln(sp, st):
            g, b = (a["ln_mix_g"], a["ln_mix_b"]) if st % 2 == 0 else (a["ln_ffn_g"], a["ln_ffn_b"])
            l = st // 2
            if st:
                sp.wait_ge(s_ln, TT * st)
            sp.dma_start(GB[:, 0, :], g[l:l + 1, :].to_broadcast([P, D])).then_inc(s_gb, 16)
            sp.dma_start(GB[:, 1, :], b[l:l + 1, :].to_broadcast([P, D])).then_inc(s_gb, 16)

        def chunk(i):
            return WB[:, i % 2, :].rearrange("p (k c) -> p k c", k=KT)

        def load_chunk(sp, src, b, c):
            sp.dma_start(chunk(b), src[:, :, ds(c * CB, CB)]).then_inc(s_wl[b], 16)

        def stream(sp, src, n0, tile0, count):
            lead = 1 if n0 == 0 else 0
            for b in range(2 * lead):
                load_chunk(sp, src, b, b)
            with sp.Fori(lead, count // 2) as i:
                for b in range(2):
                    sp.wait_ge(s_pj, 4 * i + (tile0 + 2 * (n0 + b) - 2))
                    load_chunk(sp, src, b, 2 * i + b)

        def stream_out(sp, src, l, n0, tile0):
            for c in range(4):
                if c < 2:
                    sp.wait_ge(s_pj, tile0 + 2 * (n0 + c) - 2)
                else:
                    sp.wait_ge(s_wf, 4 * l + c - 1)
                load_chunk(sp, src, c % 2, c)

        def project_channels(pe, x, base, chunks, tile0):
            with pe.Fori(0, chunks // 2) as i:
                for b in range(2):
                    pe.wait_ge(s_wl[b], 16 * i + 16 * (base // 2 + 1))
                    for c in range(2):
                        pe.wait_ge(s_pe, 4 * i + (tile0 + 2 * b + c + 1))
                        for k in range(KT):
                            ins = nc.tensor.matmul(PS[:, 4 + 2 * b + c, 0:T], chunk(b)[:, k, c * P:(c + 1) * P],
                                                   x[:, k, :], start=(k == 0), stop=(k == KT - 1))
                        ins.then_inc(s_pj, 1)

        def project_tokens(pe, x, base, chunks, tile0):
            with pe.Fori(0, chunks // 2) as i:
                for b in range(2):
                    pe.wait_ge(s_wl[b], 16 * i + 16 * (base // 2 + 1))
                    for t in range(TT):
                        pe.wait_ge(s_pe, 4 * i + (tile0 + 2 * b + t + 1))
                        for k in range(KT):
                            ins = nc.tensor.matmul(PS[:, 4 + 2 * b + t, 0:CB], x[:, k, t * P:(t + 1) * P],
                                                   chunk(b)[:, k, :], start=(k == 0), stop=(k == KT - 1))
                        ins.then_inc(s_pj, 1)

        def out_project(pe, x, base, l):
            for c in range(4):
                g = base + c
                pe.wait_ge(s_wl[g % 2], 16 * (g // 2 + 1))
                for t in range(TT):
                    for k in range(KT):
                        ins = nc.tensor.matmul(PS[:, 2 * t + c // 2, (c % 2) * CB:(c % 2) * CB + CB],
                                               x[:, k, t * P:(t + 1) * P], chunk(g)[:, k, :],
                                               start=(k == 0), stop=(k == KT - 1))
                ins.then_inc(s_wf, 1)
            pe.wait_ge(s_wf, 4 * l + 4)
            pe.sem_inc(s_res, 1)

        def copy_tiles(s, dst, tile0, iters):
            with s.Fori(0, iters) as i:
                for n in range(4):
                    s.wait_ge(s_pj, 4 * i + (tile0 + n + 1))
                    nc.scalar.copy(dst[:, ds(4 * i + n, 1), :], PS[:, 4 + n:5 + n, 0:T]).then_inc(s_pe, 1)

        def constants(g):
            link = Link(g, s_g2d)
            L.append(link)

            def keep(dst, pattern, base, mult, op, fill=0.0):
                link(nc.gpsimd.affine_select(out=dst, in_=dst, compare_op=op, fill=fill, base=base,
                                             pattern=pattern, channel_multiplier=mult))

            link(nc.gpsimd.memset(ident[:, :], 0.0))
            link.sync()
            keep(ident[:, :], [[-1, P]], 0, 1, ALU.not_equal, 1.0)
            link.sync()
            g.sem_inc(s_const, 1)
            for dst, val in ((ones[:, :], 1.0), (before[:, :], 1.0), (bones[:, :], 0.0),
                             (tri8[:, :, :], 1.0), (MK[:, :, :], 1.0), (LM[:, :, :], 1.0), (m01[:, :], 1.0),
                             (Z1[:, :, :], 0.0), (FFT[:, :, T:T + 1], 0.0), (MQ[:, :, :], 0.0)):
                link(nc.gpsimd.memset(dst, val))
            link(nc.gpsimd.iota(ioi[:, 0:T], pattern=[[1, T]], base=0, channel_multiplier=0))
            link(nc.gpsimd.iota(ioi[:, T:T + 1], pattern=[[1, 1]], base=0, channel_multiplier=1))
            link.sync()

            keep(before[:, :], [[1, P]], 0, -1, ALU.is_gt)
            keep(tri8[:, :, :], [[1, NG], [-1, NG]], 0, 0, ALU.is_gt)
            keep(MK[:, 0, :], [[1, P]], 0, -1, ALU.is_gt)
            keep(MK[:, 1, :], [[1, P]], 0, -1, ALU.is_ge)
            for q in range(TT):
                keep(MQ[:, q, :], [[-1, T]], q * P, 1, ALU.is_gt, -BIG)
            link.sync()
            for c in range(2):
                link(nc.gpsimd.memset(bones[c * HD:(c + 1) * HD, c * HD:(c + 1) * HD], 1.0))
                link.sync()
            for c in range(NCH):
                link(nc.gpsimd.memset(m01[:, c * CH:c * CH + 1], 0.0))
            link(nc.gpsimd.memset(Z1[:, :, T:T + 1], 1.0))
            link.sync()
            link(nc.gpsimd.memset(MK[0:CH, :, CH:P], 0.0))
            link.sync()
            for lv in range(6):
                w = 1 << lv
                nb = P // (2 * w)
                v = LM[:, lv, :].rearrange("p (n t) -> p n t", t=2 * w)
                lo, hi = v[:, :, 0:w], v[:, :, w:2 * w]
                link(nc.gpsimd.memset(lo, 0.0))
                for pattern, base, mult in (([[-2 * w, nb], [0, w]], 0, 1), ([[2 * w, nb], [0, w]], w - 1, -1)):
                    keep(hi, pattern, base, mult, ALU.is_ge)
                    link.sync()
            for g_, win in enumerate((2, 4, 8, 16)):
                link(nc.gpsimd.tensor_scalar(ICN[:, g_, :], ioi[:, 0:T], 1.0, float(win), ALU.add, ALU.min))
            link(nc.gpsimd.tensor_copy(iotab[:, :], ioi[:, 0:B]))
            link(nc.gpsimd.tensor_copy(iotap[:, :], ioi[:, 0:NOV]))
            link(nc.gpsimd.tensor_copy(ecol[:, :], ioi[:, T:T + 1]))
            link(nc.gpsimd.tensor_scalar(thr[:, :], ioi[:, 1:NR + 1], float(B), None, ALU.mult))
            link(nc.gpsimd.tensor_scalar(rbase[:, :], ioi[:, 1:NR + 1], -float(B), 1.0, ALU.mult, ALU.add))
            link.sync()
            g.sem_inc(s_const, 1)

        L = []

        s_pw = sem("pool_weights_loaded")
        s_dif = sem("pool_differences_ready")
        s_yp = sem("pool_product_done")
        s_cat = sem("mixed_heads_ready")
        s_z = sem("scores_done")
        s_zm = sem("masked_scores_ready")
        s_sig = sem("sigmoids_ready")
        s_w = sem("stick_weights_ready")
        s_wt = sem("stick_weights_transposed")
        s_wtc = sem("stick_weights_copied")
        s_o = sem("heads_done")
        s_l0c = sem("layer0_constants_ready")
        L0CH = 8 + 4
        w_in = a["ab_w_in"][0].rearrange("(p k) c -> p k c", k=KT)
        w_out = a["ab_w_out"][0].rearrange("(k p) c -> p k c", p=P)

        def sp_mix0(sp):
            sp.dma_start(X[:, :, :], a["x"][0].rearrange("(t p) d -> p t d", p=P)).then_inc(s_x, 16)
            stream(sp, w_in, 0, 0, 8)
            sp.dma_start(PW[:, :, :], a["ab_pool_w"][0].rearrange("g c d -> c g d")).then_inc(s_pw, 16)
            with nc.allow_non_contiguous_dma(reason="a few short vectors"):
                sp.dma_start(PSC[:, :], a["ab_pool_scale"][0].rearrange("(g p) -> p g", p=P)).then_inc(s_pw, 16)
            load_ln(sp, 0)
            sp.dma_start(WR[:, :, :, :], a["moe_w_router"].rearrange("l (p k) e -> p l k e", k=KT)).then_inc(s_vec, 16)
            sp.dma_start(EB[:, :, :].rearrange("p l e -> p (l e)"),
                         a["moe_e_bias"].rearrange("(o l) e -> o (l e)", o=1).to_broadcast([P, 2 * E])).then_inc(s_vec, 16)
            with nc.allow_non_contiguous_dma(reason="a few short vectors"):
                sp.dma_start(MU[:, :, :], a["rw_mu"][0].rearrange("m (p k) -> p m k", k=KT)).then_inc(s_vec, 16)
                for n, name in enumerate(["rw_w0", "rw_a0", "rw_k_k", "rw_k_a", "rw_r_k", "rw_lnx_g", "rw_lnx_b"]):
                    v = a[name][0] if name != "rw_r_k" else a[name][0].rearrange("h n -> (h n)")
                    sp.dma_start(VEC[:, n, :], v.rearrange("(k p) -> p k", p=P)).then_inc(s_vec, 16)
            stream_out(sp, w_out, 0, 8, 0)

        def gp_mix0(g):
            link_g = L[0]
            g.wait_ge(s_l0c, 1)
            g.wait_ge(s_pe, 4 + 4)
            src, w = UQK[:, 0:4, :], 1
            for lv, dst in enumerate([WS1, WS2, WS1, WS2]):
                link_g(nc.gpsimd.tensor_tensor(dst[:, lv:4, w:T], src[:, lv:4, w:T], src[:, lv:4, 0:T - w], ALU.add))
                link_g(nc.gpsimd.tensor_copy(dst[:, lv:4, 0:w], src[:, lv:4, 0:w]))
                link_g.sync()
                link_g(nc.gpsimd.tensor_tensor(DIF[:, lv, :], dst[:, lv, :], ICN[:, lv, :], ALU.mult))
                link_g.sync()
                nc.gpsimd.tensor_tensor(DIF[:, lv, :], DIF[:, lv, :], UQK[:, lv, :], ALU.subtract).then_inc(s_dif, 1)
                src, w = dst, 2 * w

        def pe_mix0(pe):
            pe_transpose(pe, 0)
            pe.wait_ge(s_xT, 4)
            project_channels(pe, xT, 0, 6, 0)
            project_tokens(pe, xT, 6, 2, 12)
            pe.wait_ge(s_pw, 32)
            pe.wait_ge(s_dif, 4)
            for g in range(4):
                ins = nc.tensor.matmul(PS[:, g // 2, (g % 2) * T:(g % 2) * T + T], PW[:, g, :], DIF[:, g, :],
                                       start=True, stop=True)
            ins.then_inc(s_yp, 1)
            pe.wait_ge(s_pe, 4 + 16)
            for q in range(TT):
                if q:
                    pe.wait_ge(s_cat, 4 + 1)
                for h in range(H0):
                    r = HD * (h % 2)
                    n = 4 * (h % 2) + h // 2
                    ins = nc.tensor.matmul(PS[:, 4 + n // 2, (n % 2) * T:(n % 2) * T + T],
                                           UQK[r:r + HD, 4 + h // 2, q * P:(q + 1) * P],
                                           UQK[r:r + HD, 8 + h // 2, :], start=True, stop=True)
                ins.then_inc(s_z, 1)
                pe.wait_ge(s_w, q + 1)
                if q == 0:
                    pe.wait_ge(s_cat, 4)
                for n in range(H0):
                    for k in range(TT):
                        m = 2 * n + k
                        ins = nc.tensor.transpose(PS[:, m // 4, (m % 4) * P:(m % 4) * P + P],
                                                  BET[:, n, k * P:(k + 1) * P], ident[:, :])
                ins.then_inc(s_wt, 1)
                pe.wait_ge(s_wtc, q + 1)
                for h in range(H0):
                    n = 4 * (h % 2) + h // 2
                    r = HD * (h % 2)
                    for k in range(TT):
                        ins = nc.tensor.matmul(PS[r:r + HD, 4, (h // 2) * P:(h // 2) * P + P],
                                               V0[:, k, h * HD:(h + 1) * HD], WT[:, 2 * n + k, :],
                                               start=(k == 0), stop=(k == TT - 1))
                ins.then_inc(s_o, 1)
            pe.wait_ge(s_cat, 4 + 2)
            out_project(pe, CAT, 8, 0)

        def act_mix0(s):
            s.sem_inc(s_pe, 4)
            act_transpose_copy(s, 0)
            s.wait_ge(s_xT, 4)
            copy_tiles(s, UQK, 0, 3)
            for n in range(4):
                s.wait_ge(s_pj, 12 + n + 1)
                nc.scalar.copy(V0[:, n % 2, (n // 2) * CB:(n // 2) * CB + CB], PS[:, 4 + n, 0:CB]).then_inc(s_pe, 1)
            s.wait_ge(s_yp, 1)
            for g in range(4):
                nc.scalar.activation(CAT[:, g, :], PS[:, g // 2, (g % 2) * T:(g % 2) * T + T], ACT.Copy,
                                     scale=PSC[:, g:g + 1]).then_inc(s_cat, 1)
            for q in range(TT):
                s.wait_ge(s_zm, 4 * (q + 1))
                if q:
                    s.wait_ge(s_wt, q)
                nc.scalar.activation(FFT[:, :, 0:T], ZM[:, :, :], ACT.Sigmoid, scale=-1.0).then_inc(s_sig, 1)
                nc.scalar.activation(BET[:, :, :], ZM[:, :, :], ACT.Sigmoid).then_inc(s_sig, 1)
                s.wait_ge(s_wt, q + 1)
                for n in range(4):
                    ins = nc.scalar.copy(WT[:, 4 * n:4 * n + 4, :], PS[:, n, :].rearrange("p (m q) -> p m q", m=4))
                ins.then_inc(s_wtc, 1)
                s.wait_ge(s_o, q + 1)
                nc.scalar.copy(CAT[:, 4:8, q * P:(q + 1) * P],
                               PS[:, 4, :].rearrange("p (m q) -> p m q", m=4)).then_inc(s_cat, 1)

        def dve_mix0(v, link):
            v.wait_ge(s_const, 2)
            nc.vector.reciprocal(ICN[:, :, :], ICN[:, :, :]).then_inc(s_l0c, 1)
            dve_transpose_copy(v, 0)
            for q in range(TT):
                v.wait_ge(s_z, q + 1)
                if q:
                    v.wait_ge(s_sig, 2 * q)
                for n in range(4):
                    nc.vector.scalar_tensor_tensor(
                        out=ZM[:, 2 * n:2 * n + 2, :], in0=PS[:, 4 + n, :].rearrange("p (h k) -> p h k", h=2),
                        scalar=HD ** -0.5, in1=MQ[:, q:q + 1, :].to_broadcast([P, 2, T]),
                        op0=ALU.mult, op1=ALU.add).then_inc(s_zm, 1)
                v.wait_ge(s_sig, 2 * q + 1)
                fl = lambda m: m.rearrange("p h k -> p (h k)")[:, ::-1]
                link(nc.vector.tensor_tensor_scan(out=fl(IPR), data0=fl(FFT), data1=fl(Z1), initial=1.0,
                                                  op0=ALU.mult, op1=ALU.add))
                link.sync()
                v.wait_ge(s_sig, 2 * q + 2)
                nc.vector.tensor_tensor(BET[:, :, :], BET[:, :, :], IPR[:, :, 1:T + 1], ALU.mult).then_inc(s_w, 1)

        s_lw = sem("lora_weights_loaded")
        s_xm = sem("mixed_input_ready")
        s_lh = sem("lora_hidden_done")
        s_lhc = sem("lora_hidden_ready")
        names = ["log_decay_ready", "key_squares_ready", "head_sum_done", "mean_square_ready", "root_ready",
                 "bonus_terms_ready", "bonus_sum_done", "bonus_copied", "bonus_ready", "decays_ready",
                 "operands_ready", "values_ready", "turned", "turned_copied", "values_turned", "values_copied",
                 "gram_b_done", "gram_k_done", "gram_b_ready", "gram_k_ready", "level_ready", "inverse0_ready",
                 "inverse0_turned", "product_done", "product_ready", "inverse_done", "inverse_ready",
                 "rhs_done", "rhs_ready", "solution_done", "solution_ready", "increment_done", "state_ready",
                 "y_done", "y_ready", "mean_done", "centred_ready", "variance_done", "variance_ready",
                 "deviation_ready", "normed_ready", "pair_finished"]
        r = {n: sem("rwkv_" + n) for n in names}
        NPASS = KT // 2
        L1F = 12

        def sp_mix1(sp):
            sp.wait_ge(s_ln, 2 * TT)
            for n, (dst, src) in enumerate([
                    (w1, a["rw_w_w1"][0].rearrange("(p k) c -> p k c", k=KT)),
                    (a1w, a["rw_a1"][0].rearrange("(p k) c -> p k c", k=KT)),
                    (g1, a["rw_g1"][0].rearrange("(p k) c -> p k c", k=KT)),
                    (w2[0:64, :], a["rw_w_w2"][0]), (a2[0:64, :], a["rw_a2"][0]),
                    (g2a, a["rw_g2"][0][0:P, :]), (g2b[0:32, :], a["rw_g2"][0][P:160, :])]):
                sp.dma_start(dst, src).then_inc(s_lw, 16)
            load_ln(sp, 2)
            for m, name in enumerate(["rw_w_r", "rw_w_k", "rw_w_v"]):
                stream(sp, a[name][0].rearrange("(p k) c -> p k c", k=KT), 4 * m, 16, 4)
            stream_out(sp, a["rw_w_o"][0].rearrange("(k p) c -> p k c", p=P), 1, 12, 16)

        ORDER = [0, 2, 3, 1, 4, 5]

        def dve_mix1(v, link):
            dve_transpose_copy(v, 2)
            v.wait_ge(s_xT, 12)
            v.wait_ge(s_vec, 16 * 10)
            link(nc.vector.tensor_tensor(XX[:, :, 1:T], xT[:, :, 0:T - 1], xT[:, :, 1:T], ALU.subtract))
            link(nc.vector.tensor_scalar(XX[:, :, 0:1], xT[:, :, 0:1], -1.0, None, ALU.mult))
            link(nc.vector.tensor_scalar(VEC[:, V_1KA, :], VEC[:, V_KA, :], -1.0, 1.0, ALU.mult, ALU.add))
            link.sync()
            for n, m in enumerate(ORDER):
                if 2 <= n <= 4:
                    v.wait_ge(s_pj, 16 + 8 * (n - 1))
                if n == 5:
                    v.wait_ge(s_lh, 1)
                for k in range(KT):
                    ins = nc.vector.scalar_tensor_tensor(out=XM[:, n % 2, k, :], in0=XX[:, k, :],
                                                         scalar=MU[:, m, k:k + 1], in1=xT[:, k, :],
                                                         op0=ALU.mult, op1=ALU.add)
                ins.then_inc(s_xm, 1)
            v.wait_ge(s_lh, 4)
            v.wait_ge(s_xm, 6)
            v.wait_ge(s_pe, 4 + 16 + 16 + 8 + 24)
            for b in pairs:
                link(nc.vector.memset(b.SS[:, :, :], 0.0))
            link.sync()
            with v.Fori(0, NPASS) as i:
                link.enter(i, 0, DVE_STEPS)
                dve_pass(v, link, i)
            link.leave(NPASS)

        DVE_STEPS = 44
        both = list(enumerate(pairs))

        def at(i, z, count=1, n=0):
            return 2 * count * i + (2 * n + z + 1)

        def dve_pass(v, link, i):
            row = lambda m, z: m[:, ds(2 * i + z, 1), :].rearrange("p o t -> p (o t)")
            vec = lambda n, z: VEC[:, n, ds(2 * i + z, 1)]
            tiles = lambda m: m.rearrange("p (a t) -> p a t", a=TT)
            four = lambda bank: bank.rearrange("p (m t) -> p m t", m=4)
            eye = ident[:, :].rearrange("p (o t) -> p o t", o=1).to_broadcast([P, 4, P])
            V = nc.vector
            for z, b in both:
                v.wait_ge(r["pair_finished"], 2 * i + 2)
                link(V.tensor_tensor_scan(out=b.LC, data0=m01[:, :], data1=row(SG, z), initial=0.0,
                                          op0=ALU.mult, op1=ALU.add))
                link(V.tensor_scalar(b.KKR, row(KTT, z), vec(V_KK, z), None, ALU.mult))
            link.sync()
            for z, b in both:
                V.tensor_tensor(b.SQ, b.KKR, b.KKR, ALU.mult).then_inc(r["key_squares_ready"], 1)
                V.tensor_tensor(b.LCX, b.LC, row(SG, z), ALU.subtract).then_inc(r["log_decay_ready"], 1)
            for z, b in both:
                link(V.tensor_scalar(b.KM, row(AT, z), vec(V_KA, z), vec(V_1KA, z), ALU.mult, ALU.add))
            link.sync()
            for z, b in both:
                link(V.tensor_tensor(b.KM, b.KM, row(KTT, z), ALU.mult))
            for z, b in both:
                v.wait_ge(r["head_sum_done"], at(i, z))
                V.tensor_scalar(b.TMP, PS[:, 4 * z, 0:T], 1e-24, None, ALU.max).then_inc(r["mean_square_ready"], 1)
            link.sync()
            for z, b in both:
                V.scalar_tensor_tensor(out=b.SQ, in0=b.KM, scalar=vec(V_RK, z), in1=row(RT, z), op0=ALU.mult,
                                       op1=ALU.mult).then_inc(r["bonus_terms_ready"], 1)
            for z, b in both:
                v.wait_ge(r["root_ready"], at(i, z))
                link(V.reciprocal(b.TMP, b.TMP))
            link.sync()
            for z, b in both:
                link(V.tensor_tensor(b.KK, b.KKR, b.TMP, ALU.mult))
            link.sync()
            for z, b in both:
                v.wait_ge(r["decays_ready"], at(i, z))
                link(V.tensor_tensor(b.BI, b.KK, row(AT, z), ALU.mult))
                link(V.tensor_tensor(b.KR[:, :, 0, :], tiles(b.KK), tiles(b.E2), ALU.mult))
            link.sync()
            for z, b in both:
                link(V.tensor_tensor(b.BI, b.BI, b.E3, ALU.mult))
                link(V.tensor_tensor(b.KR[:, :, 1, :], row(RT, z).rearrange("p (a t) -> p a t", a=TT), tiles(b.E1),
                                     ALU.mult))
                V.tensor_tensor(b.KI, b.KM, b.E3, ALU.mult).then_inc(r["operands_ready"], 1)
            mask = MK[:, :, :].rearrange("p (o m) t -> p o (m t)", o=1).to_broadcast([P, TT, 2 * P])
            quad = lambda m: m[:, :, :, 0, :].rearrange("p h a t -> p (h a) t")

            def masked(dst, bank, sem_):
                for h in range(2):
                    ins = V.tensor_tensor(dst[:, h, :, :, :].rearrange("p a m t -> p a (m t)"),
                                          PS[:, bank + h, :].rearrange("p (a f) -> p a f", a=TT), mask, ALU.mult)
                    if h == 0:
                        link(ins)
                    else:
                        ins.then_inc(sem_, 1)

            for z, b in both:
                v.wait_ge(r["gram_b_done"], at(i, z))
                masked(b.MP, 4 * z, r["gram_b_ready"])
            for z, b in both:
                v.wait_ge(r["gram_b_ready"], at(i, z))
                link(V.tensor_tensor(b.XI, quad(b.MP), LM[:, 0:1, :].to_broadcast([P, 4, P]), ALU.mult))
            link.sync()
            for z, b in both:
                V.tensor_tensor(b.DT, eye, b.XI, ALU.subtract).then_inc(r["inverse0_ready"], 1)
            for z, b in both:
                v.wait_ge(r["gram_k_done"], at(i, z))
                masked(b.NQ, 4 * z + 2, r["gram_k_ready"])
            for lv in range(LEVELS):
                for z, b in both:
                    v.wait_ge(r["product_done"], at(i, z, LEVELS, lv))
                    V.tensor_tensor(b.XI, eye, four(PS[:, 4 * z, :]), ALU.subtract).then_inc(r["product_ready"], 1)
            for c in range(NCH):
                t, rows = c // 2, slice(CH * (c % 2), CH * (c % 2) + CH)
                if c < NCH - 1:
                    dc = [b.E1[:, CH * c + CH - 1:CH * c + CH] for b in pairs]
                    for z, b in both:
                        if c:
                            v.wait_ge(r["state_ready"], at(i, z, NCH - 1, c - 1))
                        link(V.tensor_scalar(b.SD, b.SS[:, c, :], dc[z], None, ALU.mult))
                for z, b in both:
                    v.wait_ge(r["solution_done"], at(i, z, NCH, c))
                    V.tensor_scalar(b.UU[rows, t, :], PS[rows, 4 * z + 1, 0:P], -1.0, None,
                                    ALU.mult).then_inc(r["solution_ready"], 1)
                if c < NCH - 1:
                    link.sync()
                    for z, b in both:
                        v.wait_ge(r["increment_done"], at(i, z, NCH - 1, c))
                        for h in range(2):
                            q = slice(HD * h, HD * h + HD)
                            ins = V.scalar_tensor_tensor(out=b.SS[q, c + 1, q], in0=PS[q, 4 * z + 2, q], scalar=dc[z][q, :],
                                                         in1=b.SD[q, q], op0=ALU.mult, op1=ALU.add)
                            if h == 0:
                                link(ins)
                            else:
                                ins.then_inc(r["state_ready"], 1)
            for z, b in both:
                v.wait_ge(r["mean_done"], at(i, z))
                link(V.scalar_tensor_tensor(out=b.YC, in0=PS[:, 4 * z, 0:T], scalar=-1.0 / HD, in1=b.YY,
                                            op0=ALU.mult, op1=ALU.add))
            link.sync()
            for z, b in both:
                V.tensor_tensor(b.YQ, b.YC, b.YC, ALU.mult).then_inc(r["centred_ready"], 1)
            for z, b in both:
                v.wait_ge(r["variance_done"], at(i, z))
                V.tensor_scalar(b.TMP, PS[:, 4 * z + 1, 0:T], 1.0 / HD, GN_EPS, ALU.mult,
                                ALU.add).then_inc(r["variance_ready"], 1)
            for z, b in both:
                v.wait_ge(r["deviation_ready"], at(i, z))
                link(V.reciprocal(b.TMP, b.TMP))
            link.sync()
            for z, b in both:
                link(V.tensor_tensor(b.YC, b.YC, b.TMP, ALU.mult))
            link.sync()
            for z, b in both:
                V.tensor_scalar(b.YC, b.YC, vec(V_LG, z), vec(V_LB, z), ALU.mult, ALU.add).then_inc(r["normed_ready"], 1)

        def act_mix1(s):
            act_transpose_copy(s, 2)
            s.wait_ge(s_xT, 12)
            copy_tiles(s, RT, 16, 2)
            copy_tiles(s, KTT, 24, 2)
            with s.Fori(0, 2) as i:
                for n in range(4):
                    s.wait_ge(s_pj, 4 * i + (32 + n + 1))
                    nc.scalar.copy(V1[:, n % 2, ds((2 * i + n // 2) * CB, CB)], PS[:, 4 + n, 0:CB]).then_inc(s_pe, 1)
            s.wait_ge(s_lh, 1)
            nc.scalar.activation(LH[0:64, 0, :], PS[0:64, 0, 0:T], ACT.Tanh).then_inc(s_lhc, 1)
            s.wait_ge(s_lh, 2)
            nc.scalar.copy(LH[0:64, 1, :], PS[0:64, 1, 0:T]).then_inc(s_lhc, 1)
            s.wait_ge(s_lh, 4)
            nc.scalar.activation(LH[:, 2, :], PS[:, 2, 0:T], ACT.Sigmoid).then_inc(s_lhc, 1)
            nc.scalar.activation(LH[0:32, 3, :], PS[0:32, 3, 0:T], ACT.Sigmoid).then_inc(s_lhc, 1)
            for m in range(3):
                dst = (SG, AT, GTT)[m]
                with s.Fori(0, 2) as i:
                    for n in range(4):
                        s.wait_ge(s_pj, 4 * i + (40 + 8 * m + n + 1))
                        o = dst[:, ds(4 * i + n, 1), :].rearrange("p o t -> p (o t)")
                        if m < 2:
                            ins = nc.scalar.activation(o, PS[:, 4 + n, 0:T], ACT.Sigmoid,
                                                       bias=VEC[:, V_W0 + m, ds(4 * i + n, 1)])
                        else:
                            ins = nc.scalar.copy(o, PS[:, 4 + n, 0:T])
                        ins.then_inc(s_pe, 1)
            s.wait_ge(s_pe, 4 + 16 + 24 + 24)
            with s.Fori(0, NPASS) as i:
                act_pass(s, i)

        def act_pass(s, i):
            four = lambda bank: bank.rearrange("p (m t) -> p m t", m=4)
            A = nc.scalar
            for z, b in both:
                s.wait_ge(r["pair_finished"], 2 * i + 2)
                A.copy(b.VP[:, :, :], V1[:, :, ds(P * (2 * i + z), P)]).then_inc(r["values_ready"], 1)
            for z, b in both:
                s.wait_ge(r["log_decay_ready"], at(i, z))
                A.activation(b.E1, b.LC, ACT.Exp, scale=-CDEC)
                A.activation(b.E2, b.LCX, ACT.Exp, scale=-CDEC)
                A.activation(b.E3, b.LC, ACT.Exp, scale=CDEC).then_inc(r["decays_ready"], 1)
            for z, b in both:
                s.wait_ge(r["mean_square_ready"], at(i, z))
                A.activation(b.TMP, b.TMP, ACT.Sqrt).then_inc(r["root_ready"], 1)
            for z, b in both:
                s.wait_ge(r["values_turned"], at(i, z))
                A.copy(b.VT, PS[:, 4 * z + 2, 0:T]).then_inc(r["values_copied"], 1)
            for z, b in both:
                s.wait_ge(r["bonus_sum_done"], at(i, z))
                A.copy(b.BON, PS[:, 4 * z + 3, 0:T]).then_inc(r["bonus_copied"], 1)
            for z, b in both:
                s.wait_ge(r["turned"], at(i, z))
                A.copy(b.BKT[:, :, :, :].rearrange("p m a t -> p (m a t)"), PS[:, 4 * z + 1, :]).then_inc(r["turned_copied"], 1)
            for z, b in both:
                s.wait_ge(r["inverse0_turned"], at(i, z))
                A.copy(b.DG, four(PS[:, 4 * z + 1, :])).then_inc(r["inverse_ready"], 1)
            for lv in range(LEVELS):
                for z, b in both:
                    if lv < LEVELS - 1:
                        s.wait_ge(r["inverse_done"], at(i, z, LEVELS, lv))
                        A.copy(b.DG, four(PS[:, 4 * z + 1, :]))
                    else:
                        s.wait_ge(r["inverse_done"], at(i, z, LEVELS, lv))
                    A.copy(b.DT, four(PS[:, 4 * z + 2, :])).then_inc(r["inverse_ready"], 1)
            for c in range(NCH):
                t, rows = c // 2, slice(CH * (c % 2), CH * (c % 2) + CH)
                for z, b in both:
                    s.wait_ge(r["rhs_done"], at(i, z, NCH, c))
                    A.copy(b.R1[rows, t, :], PS[rows, 4 * z, 0:P]).then_inc(r["rhs_ready"], 1)
            for z, b in both:
                s.wait_ge(r["y_done"], at(i, z))
                A.copy(b.YY, PS[:, 4 * z + 3, 0:T]).then_inc(r["y_ready"], 1)
            for z, b in both:
                s.wait_ge(r["variance_ready"], at(i, z))
                A.activation(b.TMP, b.TMP, ACT.Sqrt).then_inc(r["deviation_ready"], 1)

        def gp_mix1(g):
            G = nc.gpsimd
            link = L[0]
            g.sem_inc(r["pair_finished"], 2)
            with g.Fori(0, NPASS) as i:
                link.enter(i, 0, 2)
                row = lambda m, z: m[:, ds(2 * i + z, 1), :].rearrange("p o t -> p (o t)")
                for z, b in both:
                    g.wait_ge(r["bonus_copied"], at(i, z))
                    g.wait_ge(r["values_copied"], at(i, z))
                    G.tensor_tensor(b.BON, b.BON, b.VT, ALU.mult).then_inc(r["bonus_ready"], 1)
                for lv in range(LEVELS):
                    for z, b in both:
                        if lv == 0:
                            g.wait_ge(r["gram_b_ready"], at(i, z))
                        if lv >= 2:
                            g.wait_ge(r["product_done"], at(i, z, LEVELS, lv - 2))
                        G.tensor_tensor(b.LVL[:, lv % 2], b.MP[:, :, :, 0, :].rearrange("p h a t -> p (h a) t"),
                                        LM[:, lv + 1:lv + 2, :].to_broadcast([P, 4, P]),
                                        ALU.mult).then_inc(r["level_ready"], 1)
                for z, b in both:
                    g.wait_ge(r["normed_ready"], at(i, z))
                    g.wait_ge(r["bonus_ready"], at(i, z))
                    link(G.tensor_tensor(b.YC, b.YC, b.BON, ALU.add))
                link.sync()
                for z, b in both:
                    G.tensor_tensor(row(RT, z), b.YC, row(GTT, z), ALU.mult).then_inc(r["pair_finished"], 1)
            link.leave(NPASS)

        def pe_mix1(pe):
            pe_transpose(pe, 2)
            pe.wait_ge(s_xT, 12)
            for n in range(2):
                pe.wait_ge(s_xm, n + 1)
                project_channels(pe, XM[:, n, :, :], L1F + 4 * n, 4, 16 + 8 * n)
            pe.wait_ge(s_xm, 3)
            project_tokens(pe, XM[:, 0, :, :], L1F + 8, 4, 32)
            pe.wait_ge(s_lw, 16 * 7)
            for n, (x, w, c0, m, bank) in enumerate([(1, w1, 0, 64, 0), (0, a1w, 0, 64, 1),
                                                     (1, g1, 0, P, 2), (1, g1, P, 32, 3)]):
                pe.wait_ge(s_xm, min(4 + n, 6))
                for k in range(KT):
                    ins = nc.tensor.matmul(PS[0:m, bank, 0:T], w[:, k, c0:c0 + m], XM[:, x, k, :],
                                           start=(k == 0), stop=(k == KT - 1))
                ins.then_inc(s_lh, 1)
            for m in range(3):
                pe.wait_ge(s_lhc, (1, 2, 4)[m])
                for n in range(KT):
                    pe.wait_ge(s_pe, 40 + 8 * m + n + 1)
                    cs = slice(n * P, (n + 1) * P)
                    if m < 2:
                        nc.tensor.matmul(PS[:, 4 + n % 4, 0:T], (w2, a2)[m][0:64, cs], LH[0:64, m, :],
                                         start=True, stop=True).then_inc(s_pj, 1)
                    else:
                        nc.tensor.matmul(PS[:, 4 + n % 4, 0:T], g2a[:, cs], LH[:, 2, :], start=True, stop=False)
                        nc.tensor.matmul(PS[:, 4 + n % 4, 0:T], g2b[0:32, cs], LH[0:32, 3, :],
                                         start=False, stop=True).then_inc(s_pj, 1)
            pe.wait_ge(s_pe, 4 + 16 + 24 + 24)
            with pe.Fori(0, NPASS) as i:
                pe_pass(pe, i)
            pe.wait_ge(r["pair_finished"], 2 * NPASS + 2)
            out_project(pe, RT, L1F + 12, 1)

        def pe_pass(pe, i):
            mm = nc.tensor.matmul
            for z, b in both:
                pe.wait_ge(r["pair_finished"], 2 * i + 2)
                pe.wait_ge(r["key_squares_ready"], at(i, z))
                mm(PS[:, 4 * z, 0:T], bones[:, :], b.SQ, start=True, stop=True).then_inc(r["head_sum_done"], 1)
            for z, b in both:
                pe.wait_ge(r["values_ready"], at(i, z))
                for t in range(TT):
                    ins = nc.tensor.transpose(PS[:, 4 * z + 2, t * P:(t + 1) * P], b.VP[:, t, :], ident[:, :])
                ins.then_inc(r["values_turned"], 1)
            for z, b in both:
                pe.wait_ge(r["bonus_terms_ready"], at(i, z))
                mm(PS[:, 4 * z + 3, 0:T], bones[:, :], b.SQ, start=True, stop=True).then_inc(r["bonus_sum_done"], 1)
            for z, b in both:
                pe.wait_ge(r["operands_ready"], at(i, z))
                for m, src in enumerate([b.BI, b.KI]):
                    for t in range(TT):
                        o = (2 * m + t) * P
                        ins = nc.tensor.transpose(PS[:, 4 * z + 1, o:o + P], src[:, t * P:(t + 1) * P], ident[:, :])
                ins.then_inc(r["turned"], 1)

            def grams(z, src, bank, sem_):
                for h in range(2):
                    q = slice(HD * h, HD * h + HD)
                    for t in range(TT):
                        ins = mm(PS[:, bank + h, t * 2 * P:(t + 1) * 2 * P], src[q, t * P:(t + 1) * P],
                                 pairs[z].KR[q, t, :, :].rearrange("p m t -> p (m t)"), start=True, stop=True)
                ins.then_inc(sem_, 1)

            for z, b in both:
                pe.wait_ge(r["mean_square_ready"], at(i, z))
                pe.wait_ge(r["turned_copied"], at(i, z))
                grams(z, b.BI, 4 * z, r["gram_b_done"])
            for z, b in both:
                pe.wait_ge(r["values_copied"], at(i, z))
                pe.wait_ge(r["bonus_copied"], at(i, z))
                grams(z, b.KI, 4 * z + 2, r["gram_k_done"])
            for z, b in both:
                pe.wait_ge(r["inverse0_ready"], at(i, z))
                for m in range(4):
                    ins = nc.tensor.transpose(PS[:, 4 * z + 1, m * P:(m + 1) * P], b.DT[:, m, :], ident[:, :])
                ins.then_inc(r["inverse0_turned"], 1)
            for lv in range(LEVELS):
                for z, b in both:
                    pe.wait_ge(r["level_ready"], at(i, z, LEVELS, lv))
                    pe.wait_ge(r["inverse_ready"], at(i, z, LEVELS + 1, lv))
                    for m in range(4):
                        ins = mm(PS[:, 4 * z, m * P:(m + 1) * P], b.LVL[:, lv % 2, m, :], b.DG[:, m, :], start=True, stop=True)
                    ins.then_inc(r["product_done"], 1)
                for z, b in both:
                    if lv == 0:
                        pe.wait_ge(r["gram_k_ready"], at(i, z))
                    pe.wait_ge(r["product_ready"], at(i, z, LEVELS, lv))
                    for m in range(4):
                        if lv < LEVELS - 1:
                            mm(PS[:, 4 * z + 1, m * P:(m + 1) * P], b.DT[:, m, :], b.XI[:, m, :], start=True, stop=True)
                    for m in range(4):
                        ins = mm(PS[:, 4 * z + 2, m * P:(m + 1) * P], b.XI[:, m, :], b.DT[:, m, :], start=True, stop=True)
                    ins.then_inc(r["inverse_done"], 1)
            for c in range(NCH):
                t, p0 = c // 2, CH * (c % 2)
                rows = slice(p0, p0 + CH)
                for z, b in both:
                    if c == 0:
                        pe.wait_ge(r["product_ready"], at(i, z, LEVELS, LEVELS - 1))
                    else:
                        pe.wait_ge(r["rhs_ready"], at(i, z, NCH, c - 1))
                    for h in range(2):
                        hc = slice(h * HD, h * HD + HD)
                        ins = mm(PS[rows, 4 * z, hc], b.NQ[:, h, t, 0, rows], b.VP[:, t, hc], start=(h == 0),
                                 stop=(c == 0), skip_group_check=True)
                    if c:
                        pe.wait_ge(r["state_ready"], at(i, z, NCH - 1, c - 1))
                        ins = mm(PS[rows, 4 * z, 0:P], b.KR[:, t, 0, rows], b.SS[:, c, :], start=False, stop=True,
                                 skip_group_check=True)
                    ins.then_inc(r["rhs_done"], 1)
                for z, b in both:
                    if c == 0:
                        pe.wait_ge(r["inverse_ready"], at(i, z, LEVELS + 1, LEVELS))
                    pe.wait_ge(r["rhs_ready"], at(i, z, NCH, c))
                    if c:
                        pe.wait_ge(r["solution_ready"], at(i, z, NCH, c - 1))
                    for h in range(2):
                        hc = slice(h * HD, h * HD + HD)
                        ins = mm(PS[:, 4 * z + 1, hc], b.DT[rows, 2 * h + t, :], b.R1[rows, t, hc], start=True, stop=True)
                    ins.then_inc(r["solution_done"], 1)
                for z, b in both:
                    pe.wait_ge(r["solution_ready"], at(i, z, NCH, c))
                    if c < NCH - 1:
                        mm(PS[:, 4 * z + 2, 0:P], b.BKT[rows, 0, t, :], b.UU[rows, t, :], start=True, stop=False)
                        mm(PS[:, 4 * z + 2, 0:P], b.BKT[rows, 1, t, :], b.VP[rows, t, :], start=False,
                           stop=True).then_inc(r["increment_done"], 1)
            for z, b in both:
                for t in range(TT):
                    for c in range(2):
                        mm(PS[:, 4 * z + 3, t * P + c * CH:t * P + (c + 1) * CH], b.SS[:, 2 * t + c, :],
                           b.KR[:, t, 1, c * CH:(c + 1) * CH], start=(c == 0), stop=False, skip_group_check=True)
                    for h in range(2):
                        hc = slice(h * HD, h * HD + HD)
                        mm(PS[hc, 4 * z + 3, t * P:(t + 1) * P], b.VP[:, t, hc], b.NQ[:, h, t, 1, :],
                           start=False, stop=False, skip_group_check=True)
                        ins = mm(PS[hc, 4 * z + 3, t * P:(t + 1) * P], b.UU[:, t, hc], b.MP[:, h, t, 1, :],
                                 start=False, stop=True, skip_group_check=True)
                ins.then_inc(r["y_done"], 1)
            for z, b in both:
                pe.wait_ge(r["y_ready"], at(i, z))
                mm(PS[:, 4 * z, 0:T], bones[:, :], b.YY, start=True, stop=True).then_inc(r["mean_done"], 1)
            for z, b in both:
                pe.wait_ge(r["centred_ready"], at(i, z))
                mm(PS[:, 4 * z + 1, 0:T], bones[:, :], b.YQ, start=True, stop=True).then_inc(r["variance_done"], 1)

        once = ["logits_done", "scores_ready", "mask_ready", "rank_done", "rank_ready", "count_ready",
                "shared_gate_up", "shared_silu", "shared_hidden"]
        by_pair = ["onehot_ready", "gathered0", "gathered1", "gathered0_copied", "gathered1_copied", "gate_up_done",
                   "silu_ready", "hidden_ready", "turned", "hidden_copied", "gates_copied", "down0", "down1",
                   "down0_copied", "down1_copied", "scattered"]
        per_layer = {n: 1 for n in once} | {n: PAIRS for n in by_pair} | {"shared_loaded": 48, "x_part": 3, "x_rest": 2}
        moe_shared = {n: sem("moe_" + n) for n in per_layer} | {
            "gu_w": [sem(f"gate_up_loaded{s}") for s in range(4)],
            "dn_w": [sem(f"down_loaded{s}") for s in range(4)]}
        per_layer |= {"gu_w": 32 * PAIRS // 2, "dn_w": 16 * PAIRS // 2}
        over_names = ["over_pe", "over_dve", "over_act", "over_loaded", "over_free", "over_link", "over_list"]

        def moe_view(l):
            q = moe_shared | {n: sem(f"l{l}_{n}") for n in over_names}
            past = {n: l * count for n, count in per_layer.items()}
            st = 2 * l + 1
            wg, wu, wd = a["moe_w_gate"][l], a["moe_w_up"][l], a["moe_w_down"][l]
            gate_src = lambda w, e: w[ds(e, 1), :, :].rearrange("o (p k) f -> p (o k) f", k=KT)
            down_src = lambda w, e: w[ds(e, 1), :, :].rearrange("o (k p) d -> p (o k) d", p=P)

            def gate_and_up(slot):
                w = RING[:, slot + 1, :] if slot < 2 else odd[:, slot - 2, :]
                return w[:, 0:4096].rearrange("p (m k f) -> p k m f", m=2, k=KT)

            def load_gate_up(sp, e, slot):
                g, u, d = wslot(slot)
                sp.dma_start(g, gate_src(wg, e)).then_inc(q["gu_w"][slot], 16)
                sp.dma_start(u, gate_src(wu, e)).then_inc(q["gu_w"][slot], 16)

            def load_down(sp, e, slot):
                sp.dma_start(wslot(slot)[2], down_src(wd, e)).then_inc(q["dn_w"][slot], 16)

            def load_expert(sp, e, slot):
                load_gate_up(sp, e, slot)
                load_down(sp, e, slot)

            def prefetch(sp):
                if l:
                    sp.wait_ge(s_res, 2)
                g, u, d = wslot(-1)
                sp.dma_start(g, a["moe_ws_gate"][l].rearrange("(p k) f -> p k f", k=KT)).then_inc(q["shared_loaded"], 16)
                sp.dma_start(u, a["moe_ws_up"][l].rearrange("(p k) f -> p k f", k=KT)).then_inc(q["shared_loaded"], 16)
                sp.dma_start(d, a["moe_ws_down"][l].rearrange("(k p) d -> p k d", p=P)).then_inc(q["shared_loaded"], 16)
                if l == 0:
                    load_expert(sp, 0, 0)

            def loads(sp):
                sp.wait_ge(s_ln, TT * st)
                for e in range(1 - l, 4):
                    load_expert(sp, e, e)
                load_ln(sp, st)
                with sp.Fori(1, PAIRS // 2) as i:
                    for half in range(2):
                        sp.wait_ge(q["gate_up_done"], 2 * i + (half - 1) + past["gate_up_done"])
                        for s in range(2):
                            load_gate_up(sp, 4 * i + 2 * half + s, 2 * half + s)
                        sp.wait_ge(q["down1"], 2 * i + (half - 1) + past["down1"])
                        for s in range(2):
                            load_down(sp, 4 * i + 2 * half + s, 2 * half + s)
                sp.wait_ge(q["count_ready"], 1 + past["count_ready"])
                most = nc.sync.value_load(cnti[0:1, 2 * l:2 * l + 1], min_val=0, max_val=T)
                with sp.If(most > B):
                    sp.wait_ge(q["over_list"], 1)
                    rounds = nc.sync.value_load(cnti[0:1, 2 * l + 1:2 * l + 2], min_val=1, max_val=NOV // 2)
                    with sp.Fori(0, rounds) as i:
                        sp.wait_ge(q["over_free"], i + 1)
                        for s in range(2):
                            e = nc.sync.value_load(elist[0:1, ds(2 * i + s, 1)], min_val=0, max_val=E - 1)
                            g, u, d = wslot(s)
                            sp.dma_start(g, gate_src(wg, e)).then_inc(q["over_loaded"], 16)
                            sp.dma_start(u, gate_src(wu, e)).then_inc(q["over_loaded"], 16)
                            sp.dma_start(d, down_src(wd, e)).then_inc(q["over_loaded"], 16)

            def gather(pe, half, sel):
                for k in range(4):
                    for t in range(TT):
                        for n in range(3):
                            ins = nc.tensor.matmul(PS[:, 6 + half, k * 2 * B:(k + 1) * 2 * B],
                                                   XB[:, n, t, 4 * half + k::KT], sel[:, t, :, :].rearrange("p s b -> p (s b)"),
                                                   start=(t == 0 and n == 0), stop=(t == TT - 1 and n == 2))
                return ins

            def gate_up(pe, slots):
                for k in range(KT):
                    for s in range(2):
                        ins = nc.tensor.matmul(PS[s * B:(s + 1) * B, 4, :], XG[:, k, s * B:(s + 1) * B],
                                               gate_and_up(slots[s])[:, k, :, :], start=(k == 0), stop=(k == KT - 1))
                return ins

            def turn(pe, buf):
                for f in range(FT):
                    nc.tensor.transpose(PS[:, 4, f * 2 * B:(f + 1) * 2 * B], HH[0:2 * B, f * P:(f + 1) * P],
                                        ident[0:2 * B, 0:2 * B])
                for t in range(TT):
                    ins = nc.tensor.transpose(PS[0:2 * B, 4, T + t * P:T + (t + 1) * P],
                                              SELG[:, buf, t, :, :].rearrange("p s b -> p (s b)"), ident[:, :])
                return ins

            def down(pe, slots, h, bank):
                for f in range(FT):
                    for s in range(2):
                        ins = nc.tensor.matmul(PS[s * B:(s + 1) * B, bank, :], HT[:, f, s * B:(s + 1) * B],
                                               wslot(slots[s])[2][:, f, h * 512:(h + 1) * 512],
                                               start=(f == 0), stop=(f == FT - 1))
                return ins

            def scatter(pe):
                for t in range(TT):
                    for h in range(2):
                        ins = nc.tensor.matmul(PS[:, 2 * t + h, :], GT[0:2 * B, t, :],
                                               Y[0:2 * B, h * 512:(h + 1) * 512], start=False, stop=True,
                                               skip_group_check=True)
                return ins

            def pe_pair(pe, i, half, first, last, use):
                slots = (2 * half, 2 * half + 1)
                for n in range(2):
                    pe.wait_ge(q[f"gathered{n}_copied"], i + 1 + past[f"gathered{n}_copied"])
                for s in slots:
                    pe.wait_ge(q["gu_w"][s], 32 * use + 32 + past["gu_w"])
                if not first:
                    pe.wait_ge(q["hidden_copied"], i + past["hidden_copied"])
                    pe.wait_ge(q["gates_copied"], i + past["gates_copied"])
                gate_up(pe, slots).then_inc(q["gate_up_done"], 1)
                if not first:
                    pe.wait_ge(q["down0_copied"], i + past["down0_copied"])
                    pe.wait_ge(q["down1_copied"], i + past["down1_copied"])
                    scatter(pe).then_inc(q["scattered"], 1)
                pe.wait_ge(q["hidden_ready"], i + 1 + past["hidden_ready"])
                turn(pe, half).then_inc(q["turned"], 1)
                if not last:
                    pe.wait_ge(q["onehot_ready"], i + 2 + past["onehot_ready"])
                    gather(pe, 0, SEL1[:, 1 - half]).then_inc(q["gathered0"], 1)
                for s in slots:
                    pe.wait_ge(q["dn_w"][s], 16 * use + 16 + past["dn_w"])
                pe.wait_ge(q["hidden_copied"], i + 1 + past["hidden_copied"])
                down(pe, slots, 0, 5).then_inc(q["down0"], 1)
                if not last:
                    gather(pe, 1, SEL1[:, 1 - half]).then_inc(q["gathered1"], 1)
                pe.wait_ge(q["down0_copied"], i + 1 + past["down0_copied"])
                down(pe, slots, 1, 5).then_inc(q["down1"], 1)

            def pe_moe(pe):
                pe_transpose(pe, st)
                pe.wait_ge(s_xT, 4 * (st + 1))
                pe.wait_ge(s_vec, 16 * 10)
                for t in range(TT):
                    for k in range(KT):
                        ins = nc.tensor.matmul(PS[:, 4, t * E:(t + 1) * E], xT[:, k, t * P:(t + 1) * P], WR[:, l, k, :],
                                               start=(k == 0), stop=(k == KT - 1))
                ins.then_inc(q["logits_done"], 1)
                pe.wait_ge(q["shared_loaded"], 48 + past["shared_loaded"])
                g, u, d = wslot(-1)
                for m, w in enumerate((g, u)):
                    for f in range(FT):
                        for k in range(KT):
                            ins = nc.tensor.matmul(PS[:, 5 + m, f * T:(f + 1) * T], w[:, k, f * P:(f + 1) * P], xT[:, k, :],
                                                   start=(k == 0), stop=(k == KT - 1))
                ins.then_inc(q["shared_gate_up"], 1)
                pe.wait_ge(q["mask_ready"], 1 + past["mask_ready"])
                nc.tensor.matmul(PS[:, 4, 0:E], before[:, :], MSK[:, 0, :], start=True, stop=True)
                nc.tensor.matmul(PS[:, 4, E:2 * E], ones[:, :], MSK[:, 0, :], start=True, stop=False)
                nc.tensor.matmul(PS[:, 4, E:2 * E], before[:, :], MSK[:, 1, :], start=False, stop=True)
                nc.tensor.matmul(PS[:, 4, 2 * E:3 * E], ones[:, :], MSK[:, 0, :], start=True, stop=False)
                nc.tensor.matmul(PS[:, 4, 2 * E:3 * E], ones[:, :], MSK[:, 1, :], start=False,
                                 stop=True).then_inc(q["rank_done"], 1)
                pe.wait_ge(q["shared_hidden"], 1 + past["shared_hidden"])
                for t in range(TT):
                    for h in range(2):
                        for f in range(FT):
                            ins = nc.tensor.matmul(PS[:, 2 * t + h, :], HS[:, f, t * P:(t + 1) * P],
                                                   d[:, f, h * 512:(h + 1) * 512], start=(f == 0), stop=(f == FT - 1))
                pe.wait_ge(q["onehot_ready"], 1 + past["onehot_ready"])
                pe.wait_ge(q["x_part"], 3 + past["x_part"])
                gather(pe, 0, SEL1[:, 0]).then_inc(q["gathered0"], 1)
                gather(pe, 1, SEL1[:, 0]).then_inc(q["gathered1"], 1)
                pe.wait_ge(q["rank_ready"], 1 + past["rank_ready"])
                pe_pair(pe, 0, 0, True, False, 0)
                pe_pair(pe, 1, 1, False, False, 0)
                with pe.Fori(1, PAIRS // 2 - 1) as i:
                    pe_pair(pe, 2 * i, 0, False, False, i)
                    pe_pair(pe, 2 * i + 1, 1, False, False, i)
                pe_pair(pe, PAIRS - 2, 0, False, False, PAIRS // 2 - 1)
                pe_pair(pe, PAIRS - 1, 1, False, True, PAIRS // 2 - 1)
                for h in range(2):
                    pe.wait_ge(q[f"down{h}_copied"], PAIRS + past[f"down{h}_copied"])
                pe.wait_ge(q["gates_copied"], PAIRS + past["gates_copied"])
                scatter(pe).then_inc(q["scattered"], 1)
                pe.wait_ge(q["count_ready"], 1 + past["count_ready"])
                most = nc.tensor.value_load(cnti[0:1, 2 * l:2 * l + 1], min_val=0, max_val=T)
                with pe.If(most > B):
                    pe_over(pe)
                pe.wait_ge(q["scattered"], PAIRS + past["scattered"])
                pe.sem_inc(s_res, 1)

            def pe_over(pe):
                pe.wait_ge(q["over_dve"], 1)
                nc.tensor.matmul(PS[0:E, 4, 0:NR], before[0:E, 0:E], F1[0:E, 0, :], start=True, stop=False)
                nc.tensor.matmul(PS[0:E, 4, 0:NR], ones[0:E, 0:E], F1[0:E, 1, :], start=False,
                                 stop=True).then_inc(q["over_pe"], 1)
                pe.wait_ge(q["over_dve"], 2)
                nc.tensor.matmul(PS[0:1, 5, 0:NOV], ecol[0:E, :], OS[0:E, 0, :], start=True, stop=True)
                nc.tensor.matmul(PS[0:1, 5, NOV:2 * NOV], ones[0:E, 0:1], OS[0:E, 0, :], start=True, stop=True)
                for t in range(TT):
                    nc.tensor.transpose(PS[0:E, 6, t * P:(t + 1) * P], RKX[:, t, 0:E], ident[:, :])
                    ins = nc.tensor.transpose(PS[0:E, 6, (2 + t) * P:(3 + t) * P], GX[:, t, 0:E], ident[:, :])
                ins.then_inc(q["over_pe"], 1)
                pe.wait_ge(q["over_dve"], 3)
                for t in range(TT):
                    o = t * NOV
                    nc.tensor.matmul(PS[:, 7, o:o + NOV], TR4[0:E, t, :], OS[0:E, 0, :], start=True, stop=False)
                    nc.tensor.matmul(PS[:, 7, o:o + NOV], ones[0:E, :], OS[0:E, 1, :], start=False, stop=True)
                    ins = nc.tensor.matmul(PS[:, 7, (2 + t) * NOV:(3 + t) * NOV], TR4[0:E, 2 + t, :], OS[0:E, 0, :],
                                           start=True, stop=True)
                ins.then_inc(q["over_pe"], 1)
                pe.wait_ge(q["over_list"], 1)
                rounds = nc.tensor.value_load(cnti[0:1, 2 * l + 1:2 * l + 2], min_val=1, max_val=NOV // 2)
                pe.sem_inc(q["over_free"], 1)
                with pe.Fori(0, rounds) as i:
                    pe.wait_ge(q["over_dve"], 5 * i + 5)
                    gather(pe, 0, SEL1[:, 0])
                    gather(pe, 1, SEL1[:, 0]).then_inc(q["over_pe"], 1)
                    pe.wait_ge(q["over_dve"], 5 * i + 6)
                    pe.wait_ge(q["over_loaded"], 96 * i + 96)
                    gate_up(pe, (0, 1)).then_inc(q["over_pe"], 1)
                    pe.wait_ge(q["over_dve"], 5 * i + 7)
                    turn(pe, 0).then_inc(q["over_pe"], 1)
                    pe.wait_ge(q["over_dve"], 5 * i + 8)
                    for h in range(2):
                        ins = down(pe, (0, 1), h, 5 + h)
                    ins.then_inc(q["over_pe"], 1)
                    pe.wait_ge(q["over_dve"], 5 * i + 9)
                    scatter(pe).then_inc(q["over_pe"], 1)
                    pe.wait_ge(q["over_pe"], 5 * i + 8)
                    pe.sem_inc(q["over_free"], 1)

            def silu(sem_):
                nc.scalar.activation(SIL[0:2 * B, :], PS[0:2 * B, 4, 0:FF], ACT.Silu).then_inc(sem_, 1)

            def copy_gathered(eng_copy, half):
                return eng_copy(XG[:, 4 * half:4 * half + 4, :].rearrange("p k b -> p (k b)"), PS[:, 6 + half, 0:8 * B])

            def act_pair(s, i, half, last):
                s.wait_ge(q["gate_up_done"], i + 1 + past["gate_up_done"])
                silu(q["silu_ready"])
                s.wait_ge(q["hidden_copied"], i + 1 + past["hidden_copied"])
                nc.scalar.copy(GT[0:2 * B, :, :].rearrange("p t b -> p (t b)"),
                               PS[0:2 * B, 4, T:2 * T]).then_inc(q["gates_copied"], 1)
                s.wait_ge(q["down0"], i + 1 + past["down0"])
                nc.scalar.copy(Y[0:2 * B, 0:512], PS[0:2 * B, 5, :]).then_inc(q["down0_copied"], 1)
                if not last:
                    s.wait_ge(q["gathered1"], i + 2 + past["gathered1"])
                    copy_gathered(nc.scalar.copy, 1).then_inc(q["gathered1_copied"], 1)

            def act_moe(s):
                s.wait_ge(s_ln, TT * st)
                part = lambda n: XB[:, n, :, :].rearrange("p t d -> p (t d)")
                nc.scalar.copy(part(0), X[:, :, :].rearrange("p t d -> p (t d)")).then_inc(q["x_part"], 1)
                act_transpose_copy(s, st)
                s.wait_ge(q["logits_done"], 1 + past["logits_done"])
                nc.scalar.activation(SCO[:, :, :].rearrange("p t e -> p (t e)"), PS[:, 4, 0:TT * E],
                                     ACT.Sigmoid).then_inc(q["scores_ready"], 1)
                for n in range(2):
                    s.wait_ge(q["x_rest"], n + 1 + past["x_rest"])
                    nc.scalar.copy(part(n + 1), XR).then_inc(q["x_part"], 1)
                s.wait_ge(q["shared_gate_up"], 1 + past["shared_gate_up"])
                nc.scalar.activation(HSs[:, :, :].rearrange("p f t -> p (f t)"), PS[:, 5, :],
                                     ACT.Silu).then_inc(q["shared_silu"], 1)
                s.wait_ge(q["gathered1"], 1 + past["gathered1"])
                copy_gathered(nc.scalar.copy, 1).then_inc(q["gathered1_copied"], 1)
                act_pair(s, 0, 0, False)
                act_pair(s, 1, 1, False)
                with s.Fori(1, PAIRS // 2 - 1) as i:
                    act_pair(s, 2 * i, 0, False)
                    act_pair(s, 2 * i + 1, 1, False)
                act_pair(s, PAIRS - 2, 0, False)
                act_pair(s, PAIRS - 1, 1, True)
                s.wait_ge(q["count_ready"], 1 + past["count_ready"])
                most = nc.scalar.value_load(cnti[0:1, 2 * l:2 * l + 1], min_val=0, max_val=T)
                with s.If(most > B):
                    s.wait_ge(q["over_list"], 1)
                    rounds = nc.scalar.value_load(cnti[0:1, 2 * l + 1:2 * l + 2], min_val=1, max_val=NOV // 2)
                    with s.Fori(0, rounds) as i:
                        s.wait_ge(q["over_pe"], 5 * i + 5)
                        silu(q["over_act"])

            def onehot(v, link, i, buf, sem_, width=E):
                spread = lambda m: m[:, :, ds(2 * i, 2)].rearrange("p t (s o) -> p t s o", o=1).to_broadcast([P, TT, 2, B])
                io = iotab[:, :].rearrange("p (t s b) -> p t s b", t=1, s=1).to_broadcast([P, TT, 2, B])
                link(nc.vector.tensor_tensor(SEL1[:, buf], spread(RKX), io, ALU.is_equal))
                link.sync()
                nc.vector.tensor_tensor(SELG[:, buf], SEL1[:, buf], spread(GX), ALU.mult).then_inc(sem_, 1)

            def hidden(sem_):
                nc.vector.tensor_tensor(HH[0:2 * B, :], SIL[0:2 * B, :], PS[0:2 * B, 4, FF:2 * FF],
                                        ALU.mult).then_inc(sem_, 1)

            def copy_hidden():
                return nc.vector.tensor_copy(HT[:, :, :].rearrange("p f b -> p (f b)"), PS[:, 4, 0:FT * 2 * B])

            def dve_pair(v, link, i, half, more, last):
                v.wait_ge(q["silu_ready"], i + 1 + past["silu_ready"])
                hidden(q["hidden_ready"])
                v.wait_ge(q["turned"], i + 1 + past["turned"])
                copy_hidden().then_inc(q["hidden_copied"], 1)
                if not last:
                    v.wait_ge(q["gathered0"], i + 2 + past["gathered0"])
                    copy_gathered(nc.vector.tensor_copy, 0).then_inc(q["gathered0_copied"], 1)
                if more:
                    onehot(v, link, i + 2, half, q["onehot_ready"])
                v.wait_ge(q["down1"], i + 1 + past["down1"])
                nc.vector.tensor_copy(Y[0:2 * B, 512:1024], PS[0:2 * B, 5, :]).then_inc(q["down1_copied"], 1)

            def dve_route(v, link):
                pair = lambda m: m[:, :, :].rearrange("p t e -> p (t e)")
                byg = lambda m: m[:, :, :].rearrange("p t (g e) -> p (t g) e", e=GE)
                v.wait_ge(q["scores_ready"], 1 + past["scores_ready"])
                link(nc.vector.tensor_tensor(BIA[:, :, :], SCO[:, :, :], EB[:, l:l + 1, :].to_broadcast([P, TT, E]),
                                             ALU.add))
                link.sync()
                for n in range(TT * NG):
                    link(nc.vector.max(top2[:, n, :], byg(BIA)[:, n, :]))
                link.sync()
                tg = grp[:, :, :].rearrange("p t g -> p (t g)")
                link(nc.vector.tensor_tensor(tg, top2[:, :, 0], top2[:, :, 1], ALU.add))
                link.sync()
                mine = grp[:, :, :].rearrange("p t (g o) -> p t g o", o=1).to_broadcast([P, TT, NG, NG])
                other = grp[:, :, :].rearrange("p t (o g) -> p t o g", o=1).to_broadcast([P, TT, NG, NG])
                tri = tri8[:, :, :].rearrange("p (o g) h -> p o g h", o=1).to_broadcast([P, TT, NG, NG])
                link(nc.vector.tensor_tensor(cmpa[:, :, :, :], other, mine, ALU.is_gt))
                link(nc.vector.tensor_tensor(cmpb[:, :, :, :], other, mine, ALU.is_equal))
                link.sync()
                link(nc.vector.tensor_tensor(cmpb[:, :, :, :], cmpb[:, :, :, :], tri, ALU.mult))
                link.sync()
                link(nc.vector.tensor_tensor(cmpa[:, :, :, :], cmpa[:, :, :, :], cmpb[:, :, :, :], ALU.add))
                link.sync()
                link(nc.vector.tensor_reduce(gcnt[:, :, :], cmpa[:, :, :, :], AX, ALU.add))
                link.sync()
                link(nc.vector.tensor_scalar(gcnt[:, :, :], gcnt[:, :, :], TOPG - 0.5, None, ALU.is_lt))
                link.sync()
                link(nc.vector.tensor_scalar(gpen[:, :, :], gcnt[:, :, :], BIG, -BIG, ALU.mult, ALU.add))
                wide = lambda m: m[:, :, :].rearrange("p t (g o) -> p (t g) o", o=1).to_broadcast([P, TT * NG, GE])
                link(nc.vector.tensor_tensor(byg(BIA), byg(BIA), wide(gcnt), ALU.mult))
                link.sync()
                link(nc.vector.tensor_tensor(byg(BIA), byg(BIA), wide(gpen), ALU.add))
                link.sync()
                for t in range(TT):
                    link(nc.vector.max(top8[:, t, :], BIA[:, t, :]))
                link.sync()
                for t in range(TT):
                    link(nc.vector.match_replace(REP[:, t, :], top8[:, t, :], BIA[:, t, :], -3.0 * BIG))
                link.sync()
                nc.vector.tensor_tensor(MSK[:, :, :], REP[:, :, :], BIA[:, :, :], ALU.not_equal).then_inc(q["mask_ready"], 1)
                v.wait_ge(q["mask_ready"], 1 + past["mask_ready"])
                link(nc.vector.tensor_tensor(SEL[:, :, :], SCO[:, :, :], MSK[:, :, :], ALU.mult))
                link.sync()
                link(nc.vector.tensor_reduce(gsum[:, :], SEL[:, :, :], AX, ALU.add))
                link.sync()
                link(nc.vector.reciprocal(gsum[:, :], gsum[:, :]))
                link.sync()
                for t in range(TT):
                    link(nc.vector.tensor_scalar(GX[:, t, 0:E], SEL[:, t, :], gsum[:, t:t + 1], 2.5, ALU.mult, ALU.mult))
                v.wait_ge(q["rank_done"], 1 + past["rank_done"])
                link(nc.vector.scalar_tensor_tensor(out=RKX[:, :, 0:E],
                                                    in0=PS[:, 4, 0:TT * E].rearrange("p (t e) -> p t e", t=TT), scalar=1.0,
                                                    in1=MSK[:, :, :], op0=ALU.add, op1=ALU.mult))
                link(nc.vector.tensor_reduce(cntf[0:1, 0:1], PS[0:1, 4, 2 * E:3 * E], AX, ALU.max))
                link(nc.vector.tensor_copy(CNT[:, :], PS[:, 4, 2 * E:3 * E]))
                link.sync()
                link(nc.vector.tensor_scalar(RKX[:, :, 0:E], RKX[:, :, 0:E], -1.0, None, ALU.add))
                link(nc.vector.tensor_copy(cnti[0:1, 2 * l:2 * l + 1], cntf[0:1, 0:1]))
                link.sync()
                v.sem_inc(q["rank_ready"], 1)
                v.sem_inc(q["count_ready"], 1)
                onehot(v, link, 0, 0, q["onehot_ready"])
                onehot(v, link, 1, 1, q["onehot_ready"])

            def dve_moe(v, link):
                dve_transpose_copy(v, st)
                dve_route(v, link)
                v.wait_ge(q["shared_silu"], 1 + past["shared_silu"])
                nc.vector.tensor_tensor(HS[:, :, :].rearrange("p f t -> p (f t)"),
                                        HSs[:, :, :].rearrange("p f t -> p (f t)"), PS[:, 6, :],
                                        ALU.mult).then_inc(q["shared_hidden"], 1)
                v.wait_ge(q["gathered0"], 1 + past["gathered0"])
                copy_gathered(nc.vector.tensor_copy, 0).then_inc(q["gathered0_copied"], 1)
                dve_pair(v, link, 0, 0, True, False)
                dve_pair(v, link, 1, 1, True, False)
                with v.Fori(1, PAIRS // 2 - 1) as i:
                    link.enter(i, 1, 2)
                    dve_pair(v, link, 2 * i, 0, True, False)
                    dve_pair(v, link, 2 * i + 1, 1, True, False)
                link.leave(PAIRS // 2 - 2)
                dve_pair(v, link, PAIRS - 2, 0, False, False)
                dve_pair(v, link, PAIRS - 1, 1, False, True)
                most = nc.vector.value_load(cnti[0:1, 2 * l:2 * l + 1], min_val=0, max_val=T)
                with v.If(most > B):
                    dve_over(v, Link(v, q["over_link"]))

            def dve_over(v, link):
                v.wait_ge(q["scattered"], PAIRS + past["scattered"])
                link(nc.vector.tensor_tensor(F2[0:E, :], ident[0:E, 0:E], CNT[0:E, :], ALU.mult))
                link.sync()
                link(nc.vector.tensor_reduce(cntf[0:E, 1:2], F2[0:E, :], AX, ALU.add))
                link.sync()
                link(nc.vector.tensor_scalar(F1[0:E, 0, :], thr[0:E, :], cntf[0:E, 1:2], None, ALU.is_lt))
                link(nc.vector.memset(F1[0:E, 1, 0:1], 0.0))
                link.sync()
                for r in range(1, NR):
                    link(nc.vector.tensor_tensor(F1[0:E, 1, r:r + 1], F1[0:E, 1, r - 1:r], F1[0:E, 0, r - 1:r], ALU.add))
                    link.sync()
                v.sem_inc(q["over_dve"], 1)
                v.wait_ge(q["over_pe"], 1)
                link(nc.vector.tensor_copy(F1[0:E, 2, :], PS[0:E, 4, 0:NR]))
                link.sync()
                wide = lambda m: m.rearrange("p (r o) -> p r o", o=1).to_broadcast([E, NR, NOV])
                link(nc.vector.tensor_tensor(OH[0:E, :, :],
                                             iotap[0:E, :].rearrange("p (o n) -> p o n", o=1).to_broadcast([E, NR, NOV]),
                                             wide(F1[0:E, 2, :]), ALU.is_equal))
                link.sync()
                link(nc.vector.tensor_tensor(OH[0:E, :, :], OH[0:E, :, :], wide(F1[0:E, 0, :]), ALU.mult))
                link.sync()
                link(nc.vector.tensor_reduce(OS[0:E, 0, :], OH[0:E, :, :].rearrange("p r n -> p n r"), AX, ALU.add))
                link.sync()
                link(nc.vector.tensor_tensor(OH[0:E, :, :], OH[0:E, :, :], wide(rbase[0:E, :]), ALU.mult))
                link.sync()
                link(nc.vector.tensor_reduce(OS[0:E, 1, :], OH[0:E, :, :].rearrange("p r n -> p n r"), AX, ALU.add))
                link.sync()
                v.sem_inc(q["over_dve"], 1)
                v.wait_ge(q["over_pe"], 2)
                link(nc.vector.tensor_copy(elist[0:1, :], PS[0:1, 5, 0:NOV]))
                link(nc.vector.tensor_reduce(cntf[0:1, 0:1], PS[0:1, 5, NOV:2 * NOV:2], AX, ALU.add))
                link(nc.vector.tensor_copy(TR4[0:E, :, :].rearrange("p m t -> p (m t)"), PS[0:E, 6, :]))
                link.sync()
                link(nc.vector.tensor_copy(cnti[0:1, 2 * l + 1:2 * l + 2], cntf[0:1, 0:1]))
                link.sync()
                v.sem_inc(q["over_dve"], 1)
                v.wait_ge(q["over_pe"], 3)
                link(nc.vector.tensor_scalar(RKX[:, :, E:E + NOV],
                                             PS[:, 7, 0:2 * NOV].rearrange("p (t n) -> p t n", t=TT), -1.0, None, ALU.add))
                link(nc.vector.tensor_copy(GX[:, :, E:E + NOV],
                                           PS[:, 7, 2 * NOV:4 * NOV].rearrange("p (t n) -> p t n", t=TT)))
                link.sync()
                v.sem_inc(q["over_dve"], 1)
                v.sem_inc(q["over_list"], 1)
                rounds = nc.vector.value_load(cnti[0:1, 2 * l + 1:2 * l + 2], min_val=1, max_val=NOV // 2)
                with v.Fori(0, rounds) as i:
                    link.enter(i, 0, 4)
                    v.wait_ge(q["over_free"], i + 1)
                    onehot(v, link, i + PAIRS, 0, q["over_dve"])
                    v.wait_ge(q["over_pe"], 5 * i + 4)
                    link(copy_gathered(nc.vector.tensor_copy, 0))
                    copy_gathered(nc.vector.tensor_copy, 1).then_inc(q["over_dve"], 1)
                    v.wait_ge(q["over_act"], i + 1)
                    hidden(q["over_dve"])
                    v.wait_ge(q["over_pe"], 5 * i + 6)
                    link(copy_hidden())
                    nc.vector.tensor_copy(GT[0:2 * B, :, :].rearrange("p t b -> p (t b)"),
                                          PS[0:2 * B, 4, T:2 * T]).then_inc(q["over_dve"], 1)
                    v.wait_ge(q["over_pe"], 5 * i + 7)
                    link(nc.vector.tensor_copy(Y[0:2 * B, 0:512], PS[0:2 * B, 5, :]))
                    nc.vector.tensor_copy(Y[0:2 * B, 512:1024], PS[0:2 * B, 6, :]).then_inc(q["over_dve"], 1)
                link.leave(NOV // 2)

            def gp_moe(g):
                part = lambda n: XB[:, n, :, :].rearrange("p t d -> p (t d)")
                for n in range(2):
                    g.wait_ge(q["x_part"], n + 1 + past["x_part"])
                    src = X[:, :, :].rearrange("p t d -> p (t d)") if n == 0 else XR
                    if n:
                        g.wait_ge(q["x_rest"], 1 + past["x_rest"])
                    nc.gpsimd.tensor_tensor(XR, src, part(n), ALU.subtract).then_inc(q["x_rest"], 1)

            return dict(prefetch=prefetch, loads=loads, pe=pe_moe, gp=gp_moe, act=act_moe, dve=dve_moe)

        moe = [moe_view(l) for l in range(2)]
        out_t = a["out"][0].rearrange("(t p) d -> p t d", p=P)

        with nc.Block() as block:
            @block.sync
            def _(sp):
                sp_mix0(sp)
                if STOP > 1:
                    moe[0]["prefetch"](sp)
                    moe[0]["loads"](sp)
                if STOP > 2:
                    sp_mix1(sp)
                if STOP > 3:
                    moe[1]["prefetch"](sp)
                    moe[1]["loads"](sp)
                sp.wait_ge(s_ln, TT * STOP)
                sp.dma_start(out_t, X[:, :, :]).then_inc(s_out, 16)
                sp.wait_ge(s_out, 16)

            @block.gpsimd
            def _(g):
                constants(g)
                gp_mix0(g)
                if STOP > 1:
                    moe[0]["gp"](g)
                if STOP > 2:
                    gp_mix1(g)
                if STOP > 3:
                    moe[1]["gp"](g)

            @block.scalar
            def _(s):
                act_mix0(s)
                act_ln(s, 0)
                if STOP > 1:
                    moe[0]["act"](s)
                    act_ln(s, 1)
                if STOP > 2:
                    act_mix1(s)
                    act_ln(s, 2)
                if STOP > 3:
                    moe[1]["act"](s)
                    act_ln(s, 3)

            @block.vector
            def _(v):
                link = Link(v, s_dve)
                dve_mix0(v, link)
                layer_norm(v, link, 0)
                if STOP > 1:
                    moe[0]["dve"](v, link)
                    layer_norm(v, link, 1)
                if STOP > 2:
                    dve_mix1(v, link)
                    layer_norm(v, link, 2)
                if STOP > 3:
                    moe[1]["dve"](v, link)
                    layer_norm(v, link, 3)

            @block.tensor
            def _(pe):
                pe_mix0(pe)
                if STOP > 1:
                    moe[0]["pe"](pe)
                if STOP > 2:
                    pe_mix1(pe)
                if STOP > 3:
                    moe[1]["pe"](pe)


_INS = ["x", "ln_mix_g", "ln_mix_b", "ln_ffn_g", "ln_ffn_b", "ab_w_in", "ab_pool_w", "ab_pool_scale", "ab_w_out",
        "rw_mu", "rw_w_r", "rw_w_k", "rw_w_v", "rw_w_w1", "rw_w_w2", "rw_w0", "rw_a1", "rw_a2", "rw_a0",
        "rw_g1", "rw_g2", "rw_k_k", "rw_k_a", "rw_r_k", "rw_lnx_g", "rw_lnx_b", "rw_w_o",
        "moe_w_router", "moe_e_bias", "moe_w_gate", "moe_w_up", "moe_w_down",
        "moe_ws_gate", "moe_ws_up", "moe_ws_down"]


def kernel(**inputs):
    import numpy as _np
    import concourse.bacc as _bacc
    from concourse import mybir as _mybir
    from concourse.bass_utils import run_bass_kernel_spmd as _run

    nc = _bacc.Bacc("TRN2", target_bir_lowering=False, num_devices=1)
    arrays, args = {}, {}
    for name in _INS:
        v = _np.ascontiguousarray(inputs[name])
        arrays[f"in_{name}"] = v
        args[name] = nc.dram_tensor(f"in_{name}", v.shape, _mybir.dt.from_np(v.dtype), kind="ExternalInput").ap()
    args["out"] = nc.dram_tensor("out_x", (1, T, D), F32, kind="ExternalOutput").ap()
    program(nc, args)
    r = _run(nc, [arrays], core_ids=[0])
    return r.results[0]["out_x"]
```

```python
import math
from contextlib import ExitStack

import numpy as np

import concourse.bass as bass
from concourse import mybir

P = 128
D = 1024
T = 256
TT = T // P
KT = D // P
E = 64
FF = 256
FT = FF // P
NG = 8
GE = E // NG
TOPG = 4
B = 64
NR = T // B - 1
NOV = T * 8 // B
PAIRS = E // 2
H0 = 8
HD = 64
CH = 64
NCH = T // CH
ALPHA = 4.0 ** 0.25
LN_EPS = 1e-5
GN_EPS = 64e-5
CDEC = math.exp(-0.5)
BIG = 1.0e30
LEVELS = 5
CB = 256

F32 = mybir.dt.float32
I32 = mybir.dt.int32
BF16 = mybir.dt.bfloat16
ALU = mybir.AluOpType
ACT = mybir.ActivationFunctionType
AX = mybir.AxisListType.X
ds = bass.ds


class Link:

    def __init__(self, eng, sem):
        self.eng, self.sem, self.base, self.n = eng, sem, 0, 0

    def __call__(self, ins):
        ins.then_inc(self.sem, 1)
        self.n += 1

    def sync(self):
        self.eng.wait_ge(self.sem, self.base + self.n)

    def enter(self, i, first, per):
        self.start, self.per = self.base + self.n, per
        self.base, self.n = self.start + (i - first) * per, 0

    def leave(self, count):
        assert self.n == self.per, (self.n, self.per)
        self.base, self.n = self.start + count * self.per, 0


def program(nc, a):
    ctx = ExitStack()
    with ctx:
        def sb(name, shape, dt=F32):
            return ctx.enter_context(nc.sbuf_tensor(name, shape, dt))

        def sem(name):
            return ctx.enter_context(nc.semaphore(name))

        X = sb("X", [P, TT, D])
        xT = sb("xT", [P, KT, T])
        GB = sb("GB", [P, 2, D])
        RING = sb("RING", [P, 3, 6144])
        WR = sb("WR", [P, 2, KT, E])
        EB = sb("EB", [P, 2, E])
        ident = sb("ident", [P, P])
        ones = sb("ones", [P, P])
        before = sb("before", [P, P])
        bones = sb("bones", [P, P])
        iotab = sb("iotab", [P, B])
        tri8 = sb("tri8", [P, NG, NG])
        MK = sb("MK", [P, 2, P])
        LM = sb("LM", [P, 6, P])
        m01 = sb("m01", [P, T])
        MU = sb("MU", [P, 6, KT])
        VEC = sb("VEC", [P, 8, KT])
        V_W0, V_A0, V_KK, V_KA, V_RK, V_LG, V_LB, V_1KA = range(8)
        thr = sb("thr", [P, NR])
        rbase = sb("rbase", [P, NR])
        iotap = sb("iotap", [P, NOV])
        ecol = sb("ecol", [P, 1])
        ioi = sb("ioi", [P, T + 1], I32)
        elist = sb("elist", [1, NOV], I32)
        stat = sb("stat", [P, 2, 6])
        mv = sb("mv", [P, 4])
        cnti = sb("cnti", [1, 4], I32)
        AFL = 24960
        AR = sb("AR", [P, AFL])
        PS = ctx.enter_context(nc.psum_tensor("PS", [P, 8, 512], F32))

        class Area:
            def __init__(self, buf, at=0, end=None):
                self.buf, self.at, self.end = buf, at, end

            def __call__(self, *shape):
                n = int(np.prod(shape))
                v = self.buf[:, self.at:self.at + n]
                self.at += n
                assert self.at <= self.end, (self.at, self.end)
                if len(shape) == 1:
                    return v
                names = "abcd"[:len(shape)]
                return v.rearrange(f"p ({' '.join(names)}) -> p {' '.join(names)}",
                                   **{c: s for c, s in zip(names, shape)})

        flat = RING[:, :, :].rearrange("p s f -> p (s f)")
        am = Area(AR, 0, AFL)
        odd = am(2, 6144)

        def wslot(s):
            w = RING[:, s + 1, :] if s < 2 else odd[:, s - 2, :]
            return (w[:, 0:2048].rearrange("p (k f) -> p k f", k=KT),
                    w[:, 2048:4096].rearrange("p (k f) -> p k f", k=KT),
                    w[:, 4096:6144].rearrange("p (k f) -> p k f", k=FT))

        SCO = am(TT, E)
        BIA = am(TT, E)
        top2 = am(TT * NG, 8)
        grp = am(TT, NG)
        cmpa = am(TT, NG, NG)
        cmpb = am(TT, NG, NG)
        gcnt = am(TT, NG)
        gpen = am(TT, NG)
        MSK = am(TT, E)
        REP = am(TT, E)
        top8 = am(TT, 8)
        SEL = am(TT, E)
        gsum = am(TT)
        RKX = am(TT, E + NOV)
        GX = am(TT, E + NOV)
        HS = am(FT, T)
        HSs = am(FT, T)
        XB = am(3 * TT * D // 2).bitcast(BF16).rearrange("p (n t d) -> p n t d", n=3, t=TT)
        XR = am(TT * D)
        SEL1 = am(2 * TT * B).bitcast(BF16).rearrange("p (u t s b) -> p u t s b", u=2, t=TT, s=2)
        SELG = am(2, TT, 2, B)
        XG = am(KT, 2 * B)
        SIL = am(FF)
        HH = am(FF)
        HT = am(FT, 2 * B)
        GT = am(TT, P)
        Y = am(D)
        F1 = am(3, NR)
        OH = am(NR, NOV)
        OS = am(2, NOV)
        TR4 = am(4, P)
        F2 = am(E)
        CNT = am(E)
        cntf = am(2)
        ax = Area(AR, 0, AFL)
        WB = ax(2, 2048)
        mix0 = ax.at
        a0_ = Area(AR, mix0, AFL)
        CAT = a0_(KT, T)
        UQK = a0_(12, T)
        V0 = a0_(TT, 512)
        ZM = a0_(H0, T)
        assert a0_.at == 12288
        BET = a0_(H0, T)
        FFT = a0_(H0, T + 1)
        IPR = a0_(H0, T + 1)
        Z1 = a0_(H0, T + 1)
        WT = a0_(2 * H0, P)
        MQ = a0_(TT, T)
        a0b = Area(flat, 12288, 18432)
        PW = a0b(4, P)
        PSC = a0b(4)
        WS1 = a0b(4, T)
        WS2 = a0b(4, T)
        ICN = a0b(4, T)
        DIF = a0b(4, T)
        a1_ = Area(AR, mix0, AFL)
        KTT = a1_(KT, T)
        RT = a1_(KT, T)
        AT = a1_(KT, T)
        SG = a1_(KT, T)
        assert a1_.at == 12288
        V1 = a1_(TT, D)
        GTT = a1_(KT, T)
        XX = a1_(KT, T)
        YTK = XX.rearrange("p k t -> p (k t)").rearrange("p (t d) -> p t d", t=TT)
        BONT = a1_(TT, 16)
        STS = a1_(TT, 16, 6)
        MVS = a1_(TT, 16, 2)
        RS = a1_(TT, 16)
        NB = a1_(16)
        DCE = a1_(NCH, KT)
        l1x = a1_.at
        XM = a1_(2, KT, T)
        LH = a1_(4, T)
        g2b = a1_(D)
        a1s = Area(flat, 12288, 18432)
        w1 = a1s(KT, 64)
        a1w = a1s(KT, 64)
        g1 = a1s(KT, 160)
        w2 = a1s(D)
        a2 = a1s(D)
        g2a = a1s(D)
        SSQ = a1s(T)
        a1t = Area(flat, 6144, 12288)
        T1, T2, T3 = a1t(KT, T), a1t(KT, T), a1t(KT, T)
        gfl = GTT.rearrange("p k t -> p (k t)")
        OWN, WIN = gfl[:, 0:D], gfl[:, D:D + 2 * P]
        area_a = Area(AR, l1x, AFL)
        area_b = Area(flat, 6144, 18432)

        def take(*shape):
            n = int(np.prod(shape))
            return (area_a if area_a.at + n <= area_a.end else area_b)(*shape)

        LGB = take(2, D)
        class Pair:
            def __init__(self):
                self.XI, self.DG, self.DT = [take(4, P) for _ in range(3)]
                self.MP = take(2, TT, 2, P)
                self.NQ = take(2, TT, 2, P)
                self.KR = take(TT, 2, P)
                self.BIK = take(2, T)
                self.BKT = take(2, TT, P)
                self.SS = take(NCH, P)
                self.LVL = take(2, 4, P)
                self.VP = take(TT, P)
                self.R1 = take(TT, P)
                self.UU = take(TT, P)
                self.SD = take(P)
                self.DC = take(NCH)
                self.ST = take(TT, 2, 6)

        pairs = [Pair() for _ in range(2)]

        s_const = sem("constants_ready")
        s_g2d = sem("gpsimd_steps")
        s_dve = sem("vector_steps")
        s_vec = sem("vectors_loaded")
        s_x = sem("x_loaded")
        s_gb = sem("ln_params_loaded")
        s_ln = sem("ln_done")
        s_var = sem("ln_variance_ready")
        s_std = sem("ln_deviation_ready")
        s_tr = sem("x_transposed")
        s_xT = sem("xT_ready")
        s_wl = [sem(f"mixer_chunk_loaded{b}") for b in range(2)]
        s_wf = sem("mixer_chunk_used")
        s_pj = sem("projection_done")
        s_pe = sem("projection_copied")
        s_res = sem("residual_done")
        s_out = sem("out_stored")

        def dve_transpose_copy(v, st):
            for n in range(4):
                if n % 2 == 0:
                    v.wait_ge(s_tr, 4 * st + n + 1)
                    nc.vector.tensor_copy(xT[:, 4 * (n % 2):4 * (n % 2) + 4, P * (n // 2):P * (n // 2) + P],
                                          PS[:, 4 + n, :].rearrange("p (k t) -> p k t", k=4)).then_inc(s_xT, 1)

        def act_transpose_copy(s, st):
            for n in range(4):
                if n % 2 == 1:
                    s.wait_ge(s_tr, 4 * st + n + 1)
                    nc.scalar.copy(xT[:, 4 * (n % 2):4 * (n % 2) + 4, P * (n // 2):P * (n // 2) + P],
                                   PS[:, 4 + n, :].rearrange("p (k t) -> p k t", k=4)).then_inc(s_xT, 1)

        def pe_transpose(pe, st):
            if st == 0:
                pe.wait_ge(s_x, 16)
                pe.wait_ge(s_const, 1)
            for n in range(4):
                if st and n % 2 == 0:
                    pe.wait_ge(s_ln, TT * (st - 1) + n // 2 + 1)
                for k in range(4):
                    ins = nc.tensor.transpose(PS[:, 4 + n, k * P:(k + 1) * P],
                                              X[:, n // 2, (4 * (n % 2) + k)::KT], ident[:, :])
                ins.then_inc(s_tr, 1)

        def layer_norm(v, link, st):
            v.wait_ge(s_gb, 32 * (st + 1))
            for t in range(TT):
                v.wait_ge(s_res, TT * st + t + 1)
                for h in range(2):
                    link(nc.vector.scalar_tensor_tensor(out=X[:, t, 512 * h:512 * h + 512],
                                                        in0=X[:, t, 512 * h:512 * h + 512], scalar=ALPHA,
                                                        in1=PS[:, 2 * t + h, :], op0=ALU.mult, op1=ALU.add))
                link.sync()
                for h in range(2):
                    link(nc.vector.bn_stats(stat[:, h, :], X[:, t, 512 * h:512 * h + 512]))
                link.sync()
                link(nc.vector.bn_aggr(mv[:, 0:2], stat[:, :, :]))
                link.sync()
                nc.vector.tensor_scalar(mv[:, 3:4], mv[:, 1:2], LN_EPS, None, ALU.add).then_inc(s_var, 1)
                v.wait_ge(s_std, TT * st + t + 1)
                link(nc.vector.reciprocal(mv[:, 2:3], mv[:, 3:4]))
                link.sync()
                link(nc.vector.scalar_tensor_tensor(out=X[:, t, :], in0=X[:, t, :], scalar=mv[:, 0:1], in1=GB[:, 0, :],
                                                    op0=ALU.subtract, op1=ALU.mult))
                link.sync()
                nc.vector.scalar_tensor_tensor(out=X[:, t, :], in0=X[:, t, :], scalar=mv[:, 2:3], in1=GB[:, 1, :],
                                               op0=ALU.mult, op1=ALU.add).then_inc(s_ln, 1)

        def act_ln(s, st):
            for t in range(TT):
                s.wait_ge(s_var, TT * st + t + 1)
                nc.scalar.activation(mv[:, 3:4], mv[:, 3:4], ACT.Sqrt).then_inc(s_std, 1)

        def load_ln(sp, st):
            g, b = (a["ln_mix_g"], a["ln_mix_b"]) if st % 2 == 0 else (a["ln_ffn_g"], a["ln_ffn_b"])
            l = st // 2
            if st:
                sp.wait_ge(s_ln, TT * st)
            sp.dma_start(GB[:, 0, :], g[l:l + 1, :].to_broadcast([P, D])).then_inc(s_gb, 16)
            sp.dma_start(GB[:, 1, :], b[l:l + 1, :].to_broadcast([P, D])).then_inc(s_gb, 16)

        def chunk(i):
            return WB[:, i % 2, :].rearrange("p (k c) -> p k c", k=KT)

        def load_chunk(sp, src, b, c):
            sp.dma_start(chunk(b), src[:, :, ds(c * CB, CB)]).then_inc(s_wl[b], 16)

        def stream(sp, src, n0, tile0, count):
            lead = 1 if n0 == 0 else 0
            for b in range(2 * lead):
                load_chunk(sp, src, b, b)
            with sp.Fori(lead, count // 2) as i:
                for b in range(2):
                    sp.wait_ge(s_pj, 4 * i + (tile0 + 2 * (n0 + b) - 2))
                    load_chunk(sp, src, b, 2 * i + b)

        def project_channels(pe, x, base, chunks, tile0, x_whole=None):
            with pe.Fori(0, chunks // 2) as i:
                for b in range(2):
                    pe.wait_ge(s_wl[b], 16 * i + 16 * (base // 2 + 1))
                    for c in range(2):
                        pe.wait_ge(s_pe, 4 * i + (tile0 + 2 * b + c + 1))
                        for k in range(KT):
                            if k == KT // 2 and b == 0 and c == 0 and x_whole:
                                x_whole()
                            ins = nc.tensor.matmul(PS[:, 4 + 2 * b + c, 0:T], chunk(b)[:, k, c * P:(c + 1) * P],
                                                   x[:, k, :], start=(k == 0), stop=(k == KT - 1))
                        ins.then_inc(s_pj, 1)

        def project_tokens(pe, x, base, chunks, tile0):
            with pe.Fori(0, chunks // 2) as i:
                for b in range(2):
                    pe.wait_ge(s_wl[b], 16 * i + 16 * (base // 2 + 1))
                    for t in range(TT):
                        pe.wait_ge(s_pe, 4 * i + (tile0 + 2 * b + t + 1))
                        for k in range(KT):
                            ins = nc.tensor.matmul(PS[:, 4 + 2 * b + t, 0:CB], x[:, k, t * P:(t + 1) * P],
                                                   chunk(b)[:, k, :], start=(k == 0), stop=(k == KT - 1))
                        ins.then_inc(s_pj, 1)

        def out_project(pe, x, base, l, tile_ready):
            for c in range(4):
                g = base + c
                pe.wait_ge(s_wl[g % 2], 16 * (g // 2 + 1))
                for t in range(TT):
                    if c == 0:
                        tile_ready(t)
                    for k in range(KT):
                        ins = nc.tensor.matmul(PS[:, 2 * t + c // 2, (c % 2) * CB:(c % 2) * CB + CB],
                                               x[:, k, t * P:(t + 1) * P], chunk(g)[:, k, :],
                                               start=(k == 0), stop=(k == KT - 1))
                    if c == 3 and t == 0:
                        ins.then_inc(s_res, 1)
                ins.then_inc(s_wf, 1)
            pe.wait_ge(s_wf, 4 * l + 4)
            pe.sem_inc(s_res, 1)

        def copy_tiles(s, dst, tile0, iters):
            with s.Fori(0, iters) as i:
                for n in range(4):
                    s.wait_ge(s_pj, 4 * i + (tile0 + n + 1))
                    nc.scalar.copy(dst[:, ds(4 * i + n, 1), :], PS[:, 4 + n:5 + n, 0:T]).then_inc(s_pe, 1)

        def constants(g):
            link = Link(g, s_g2d)
            L.append(link)

            def keep(dst, pattern, base, mult, op, fill=0.0):
                link(nc.gpsimd.affine_select(out=dst, in_=dst, compare_op=op, fill=fill, base=base,
                                             pattern=pattern, channel_multiplier=mult))

            link(nc.gpsimd.memset(ident[:, :], 0.0))
            link.sync()
            keep(ident[:, :], [[-1, P]], 0, 1, ALU.not_equal, 1.0)
            link.sync()
            g.sem_inc(s_const, 1)
            for dst, val in ((ones[:, :], 1.0), (before[:, :], 1.0), (bones[:, :], 0.0),
                             (tri8[:, :, :], 1.0), (MK[:, :, :], 1.0), (LM[:, :, :], 1.0), (m01[:, :], 1.0),
                             (Z1[:, :, :], 0.0), (FFT[:, :, T:T + 1], 0.0), (MQ[:, :, :], 0.0)):
                link(nc.gpsimd.memset(dst, val))
            link(nc.gpsimd.iota(ioi[:, 0:T], pattern=[[1, T]], base=0, channel_multiplier=0))
            link(nc.gpsimd.iota(ioi[:, T:T + 1], pattern=[[1, 1]], base=0, channel_multiplier=1))
            link.sync()

            keep(before[:, :], [[1, P]], 0, -1, ALU.is_gt)
            keep(tri8[:, :, :], [[1, NG], [-1, NG]], 0, 0, ALU.is_gt)
            keep(MK[:, 0, :], [[1, P]], 0, -1, ALU.is_gt)
            keep(MK[:, 1, :], [[1, P]], 0, -1, ALU.is_ge)
            for q in range(TT):
                keep(MQ[:, q, :], [[-1, T]], q * P, 1, ALU.is_gt, -BIG)
            link.sync()
            for c in range(2):
                link(nc.gpsimd.memset(bones[c * HD:(c + 1) * HD, c * HD:(c + 1) * HD], 1.0))
                link.sync()
            for c in range(NCH):
                link(nc.gpsimd.memset(m01[:, c * CH:c * CH + 1], 0.0))
            link(nc.gpsimd.memset(Z1[:, :, T:T + 1], 1.0))
            link.sync()
            link(nc.gpsimd.memset(MK[0:CH, :, CH:P], 0.0))
            link.sync()
            for lv in range(6):
                w = 1 << lv
                nb = P // (2 * w)
                v = LM[:, lv, :].rearrange("p (n t) -> p n t", t=2 * w)
                lo, hi = v[:, :, 0:w], v[:, :, w:2 * w]
                link(nc.gpsimd.memset(lo, 0.0))
                for pattern, base, mult in (([[-2 * w, nb], [0, w]], 0, 1), ([[2 * w, nb], [0, w]], w - 1, -1)):
                    keep(hi, pattern, base, mult, ALU.is_ge)
                    link.sync()
            for g_, win in enumerate((2, 4, 8, 16)):
                link(nc.gpsimd.tensor_scalar(ICN[:, g_, :], ioi[:, 0:T], 1.0, float(win), ALU.add, ALU.min))
            link(nc.gpsimd.tensor_copy(iotab[:, :], ioi[:, 0:B]))
            link(nc.gpsimd.tensor_copy(iotap[:, :], ioi[:, 0:NOV]))
            link(nc.gpsimd.tensor_copy(ecol[:, :], ioi[:, T:T + 1]))
            link(nc.gpsimd.tensor_scalar(thr[:, :], ioi[:, 1:NR + 1], float(B), None, ALU.mult))
            link(nc.gpsimd.tensor_scalar(rbase[:, :], ioi[:, 1:NR + 1], -float(B), 1.0, ALU.mult, ALU.add))
            link.sync()
            g.sem_inc(s_const, 1)

        L = []

        s_pw = sem("pool_weights_loaded")
        s_dif = sem("pool_differences_ready")
        s_yp = sem("pool_product_done")
        s_cat = sem("mixed_heads_ready")
        s_z = sem("scores_done")
        s_zm = sem("masked_scores_ready")
        s_sig = sem("sigmoids_ready")
        s_w = sem("stick_weights_ready")
        s_wt = sem("stick_weights_transposed")
        s_wtc = sem("stick_weights_copied")
        s_o = sem("heads_done")
        s_l0c = sem("layer0_constants_ready")
        L0CH = 8 + 4
        w_in = a["ab_w_in"][0].rearrange("(p k) c -> p k c", k=KT)
        w_out = a["ab_w_out"][0].rearrange("(k p) c -> p k c", p=P)

        def sp_mix0(sp):
            sp.dma_start(X[:, :, :], a["x"][0].rearrange("(t p) d -> p t d", p=P)).then_inc(s_x, 16)
            stream(sp, w_in, 0, 0, 8)
            sp.dma_start(PW[:, :, :], a["ab_pool_w"][0].rearrange("g c d -> c g d")).then_inc(s_pw, 16)
            with nc.allow_non_contiguous_dma(reason="a few short vectors"):
                sp.dma_start(PSC[:, :], a["ab_pool_scale"][0].rearrange("(g p) -> p g", p=P)).then_inc(s_pw, 16)
            load_ln(sp, 0)
            sp.dma_start(WR[:, :, :, :], a["moe_w_router"].rearrange("l (p k) e -> p l k e", k=KT)).then_inc(s_vec, 16)
            sp.dma_start(EB[:, :, :].rearrange("p l e -> p (l e)"),
                         a["moe_e_bias"].rearrange("(o l) e -> o (l e)", o=1).to_broadcast([P, 2 * E])).then_inc(s_vec, 16)
            with nc.allow_non_contiguous_dma(reason="a few short vectors"):
                sp.dma_start(MU[:, :, :], a["rw_mu"][0].rearrange("m (p k) -> p m k", k=KT)).then_inc(s_vec, 16)
                for n, name in enumerate(["rw_w0", "rw_a0", "rw_k_k", "rw_k_a", "rw_r_k", "rw_lnx_g", "rw_lnx_b"]):
                    v = a[name][0] if name != "rw_r_k" else a[name][0].rearrange("h n -> (h n)")
                    sp.dma_start(VEC[:, n, :], v.rearrange("(k p) -> p k", p=P)).then_inc(s_vec, 16)
            for c in range(2):
                sp.wait_ge(s_pj, 2 * (8 + c) - 2)
                load_chunk(sp, w_out, c, c)
            moe[0]["prefetch"](sp)
            sp.wait_ge(s_cat, 4)
            moe[0]["load_expert"](sp, 1, 1)
            for c in range(2, 4):
                sp.wait_ge(s_wf, c - 1)
                load_chunk(sp, w_out, c % 2, c)
            sp.wait_ge(s_o, 2)
            moe[0]["load_expert"](sp, 3, 3)

        def gp_mix0(g):
            link_g = L[0]
            g.wait_ge(s_l0c, 1)
            g.wait_ge(s_pe, 4 + 4)
            src, w = UQK[:, 0:4, :], 1
            for lv, dst in enumerate([WS1, WS2, WS1, WS2]):
                link_g(nc.gpsimd.tensor_tensor(dst[:, lv:4, w:T], src[:, lv:4, w:T], src[:, lv:4, 0:T - w], ALU.add))
                link_g(nc.gpsimd.tensor_copy(dst[:, lv:4, 0:w], src[:, lv:4, 0:w]))
                link_g.sync()
                link_g(nc.gpsimd.tensor_tensor(DIF[:, lv, :], dst[:, lv, :], ICN[:, lv, :], ALU.mult))
                link_g.sync()
                nc.gpsimd.tensor_tensor(DIF[:, lv, :], DIF[:, lv, :], UQK[:, lv, :], ALU.subtract).then_inc(s_dif, 1)
                src, w = dst, 2 * w

        def pe_mix0(pe):
            pe_transpose(pe, 0)
            pe.wait_ge(s_xT, 4)
            project_channels(pe, xT, 0, 6, 0)

            def scores(q):
                for h in range(H0):
                    r = HD * (h % 2)
                    n = 4 * (h % 2) + h // 2
                    ins = nc.tensor.matmul(PS[:, 4 * q + n // 2, (n % 2) * T:(n % 2) * T + T],
                                           UQK[r:r + HD, 4 + h // 2, q * P:(q + 1) * P],
                                           UQK[r:r + HD, 8 + h // 2, :], start=True, stop=True)
                ins.then_inc(s_z, 1)

            def turn_weights(q):
                pe.wait_ge(s_w, q + 1)
                for n in range(H0):
                    for k in range(TT):
                        m = 2 * n + k
                        ins = nc.tensor.transpose(PS[:, m // 4, (m % 4) * P:(m % 4) * P + P],
                                                  BET[:, n, k * P:(k + 1) * P], ident[:, :])
                ins.then_inc(s_wt, 1)

            def heads(q):
                pe.wait_ge(s_wtc, q + 1)
                for h in range(H0):
                    n = 4 * (h % 2) + h // 2
                    r = HD * (h % 2)
                    for k in range(TT):
                        ins = nc.tensor.matmul(PS[r:r + HD, 6 + q, (h // 2) * P:(h // 2) * P + P],
                                               V0[:, k, h * HD:(h + 1) * HD], WT[:, 2 * n + k, :],
                                               start=(k == 0), stop=(k == TT - 1))
                ins.then_inc(s_o, 1)

            pe.wait_ge(s_pe, 4 + 12)
            scores(0)
            project_tokens(pe, xT, 6, 2, 12)
            pe.wait_ge(s_pe, 4 + 16)
            scores(1)
            turn_weights(0)
            pe.wait_ge(s_pw, 32)
            pe.wait_ge(s_dif, 4)
            pe.wait_ge(s_zm, 8)
            for g in range(4):
                ins = nc.tensor.matmul(PS[:, 4 + g // 2, (g % 2) * T:(g % 2) * T + T], PW[:, g, :], DIF[:, g, :],
                                       start=True, stop=True)
            ins.then_inc(s_yp, 1)
            heads(0)
            turn_weights(1)
            heads(1)
            out_project(pe, CAT, 8, 0, lambda t: pe.wait_ge(s_cat, 4 + t + 1))

        def act_mix0(s):
            s.sem_inc(s_pe, 4)
            act_transpose_copy(s, 0)
            s.wait_ge(s_xT, 4)
            copy_tiles(s, UQK, 0, 3)

            def turned(q):
                s.wait_ge(s_wt, q + 1)
                for n in range(4):
                    ins = nc.scalar.copy(WT[:, 4 * n:4 * n + 4, :], PS[:, n, :].rearrange("p (m q) -> p m q", m=4))
                ins.then_inc(s_wtc, 1)

            def heads_out(q):
                s.wait_ge(s_o, q + 1)
                nc.scalar.copy(CAT[:, 4:8, q * P:(q + 1) * P],
                               PS[:, 6 + q, :].rearrange("p (m q) -> p m q", m=4)).then_inc(s_cat, 1)

            s.wait_ge(s_zm, 4)
            nc.scalar.activation(FFT[:, :, 0:T], ZM[:, :, :], ACT.Sigmoid, scale=-1.0).then_inc(s_sig, 1)
            nc.scalar.activation(BET[:, :, :], ZM[:, :, :], ACT.Sigmoid).then_inc(s_sig, 1)
            for n in range(4):
                s.wait_ge(s_pj, 12 + n + 1)
                nc.scalar.copy(V0[:, n % 2, (n // 2) * CB:(n // 2) * CB + CB], PS[:, 4 + n, 0:CB]).then_inc(s_pe, 1)
            s.wait_ge(s_zm, 8)
            s.wait_ge(s_w, 1)
            nc.scalar.activation(FFT[:, :, 0:T], ZM[:, :, :], ACT.Sigmoid, scale=-1.0).then_inc(s_sig, 1)
            turned(0)
            nc.scalar.activation(BET[:, :, :], ZM[:, :, :], ACT.Sigmoid).then_inc(s_sig, 1)
            s.wait_ge(s_yp, 1)
            for g in range(4):
                nc.scalar.activation(CAT[:, g, :], PS[:, 4 + g // 2, (g % 2) * T:(g % 2) * T + T], ACT.Copy,
                                     scale=PSC[:, g:g + 1]).then_inc(s_cat, 1)
            heads_out(0)
            s.wait_ge(s_o, 1)
            turned(1)
            heads_out(1)

        def dve_mix0(v, link):
            dve_transpose_copy(v, 0)
            v.wait_ge(s_const, 2)
            nc.vector.reciprocal(ICN[:, :, :], ICN[:, :, :]).then_inc(s_l0c, 1)
            for q in range(TT):
                v.wait_ge(s_z, q + 1)
                if q:
                    v.wait_ge(s_sig, 2 * q)
                for n in range(4):
                    nc.vector.scalar_tensor_tensor(
                        out=ZM[:, 2 * n:2 * n + 2, :], in0=PS[:, 4 * q + n, :].rearrange("p (h k) -> p h k", h=2),
                        scalar=HD ** -0.5, in1=MQ[:, q:q + 1, :].to_broadcast([P, 2, T]),
                        op0=ALU.mult, op1=ALU.add).then_inc(s_zm, 1)
                v.wait_ge(s_sig, 2 * q + 1)
                fl = lambda m: m.rearrange("p h k -> p (h k)")[:, ::-1]
                link(nc.vector.tensor_tensor_scan(out=fl(IPR), data0=fl(FFT), data1=fl(Z1), initial=1.0,
                                                  op0=ALU.mult, op1=ALU.add))
                link.sync()
                v.wait_ge(s_sig, 2 * q + 2)
                nc.vector.tensor_tensor(BET[:, :, :], BET[:, :, :], IPR[:, :, 1:T + 1], ALU.mult).then_inc(s_w, 1)

        s_lw = sem("lora_weights_loaded")
        s_xm = sem("mixed_input_ready")
        s_lh = sem("lora_hidden_done")
        s_lhc = sem("lora_hidden_ready")
        names = ["head_maps_ready", "keys_scaled", "key_squares_ready", "head_squares_done",
                 "head_squares_guarded", "root_ready", "norm_ready", "norm_spread", "log_decay_ready", "key_norm_used",
                 "keys_mixed", "decays_ready", "bonus_terms_ready", "bonus_done", "bonus_ready", "operands_ready",
                 "norm_params_loaded", "pairs_done", "pair_operands_ready", "pair_decayed_ready", "pair_values_ready",
                 "residual_terms_ready", "turned", "turned_copied",
                 "gram_b_done", "gram_k_done", "gram_b_ready", "gram_k_ready", "level_ready", "inverse0_ready",
                 "inverse0_turned", "product_done", "product_ready", "inverse_done", "inverse_ready",
                 "rhs_done", "rhs_ready", "solution_done", "solution_ready", "increment_done", "state_ready",
                 "y_done", "y_copied", "variance_ready", "deviation_ready", "scales_ready", "scaled", "normed_ready", "result_turned",
                 "result_ready"]
        r = {n: sem("rwkv_" + n) for n in names}
        NPASS = KT // 2
        L1F = 12

        TK, TW, TA, TR, TV, TG = range(16, 64, 8)
        PROJECTED = 64
        FREE = 2

        def sp_mix1(sp):
            sp.wait_ge(s_res, 2 * TT)
            wk, wr, wv = [a[name][0].rearrange("(p k) c -> p k c", k=KT) for name in ("rw_w_k", "rw_w_r", "rw_w_v")]
            for c in range(2):
                load_chunk(sp, wk, c, c)
            for dst, src in [(w1, a["rw_w_w1"][0].rearrange("(p k) c -> p k c", k=KT)),
                             (a1w, a["rw_a1"][0].rearrange("(p k) c -> p k c", k=KT)),
                             (w2[0:64, :], a["rw_w_w2"][0]), (a2[0:64, :], a["rw_a2"][0])]:
                sp.dma_start(dst, src).then_inc(s_lw, 16)
            for c in range(2, 4):
                sp.wait_ge(s_pj, TK + 2 * (c - 1))
                load_chunk(sp, wk, c % 2, c)
            load_ln(sp, 2)
            for src, ready in ((wr, (TK + 6, TK + 8, TR + 2, TR + 4)), (wv, (TR + 6, TR + 8, TV + 2, TV + 4))):
                for c in range(4):
                    sp.wait_ge(s_pj, ready[c])
                    load_chunk(sp, src, c % 2, c)
                    if src is wr and c == 1:
                        for dst, s_ in [(g1, a["rw_g1"][0].rearrange("(p k) c -> p k c", k=KT)),
                                        (g2a, a["rw_g2"][0][0:P, :]), (g2b[0:32, :], a["rw_g2"][0][P:160, :])]:
                            sp.dma_start(dst, s_).then_inc(s_lw, 16)
            wo = a["rw_w_o"][0].rearrange("(k p) c -> p k c", p=P)
            for c in range(2):
                sp.wait_ge(s_pj, TV + 6 + 2 * c)
                load_chunk(sp, wo, c, c)
            sp.wait_ge(s_pj, PROJECTED)
            sp.wait_ge(r["bonus_done"], 1)
            for n, name in enumerate(["rw_lnx_g", "rw_lnx_b"]):
                sp.dma_start(LGB[:, n, :], a[name][0:1, :].to_broadcast([P, D])).then_inc(r["norm_params_loaded"], 16)
            moe[1]["prefetch"](sp)
            sp.wait_ge(r["pairs_done"], 1)
            sp.wait_ge(r["variance_ready"], 1)
            for e in range(2):
                moe[1]["load_expert"](sp, e, e)
            for c in range(2, 4):
                sp.wait_ge(s_wf, 4 + c - 1)
                load_chunk(sp, wo, c % 2, c)
            moe[1]["load_expert"](sp, 3, 3)

        def dve_mix1(v, link):
            V = nc.vector
            flat2 = lambda m: m.rearrange("p k t -> p (k t)")
            dve_transpose_copy(v, 2)
            v.wait_ge(s_xT, 12)
            v.wait_ge(s_vec, 16 * 10)
            link(V.tensor_scalar(VEC[:, V_1KA, :], VEC[:, V_KA, :], -1.0, 1.0, ALU.mult, ALU.add))

            def mix(buf, m, tiles=range(KT)):
                for k in tiles:
                    ins = V.scalar_tensor_tensor(out=XM[:, buf, k, :], in0=XX[:, k, :], scalar=MU[:, m, k:k + 1],
                                                 in1=xT[:, k, :], op0=ALU.mult, op1=ALU.add)
                ins.then_inc(s_xm, 1)

            MR, MW, MK_, MV, MA, MG = range(6)
            for h in range(2):
                ks = slice(4 * h, 4 * h + 4)
                link(V.tensor_tensor(XX[:, ks, 1:T], xT[:, ks, 0:T - 1], xT[:, ks, 1:T], ALU.subtract))
                link(V.tensor_scalar(XX[:, ks, 0:1], xT[:, ks, 0:1], -1.0, None, ALU.mult))
                link.sync()
                mix(0, MK_, range(4 * h, 4 * h + 4))
            mix(1, MW)
            v.wait_ge(s_pj, TK + 8)
            mix(0, MA)
            v.wait_ge(s_pe, 4 + TK + 8)
            for k in range(KT):
                ins = V.tensor_scalar(T1[:, k, :], KTT[:, k, :], VEC[:, V_KK, k:k + 1], None, ALU.mult)
            ins.then_inc(r["keys_scaled"], 1)
            v.wait_ge(s_lh, 1)
            mix(1, MR)
            v.wait_ge(s_lh, 2)
            mix(0, MV)
            v.wait_ge(s_pe, 4 + TW + 8)
            for k in range(KT):
                link(V.tensor_tensor_scan(out=T3[:, k, :], data0=m01[:, :], data1=SG[:, k, :], initial=0.0,
                                          op0=ALU.mult, op1=ALU.add))
            link.sync()
            V.tensor_tensor(flat2(SG), flat2(T3), flat2(SG), ALU.subtract).then_inc(r["log_decay_ready"], 1)
            v.wait_ge(s_pe, 4 + TA + 8)
            for k in range(KT):
                link(V.tensor_scalar(T2[:, k, :], AT[:, k, :], VEC[:, V_KA, k:k + 1], VEC[:, V_1KA, k:k + 1],
                                     ALU.mult, ALU.add))
            link.sync()
            v.wait_ge(r["keys_scaled"], 1)
            V.tensor_tensor(flat2(KTT), flat2(KTT), flat2(T2), ALU.mult).then_inc(r["keys_mixed"], 1)
            v.wait_ge(r["head_squares_done"], 1)
            V.tensor_scalar(SSQ, PS[:, 0, 0:T], 1e-24, None, ALU.max).then_inc(r["head_squares_guarded"], 1)
            v.wait_ge(r["root_ready"], 1)
            V.reciprocal(SSQ, SSQ).then_inc(r["norm_ready"], 1)
            v.wait_ge(s_pj, TR + 8)
            mix(1, MG)
            v.wait_ge(r["norm_spread"], 1)
            for n in range(4):
                ins = V.tensor_tensor(flat2(T1)[:, 512 * n:512 * n + 512], flat2(T1)[:, 512 * n:512 * n + 512],
                                      PS[:, n, :], ALU.mult)
                if n < 3:
                    link(ins)
            ins.then_inc(r["key_norm_used"], 1)
            v.wait_ge(r["key_norm_used"], 1)
            link.sync()
            v.wait_ge(r["decays_ready"], 1)
            link(V.tensor_tensor(flat2(SG), flat2(T1), flat2(SG), ALU.mult))
            link(V.tensor_tensor(flat2(AT), flat2(AT), flat2(T1), ALU.mult))
            link(V.tensor_copy(DCE[:, :, :].rearrange("p c k -> p k c"), T2[:, :, CH - 1::CH]))
            link.sync()
            link(V.tensor_tensor(flat2(AT), flat2(AT), flat2(T3), ALU.mult))
            v.wait_ge(s_pe, 4 + TR + 8)
            for k in range(KT):
                ins = V.scalar_tensor_tensor(out=T1[:, k, :], in0=KTT[:, k, :], scalar=VEC[:, V_RK, k:k + 1],
                                             in1=RT[:, k, :], op0=ALU.mult, op1=ALU.mult)
            ins.then_inc(r["bonus_terms_ready"], 1)
            v.wait_ge(r["bonus_terms_ready"], 1)
            link(V.tensor_tensor(flat2(RT), flat2(RT), flat2(T2), ALU.mult))
            link(V.tensor_tensor(flat2(KTT), flat2(KTT), flat2(T3), ALU.mult))
            link.sync()
            v.sem_inc(r["operands_ready"], 1)
            v.wait_ge(s_pj, PROJECTED)
            v.wait_ge(r["bonus_done"], 1)
            for b in pairs:
                link(V.memset(b.SS[:, :, :], 0.0))
            link.sync()
            with v.Fori(0, NPASS) as i:
                link.enter(i, 0, DVE_STEPS)
                dve_pass(v, link, i)
            link.leave(NPASS)
            link.sync()
            for t in range(TT):
                for h in range(16):
                    link(V.bn_aggr(MVS[:, t, h, :], STS[:, t, h, :]))
            link.sync()
            V.tensor_scalar(RS[:, :, :], MVS[:, :, :, 1], GN_EPS, None, ALU.add).then_inc(r["variance_ready"], 1)
            v.wait_ge(r["deviation_ready"], 1)
            link(V.reciprocal(RS[:, :, :], RS[:, :, :]))
            link.sync()
            V.scalar_tensor_tensor(out=NB, in0=MVS[:, 1, :, 0], scalar=-1.0, in1=RS[:, 1, :], op0=ALU.mult,
                                   op1=ALU.mult).then_inc(r["scales_ready"], 1)
            v.wait_ge(r["norm_params_loaded"], 32)
            wide = lambda m: m.rearrange("p (h o) -> p h o", o=1).to_broadcast([P, 16, HD])
            for t in range(TT):
                y = YTK[:, t, :]
                yh = y.rearrange("p (h d) -> p h d", h=16)
                if t == 0:
                    link(V.tensor_tensor(yh, yh, wide(MVS[:, t, :, 0]), ALU.subtract))
                    link.sync()
                    link(V.tensor_tensor(yh, yh, wide(RS[:, t, :]), ALU.mult))
                    link.sync()
                else:
                    v.wait_ge(r["scaled"], 1)
                link(V.tensor_tensor(y, y, LGB[:, 0, :], ALU.mult))
                link.sync()
                v.wait_ge(r["residual_terms_ready"], FREE + 2 * NPASS)
                V.tensor_tensor(y, y, V1[:, t, :], ALU.add).then_inc(r["normed_ready"], 1)
                for h in range(2):
                    v.wait_ge(r["result_turned"], 2 * t + h + 1)
                    V.tensor_tensor(KTT[:, 4 * h:4 * h + 4, t * P:(t + 1) * P],
                                    PS[:, 4 + 2 * t + h, :].rearrange("p (k t) -> p k t", k=4),
                                    GTT[:, 4 * h:4 * h + 4, t * P:(t + 1) * P], ALU.mult).then_inc(r["result_ready"], 1)

        DVE_STEPS = 30
        both = list(enumerate(pairs))

        def at(i, z, count=1, n=0):
            return 2 * count * i + (2 * n + z + 1)

        def dve_pass(v, link, i):
            four = lambda bank: bank.rearrange("p (m t) -> p m t", m=4)
            eye = ident[:, :].rearrange("p (o t) -> p o t", o=1).to_broadcast([P, 4, P])
            V = nc.vector
            for z, b in both:
                link(V.tensor_copy(b.DC[:, :], DCE[:, :, ds(2 * i + z, 1)].rearrange("p c o -> p (c o)")))
            mask = MK[:, :, :].rearrange("p (o m) t -> p o (m t)", o=1).to_broadcast([P, TT, 2 * P])
            quad = lambda m: m[:, :, :, 0, :].rearrange("p h a t -> p (h a) t")

            def masked(dst, bank, sem_):
                for h in range(2):
                    ins = V.tensor_tensor(dst[:, h, :, :, :].rearrange("p a m t -> p a (m t)"),
                                          PS[:, bank + h, :].rearrange("p (a f) -> p a f", a=TT), mask, ALU.mult)
                    if h == 0:
                        link(ins)
                    else:
                        ins.then_inc(sem_, 1)

            for z, b in both:
                v.wait_ge(r["gram_b_done"], at(i, z))
                masked(b.MP, 4 * z, r["gram_b_ready"])
            link.sync()
            for z, b in both:
                v.wait_ge(r["gram_b_ready"], at(i, z))
                link(V.tensor_tensor(b.XI, quad(b.MP), LM[:, 0:1, :].to_broadcast([P, 4, P]), ALU.mult))
            link.sync()
            for z, b in both:
                V.tensor_tensor(b.DT, eye, b.XI, ALU.subtract).then_inc(r["inverse0_ready"], 1)
            for z, b in both:
                v.wait_ge(r["gram_k_done"], at(i, z) + FREE)
                masked(b.NQ, 4 * z + 2, r["gram_k_ready"])
            for lv in range(LEVELS):
                for z, b in both:
                    v.wait_ge(r["product_done"], at(i, z, LEVELS, lv))
                    V.tensor_tensor(b.XI, eye, four(PS[:, 4 * z, :]), ALU.subtract).then_inc(r["product_ready"], 1)
            for c in range(NCH):
                t, rows = c // 2, slice(CH * (c % 2), CH * (c % 2) + CH)
                if c < NCH - 1:
                    dc = [b.DC[:, c:c + 1] for b in pairs]
                    for z, b in both:
                        if c:
                            v.wait_ge(r["state_ready"], at(i, z, NCH - 1, c - 1))
                        link(V.tensor_scalar(b.SD, b.SS[:, c, :], dc[z], None, ALU.mult))
                for z, b in both:
                    v.wait_ge(r["solution_done"], at(i, z, NCH, c))
                    V.tensor_scalar(b.UU[rows, t, :], PS[rows, 4 * z + 1, 0:P], -1.0, None,
                                    ALU.mult).then_inc(r["solution_ready"], 1)
                if c < NCH - 1:
                    link.sync()
                    for z, b in both:
                        v.wait_ge(r["increment_done"], at(i, z, NCH - 1, c))
                        for h in range(2):
                            q = slice(HD * h, HD * h + HD)
                            ins = V.scalar_tensor_tensor(out=b.SS[q, c + 1, q], in0=PS[q, 4 * z + 2, q], scalar=dc[z][q, :],
                                                         in1=b.SD[q, q], op0=ALU.mult, op1=ALU.add)
                            if h == 0:
                                link(ins)
                            else:
                                ins.then_inc(r["state_ready"], 1)
            for z, b in both:
                v.wait_ge(r["y_copied"], at(i, z) + FREE)
                for t in range(TT):
                    for h in range(2):
                        link(V.bn_stats(b.ST[:, t, h, :], YTK[:, t, ds(2 * P * i + (P * z + HD * h), HD)]))
            link.sync()
            for z, b in both:
                link(V.tensor_copy(STS[:, :, ds(4 * i + 2 * z, 2), :], b.ST[:, :, :, :]))

        def act_mix1(s):
            A = nc.scalar
            flat2 = lambda m: m.rearrange("p k t -> p (k t)")
            act_transpose_copy(s, 2)
            s.wait_ge(s_xT, 12)
            copy_tiles(s, KTT, TK, 2)
            s.wait_ge(s_lh, 1)
            A.activation(LH[0:64, 0, :], PS[0:64, 0, 0:T], ACT.Tanh).then_inc(s_lhc, 1)
            s.wait_ge(s_lh, 2)
            A.copy(LH[0:64, 1, :], PS[0:64, 1, 0:T]).then_inc(s_lhc, 1)
            for m in range(2):
                dst = (SG, AT)[m]
                with s.Fori(0, 2) as i:
                    for n in range(4):
                        s.wait_ge(s_pj, 4 * i + ((TW, TA)[m] + n + 1))
                        A.activation(dst[:, ds(4 * i + n, 1), :].rearrange("p o t -> p (o t)"), PS[:, 4 + n, 0:T],
                                     ACT.Sigmoid, bias=VEC[:, V_W0 + m, ds(4 * i + n, 1)]).then_inc(s_pe, 1)
            s.wait_ge(r["head_squares_guarded"], 1)
            A.activation(SSQ, SSQ, ACT.Sqrt).then_inc(r["root_ready"], 1)
            s.wait_ge(r["head_squares_done"], 1)
            copy_tiles(s, RT, TR, 2)
            s.wait_ge(r["log_decay_ready"], 1)
            s.wait_ge(r["keys_mixed"], 1)
            A.activation(flat2(T2), flat2(T3), ACT.Exp, scale=-CDEC)
            A.activation(flat2(SG), flat2(SG), ACT.Exp, scale=-CDEC)
            A.activation(flat2(T3), flat2(T3), ACT.Exp, scale=CDEC).then_inc(r["decays_ready"], 1)
            with s.Fori(0, 2) as i:
                for n in range(4):
                    s.wait_ge(s_pj, 4 * i + (TV + n + 1))
                    A.copy(V1[:, n % 2, ds((2 * i + n // 2) * CB, CB)], PS[:, 4 + n, 0:CB]).then_inc(s_pe, 1)
            s.wait_ge(s_lh, 4)
            A.activation(LH[:, 2, :], PS[:, 2, 0:T], ACT.Sigmoid).then_inc(s_lhc, 1)
            A.activation(LH[0:32, 3, :], PS[0:32, 3, 0:T], ACT.Sigmoid).then_inc(s_lhc, 1)
            copy_tiles(s, GTT, TG, 2)
            s.wait_ge(r["bonus_done"], 1)
            A.copy(BONT[:, :, :].rearrange("p t h -> p (t h)"), PS[:, 0, 0:TT * 16]).then_inc(r["bonus_ready"], 1)
            s.sem_inc(r["y_copied"], FREE)
            s.wait_ge(s_pe, 4 + PROJECTED)
            s.wait_ge(r["operands_ready"], 1)
            with s.Fori(0, NPASS) as i:
                act_pass(s, i)
            s.wait_ge(r["variance_ready"], 1)
            A.activation(RS[:, :, :], RS[:, :, :], ACT.Sqrt).then_inc(r["deviation_ready"], 1)
            s.wait_ge(r["scales_ready"], 1)
            for h in range(16):
                y = YTK[:, 1, h * HD:(h + 1) * HD]
                ins = A.activation(y, y, ACT.Identity, scale=RS[:, 1, h:h + 1], bias=NB[:, h:h + 1])
            ins.then_inc(r["scaled"], 1)

        def act_pass(s, i):
            four = lambda bank: bank.rearrange("p (m t) -> p m t", m=4)
            row = lambda m, z: m[:, ds(2 * i + z, 1), :].rearrange("p o (a t) -> p (o a) t", a=TT)
            A = nc.scalar
            for z, b in both:
                s.wait_ge(r["y_done"], at(i, z))
                A.copy(b.KR[:, :, 0, :], row(SG, z))
                A.copy(b.KR[:, :, 1, :], row(RT, z)).then_inc(r["pair_decayed_ready"], 1)
            for z, b in both:
                s.wait_ge(r["turned"], at(i, z))
                A.copy(b.BKT[:, :, :, :].rearrange("p m a t -> p (m a t)"), PS[:, 4 * z + 2, :]).then_inc(r["turned_copied"], 1)
            for z, b in both:
                s.wait_ge(r["residual_terms_ready"], at(i, z))
                A.copy(b.VP[:, :, :], V1[:, :, ds(P * (2 * i + z), P)]).then_inc(r["pair_values_ready"], 1)
            for z, b in both:
                s.wait_ge(r["inverse0_turned"], at(i, z))
                A.copy(b.DG, four(PS[:, 4 * z + 1, :])).then_inc(r["inverse_ready"], 1)
            for lv in range(LEVELS):
                for z, b in both:
                    s.wait_ge(r["inverse_done"], at(i, z, LEVELS, lv))
                    if lv < LEVELS - 1:
                        A.copy(b.DG, four(PS[:, 4 * z + 1, :]))
                    A.copy(b.DT, four(PS[:, 4 * z + 2, :])).then_inc(r["inverse_ready"], 1)
            for c in range(NCH):
                t, rows = c // 2, slice(CH * (c % 2), CH * (c % 2) + CH)
                for z, b in both:
                    s.wait_ge(r["rhs_done"], at(i, z, NCH, c))
                    A.copy(b.R1[rows, t, :], PS[rows, 4 * z, 0:P]).then_inc(r["rhs_ready"], 1)
            for z, b in both:
                s.wait_ge(r["y_done"], at(i, z) + FREE)
                A.copy(YTK[:, :, ds(P * (2 * i + z), P)],
                       PS[:, 4 * z + 3, 0:T].rearrange("p (t d) -> p t d", t=TT)).then_inc(r["y_copied"], 1)

        def gp_mix1(g):
            G = nc.gpsimd
            link = L[0]
            flat2 = lambda m: m.rearrange("p k t -> p (k t)")
            g.wait_ge(s_ln, 2 * TT)
            link(G.memset(OWN, 1.0))
            link(G.memset(WIN, 0.0))
            link.sync()
            for pattern, base, mult in (([[1, D]], 0, -HD), ([[-1, D]], HD - 1, HD)):
                link(G.affine_select(out=OWN, in_=OWN, compare_op=ALU.is_ge, fill=0.0, base=base, pattern=pattern,
                                     channel_multiplier=mult))
                link.sync()
            link(G.tensor_copy(WIN[:, P - 2:P], bones[:, 0:P:HD]))
            link.sync()
            g.sem_inc(r["head_maps_ready"], 1)
            g.wait_ge(r["keys_scaled"], 1)
            G.tensor_tensor(flat2(RT), flat2(T1), flat2(T1), ALU.mult).then_inc(r["key_squares_ready"], 1)
            g.sem_inc(r["residual_terms_ready"], FREE)
            g.wait_ge(s_pj, PROJECTED)
            g.wait_ge(r["bonus_done"], 1)
            g.wait_ge(r["operands_ready"], 1)
            with g.Fori(0, NPASS) as i:
                link.enter(i, 0, 2)
                row = lambda m, z: m[:, ds(2 * i + z, 1), :].rearrange("p o t -> p (o t)")
                for z, b in both:
                    g.wait_ge(r["gram_k_done"], at(i, z))
                    G.tensor_copy(b.BIK[:, 0, :], row(AT, z))
                    G.tensor_copy(b.BIK[:, 1, :], row(KTT, z)).then_inc(r["pair_operands_ready"], 1)
                for lv in range(LEVELS):
                    for z, b in both:
                        if lv == 0:
                            g.wait_ge(r["gram_b_ready"], at(i, z))
                        if lv >= 2:
                            g.wait_ge(r["product_done"], at(i, z, LEVELS, lv - 2))
                        G.tensor_tensor(b.LVL[:, lv % 2], b.MP[:, :, :, 0, :].rearrange("p h a t -> p (h a) t"),
                                        LM[:, lv + 1:lv + 2, :].to_broadcast([P, 4, P]),
                                        ALU.mult).then_inc(r["level_ready"], 1)
                for z, b in both:
                    n = P * (2 * i + z)
                    dst = V1[:, :, ds(n, P)]
                    g.wait_ge(r["bonus_ready"], 1)
                    g.wait_ge(r["pair_values_ready"], at(i, z))
                    link(G.tensor_tensor(dst.rearrange("p t (h d) -> p t h d", h=2),
                                         b.VP[:, :, :].rearrange("p t (h d) -> p t h d", h=2),
                                         BONT[:, :, ds(4 * i + 2 * z, 2)].rearrange("p t (h o) -> p t h o", o=1)
                                         .to_broadcast([P, TT, 2, HD]), ALU.mult))
                link.sync()
                g.wait_ge(r["norm_params_loaded"], 32)
                for z, b in both:
                    n = P * (2 * i + z)
                    dst = V1[:, :, ds(n, P)]
                    G.tensor_tensor(dst, dst, LGB[:, 1:2, ds(n, P)].to_broadcast([P, TT, P]),
                                    ALU.add).then_inc(r["residual_terms_ready"], 1)
            link.leave(NPASS)

        def pe_mix1(pe):
            mm = nc.tensor.matmul

            def hidden_low_rank(x, w, c0, m, bank):
                for k in range(KT):
                    ins = mm(PS[0:m, bank, 0:T], w[:, k, c0:c0 + m], XM[:, x, k, :], start=(k == 0), stop=(k == KT - 1))
                ins.then_inc(s_lh, 1)

            def out_low_rank(tile0, parts):
                for n in range(KT):
                    pe.wait_ge(s_pe, tile0 + n + 1)
                    for j, (w, h) in enumerate(parts):
                        ins = mm(PS[:, 4 + n % 4, 0:T], w[:, n * P:(n + 1) * P], h, start=(j == 0), stop=(j == len(parts) - 1))
                    ins.then_inc(s_pj, 1)

            pe_transpose(pe, 2)
            pe.wait_ge(s_xT, 12)
            pe.wait_ge(s_xm, 1)
            project_channels(pe, XM[:, 0, :, :], L1F, 4, TK, lambda: pe.wait_ge(s_xm, 2))
            pe.wait_ge(s_lw, 16 * 4)
            for n, w in enumerate((w1, a1w)):
                pe.wait_ge(s_xm, 3 + n)
                hidden_low_rank(1 - n, w, 0, 64, n)
            pe.wait_ge(s_lhc, 1)
            out_low_rank(TW, [(w2[0:64, :], LH[0:64, 0, :])])
            pe.wait_ge(s_lhc, 2)
            out_low_rank(TA, [(a2[0:64, :], LH[0:64, 1, :])])
            pe.wait_ge(r["head_maps_ready"], 1)
            pe.wait_ge(r["key_squares_ready"], 1)
            for k in range(KT):
                c0 = P - 2 - 2 * k
                ins = mm(PS[:, 0, 0:T], WIN[:, c0:c0 + P], RT[:, k, :], start=(k == 0), stop=(k == KT - 1))
            ins.then_inc(r["head_squares_done"], 1)
            pe.wait_ge(s_xm, 5)
            project_channels(pe, XM[:, 1, :, :], L1F + 4, 4, TR)
            pe.wait_ge(r["norm_ready"], 1)
            for k in range(KT):
                ins = mm(PS[:, k // 2, (k % 2) * T:(k % 2) * T + T], OWN[:, k * P:(k + 1) * P], SSQ, start=True, stop=True)
            ins.then_inc(r["norm_spread"], 1)
            pe.wait_ge(s_xm, 6)
            project_tokens(pe, XM[:, 0, :, :], L1F + 8, 4, TV)
            pe.wait_ge(s_lw, 16 * 7)
            pe.wait_ge(s_xm, 7)
            pe.wait_ge(r["key_norm_used"], 1)
            hidden_low_rank(1, g1, 0, P, 2)
            hidden_low_rank(1, g1, P, 32, 3)
            pe.wait_ge(s_lhc, 4)
            out_low_rank(TG, [(g2a, LH[:, 2, :]), (g2b[0:32, :], LH[0:32, 3, :])])
            pe.wait_ge(r["bonus_terms_ready"], 1)
            for t in range(TT):
                for k in range(KT):
                    ins = mm(PS[:, 0, 16 * t + 2 * k:16 * t + 2 * k + 2], T1[:, k, t * P:(t + 1) * P], bones[:, 0:P:HD],
                             start=True, stop=True)
            ins.then_inc(r["bonus_done"], 1)
            pe.wait_ge(s_pe, 4 + PROJECTED)
            pe.wait_ge(r["bonus_ready"], 1)
            pe.sem_inc(r["gram_k_done"], FREE)
            pe.sem_inc(r["y_done"], FREE)
            with pe.Fori(0, NPASS) as i:
                pe_pass(pe, i)
            pe.wait_ge(r["y_copied"], FREE + 2 * NPASS)
            pe.wait_ge(r["residual_terms_ready"], FREE + 2 * NPASS)
            pe.sem_inc(r["pairs_done"], 1)

            def tile_ready(t):
                pe.wait_ge(r["normed_ready"], t + 1)
                for h in range(2):
                    for k in range(4):
                        c0 = (4 * h + k) * P
                        ins = nc.tensor.transpose(PS[:, 4 + 2 * t + h, k * P:(k + 1) * P], YTK[:, t, c0:c0 + P], ident[:, :])
                    ins.then_inc(r["result_turned"], 1)
                pe.wait_ge(r["result_ready"], 2 * (t + 1))

            out_project(pe, KTT, L1F + 12, 1, tile_ready)

        def pe_pass(pe, i):
            mm = nc.tensor.matmul
            for z, b in both:
                pe.wait_ge(r["pair_operands_ready"], at(i, z))
                for m in range(2):
                    for t in range(TT):
                        o = (2 * m + t) * P
                        ins = nc.tensor.transpose(PS[:, 4 * z + 2, o:o + P], b.BIK[:, m, t * P:(t + 1) * P], ident[:, :])
                ins.then_inc(r["turned"], 1)

            def grams(z, m, bank, sem_):
                b = pairs[z]
                for h in range(2):
                    q = slice(HD * h, HD * h + HD)
                    for t in range(TT):
                        ins = mm(PS[:, bank + h, t * 2 * P:(t + 1) * 2 * P], b.BIK[q, m, t * P:(t + 1) * P],
                                 b.KR[q, t, :, :].rearrange("p m t -> p (m t)"), start=True, stop=True)
                ins.then_inc(sem_, 1)

            for z, b in both:
                pe.wait_ge(r["pair_decayed_ready"], at(i, z))
                grams(z, 0, 4 * z, r["gram_b_done"])
            for z, b in both:
                pe.wait_ge(r["turned_copied"], at(i, z))
                pe.wait_ge(r["y_copied"], at(i, z))
                grams(z, 1, 4 * z + 2, r["gram_k_done"])
            for z, b in both:
                pe.wait_ge(r["inverse0_ready"], at(i, z))
                for m in range(4):
                    ins = nc.tensor.transpose(PS[:, 4 * z + 1, m * P:(m + 1) * P], b.DT[:, m, :], ident[:, :])
                ins.then_inc(r["inverse0_turned"], 1)
            for lv in range(LEVELS):
                for z, b in both:
                    pe.wait_ge(r["level_ready"], at(i, z, LEVELS, lv))
                    pe.wait_ge(r["inverse_ready"], at(i, z, LEVELS + 1, lv))
                    for m in range(4):
                        ins = mm(PS[:, 4 * z, m * P:(m + 1) * P], b.LVL[:, lv % 2, m, :], b.DG[:, m, :], start=True, stop=True)
                    ins.then_inc(r["product_done"], 1)
                for z, b in both:
                    if lv == 0:
                        pe.wait_ge(r["gram_k_ready"], at(i, z))
                    pe.wait_ge(r["product_ready"], at(i, z, LEVELS, lv))
                    for m in range(4):
                        if lv < LEVELS - 1:
                            mm(PS[:, 4 * z + 1, m * P:(m + 1) * P], b.DT[:, m, :], b.XI[:, m, :], start=True, stop=True)
                    for m in range(4):
                        ins = mm(PS[:, 4 * z + 2, m * P:(m + 1) * P], b.XI[:, m, :], b.DT[:, m, :], start=True, stop=True)
                    ins.then_inc(r["inverse_done"], 1)
            for c in range(NCH):
                t, p0 = c // 2, CH * (c % 2)
                rows = slice(p0, p0 + CH)
                for z, b in both:
                    if c == 0:
                        pe.wait_ge(r["pair_values_ready"], at(i, z))
                        pe.wait_ge(r["product_ready"], at(i, z, LEVELS, LEVELS - 1))
                    else:
                        pe.wait_ge(r["rhs_ready"], at(i, z, NCH, c - 1))
                    for h in range(2):
                        hc = slice(h * HD, h * HD + HD)
                        ins = mm(PS[rows, 4 * z, hc], b.NQ[:, h, t, 0, rows], b.VP[:, t, hc], start=(h == 0),
                                 stop=(c == 0), skip_group_check=True)
                    if c:
                        pe.wait_ge(r["state_ready"], at(i, z, NCH - 1, c - 1))
                        ins = mm(PS[rows, 4 * z, 0:P], b.KR[:, t, 0, rows], b.SS[:, c, :], start=False, stop=True,
                                 skip_group_check=True)
                    ins.then_inc(r["rhs_done"], 1)
                for z, b in both:
                    if c == 0:
                        pe.wait_ge(r["inverse_ready"], at(i, z, LEVELS + 1, LEVELS))
                    pe.wait_ge(r["rhs_ready"], at(i, z, NCH, c))
                    if c:
                        pe.wait_ge(r["solution_ready"], at(i, z, NCH, c - 1))
                    for h in range(2):
                        hc = slice(h * HD, h * HD + HD)
                        ins = mm(PS[:, 4 * z + 1, hc], b.DT[rows, 2 * h + t, :], b.R1[rows, t, hc], start=True, stop=True)
                    ins.then_inc(r["solution_done"], 1)
                for z, b in both:
                    pe.wait_ge(r["solution_ready"], at(i, z, NCH, c))
                    if c < NCH - 1:
                        mm(PS[:, 4 * z + 2, 0:P], b.BKT[rows, 0, t, :], b.UU[rows, t, :], start=True, stop=False)
                        mm(PS[:, 4 * z + 2, 0:P], b.BKT[rows, 1, t, :], b.VP[rows, t, :], start=False,
                           stop=True).then_inc(r["increment_done"], 1)
            for z, b in both:
                for t in range(TT):
                    o = t * P
                    for c in range(2):
                        rows = slice(c * CH, (c + 1) * CH)
                        mm(PS[rows, 4 * z + 3, o:o + P], b.KR[:, t, 1, rows], b.SS[:, 2 * t + c, :], start=True, stop=False,
                           skip_group_check=True)
                    for h in range(2):
                        hc = slice(h * HD, h * HD + HD)
                        mm(PS[:, 4 * z + 3, o + h * HD:o + h * HD + HD], b.NQ[:, h, t, 1, :], b.VP[:, t, hc],
                           start=False, stop=False, skip_group_check=True)
                        ins = mm(PS[:, 4 * z + 3, o + h * HD:o + h * HD + HD], b.MP[:, h, t, 1, :], b.UU[:, t, hc],
                                 start=False, stop=True, skip_group_check=True)
                ins.then_inc(r["y_done"], 1)

        once = ["logits_done", "scores_ready", "mask_ready", "rank_done", "rank_ready", "count_ready",
                "shared_gate_up", "shared_silu", "shared_hidden"]
        by_pair = ["onehot_ready", "gathered0", "gathered1", "gathered0_copied", "gathered1_copied", "gate_up_done",
                   "silu_ready", "hidden_ready", "turned", "hidden_copied", "gates_copied", "down0", "down1",
                   "down0_copied", "down1_copied", "scattered"]
        per_layer = {n: 1 for n in once} | {n: PAIRS for n in by_pair} | {"shared_loaded": 48, "x_part": 3, "x_rest": 2}
        moe_shared = {n: sem("moe_" + n) for n in per_layer} | {
            "gu_w": [sem(f"gate_up_loaded{s}") for s in range(4)],
            "dn_w": [sem(f"down_loaded{s}") for s in range(4)]}
        per_layer |= {"gu_w": 32 * PAIRS // 2, "dn_w": 16 * PAIRS // 2}
        over_names = ["over_pe", "over_dve", "over_act", "over_loaded", "over_free", "over_link", "over_list"]

        def moe_view(l):
            q = moe_shared | {n: sem(f"l{l}_{n}") for n in over_names}
            past = {n: l * count for n, count in per_layer.items()}
            st = 2 * l + 1
            wg, wu, wd = a["moe_w_gate"][l], a["moe_w_up"][l], a["moe_w_down"][l]
            gate_src = lambda w, e: w[ds(e, 1), :, :].rearrange("o (p k) f -> p (o k) f", k=KT)
            down_src = lambda w, e: w[ds(e, 1), :, :].rearrange("o (k p) d -> p (o k) d", p=P)

            def gate_and_up(slot):
                w = RING[:, slot + 1, :] if slot < 2 else odd[:, slot - 2, :]
                return w[:, 0:4096].rearrange("p (m k f) -> p k m f", m=2, k=KT)

            def load_gate_up(sp, e, slot):
                g, u, d = wslot(slot)
                sp.dma_start(g, gate_src(wg, e)).then_inc(q["gu_w"][slot], 16)
                sp.dma_start(u, gate_src(wu, e)).then_inc(q["gu_w"][slot], 16)

            def load_down(sp, e, slot):
                sp.dma_start(wslot(slot)[2], down_src(wd, e)).then_inc(q["dn_w"][slot], 16)

            def load_expert(sp, e, slot):
                load_gate_up(sp, e, slot)
                load_down(sp, e, slot)

            def prefetch(sp):
                if l:
                    sp.wait_ge(s_res, 2 * TT)
                g, u, d = wslot(-1)
                sp.dma_start(g, a["moe_ws_gate"][l].rearrange("(p k) f -> p k f", k=KT)).then_inc(q["shared_loaded"], 16)
                sp.dma_start(u, a["moe_ws_up"][l].rearrange("(p k) f -> p k f", k=KT)).then_inc(q["shared_loaded"], 16)
                sp.dma_start(d, a["moe_ws_down"][l].rearrange("(k p) d -> p k d", p=P)).then_inc(q["shared_loaded"], 16)
                if l == 0:
                    load_expert(sp, 0, 0)

            def loads(sp):
                sp.wait_ge(s_res, TT * st)
                load_expert(sp, 2, 2)
                load_ln(sp, st)
                with sp.Fori(1, PAIRS // 2) as i:
                    for half in range(2):
                        sp.wait_ge(q["gate_up_done"], 2 * i + (half - 1) + past["gate_up_done"])
                        for s in range(2):
                            load_gate_up(sp, 4 * i + 2 * half + s, 2 * half + s)
                        sp.wait_ge(q["down1"], 2 * i + (half - 1) + past["down1"])
                        for s in range(2):
                            load_down(sp, 4 * i + 2 * half + s, 2 * half + s)
                sp.wait_ge(q["count_ready"], 1 + past["count_ready"])
                most = nc.sync.value_load(cnti[0:1, 2 * l:2 * l + 1], min_val=0, max_val=T)
                with sp.If(most > B):
                    sp.wait_ge(q["over_list"], 1)
                    rounds = nc.sync.value_load(cnti[0:1, 2 * l + 1:2 * l + 2], min_val=1, max_val=NOV // 2)
                    with sp.Fori(0, rounds) as i:
                        sp.wait_ge(q["over_free"], i + 1)
                        for s in range(2):
                            e = nc.sync.value_load(elist[0:1, ds(2 * i + s, 1)], min_val=0, max_val=E - 1)
                            g, u, d = wslot(s)
                            sp.dma_start(g, gate_src(wg, e)).then_inc(q["over_loaded"], 16)
                            sp.dma_start(u, gate_src(wu, e)).then_inc(q["over_loaded"], 16)
                            sp.dma_start(d, down_src(wd, e)).then_inc(q["over_loaded"], 16)

            def gather(pe, half, sel):
                for k in range(4):
                    for t in range(TT):
                        for n in range(3):
                            ins = nc.tensor.matmul(PS[:, 6 + half, k * 2 * B:(k + 1) * 2 * B],
                                                   XB[:, n, t, 4 * half + k::KT], sel[:, t, :, :].rearrange("p s b -> p (s b)"),
                                                   start=(t == 0 and n == 0), stop=(t == TT - 1 and n == 2))
                return ins

            def gate_up(pe, slots):
                for k in range(KT):
                    for s in range(2):
                        ins = nc.tensor.matmul(PS[s * B:(s + 1) * B, 4, :], XG[:, k, s * B:(s + 1) * B],
                                               gate_and_up(slots[s])[:, k, :, :], start=(k == 0), stop=(k == KT - 1))
                return ins

            def turn(pe, buf):
                for f in range(FT):
                    nc.tensor.transpose(PS[:, 4, f * 2 * B:(f + 1) * 2 * B], HH[0:2 * B, f * P:(f + 1) * P],
                                        ident[0:2 * B, 0:2 * B])
                for t in range(TT):
                    ins = nc.tensor.transpose(PS[0:2 * B, 4, T + t * P:T + (t + 1) * P],
                                              SELG[:, buf, t, :, :].rearrange("p s b -> p (s b)"), ident[:, :])
                return ins

            def down(pe, slots, h, bank):
                for f in range(FT):
                    for s in range(2):
                        ins = nc.tensor.matmul(PS[s * B:(s + 1) * B, bank, :], HT[:, f, s * B:(s + 1) * B],
                                               wslot(slots[s])[2][:, f, h * 512:(h + 1) * 512],
                                               start=(f == 0), stop=(f == FT - 1))
                return ins

            def scatter(pe, halves=range(2)):
                for h in halves:
                    for t in range(TT):
                        ins = nc.tensor.matmul(PS[:, 2 * t + h, :], GT[0:2 * B, t, :],
                                               Y[0:2 * B, h * 512:(h + 1) * 512], start=False, stop=True,
                                               skip_group_check=True)
                return ins

            def shared_down(pe):
                pe.wait_ge(q["shared_hidden"], 1 + past["shared_hidden"])
                for t in range(TT):
                    for h in range(2):
                        for f in range(FT):
                            nc.tensor.matmul(PS[:, 2 * t + h, :], HS[:, f, t * P:(t + 1) * P],
                                             wslot(-1)[2][:, f, h * 512:(h + 1) * 512], start=(f == 0), stop=(f == FT - 1))

            def pe_pair(pe, i, half, first, last, use):
                slots = (2 * half, 2 * half + 1)
                for n in range(2):
                    pe.wait_ge(q[f"gathered{n}_copied"], i + 1 + past[f"gathered{n}_copied"])
                for s in slots:
                    pe.wait_ge(q["gu_w"][s], 32 * use + 32 + past["gu_w"])
                if not first:
                    pe.wait_ge(q["hidden_copied"], i + past["hidden_copied"])
                    pe.wait_ge(q["gates_copied"], i + past["gates_copied"])
                gate_up(pe, slots).then_inc(q["gate_up_done"], 1)
                if first:
                    shared_down(pe)
                else:
                    pe.wait_ge(q["down0_copied"], i + past["down0_copied"])
                    pe.wait_ge(q["down1_copied"], i + past["down1_copied"])
                    scatter(pe).then_inc(q["scattered"], 1)
                pe.wait_ge(q["hidden_ready"], i + 1 + past["hidden_ready"])
                turn(pe, half).then_inc(q["turned"], 1)
                if not last:
                    pe.wait_ge(q["onehot_ready"], i + 2 + past["onehot_ready"])
                    gather(pe, 0, SEL1[:, 1 - half]).then_inc(q["gathered0"], 1)
                for s in slots:
                    pe.wait_ge(q["dn_w"][s], 16 * use + 16 + past["dn_w"])
                pe.wait_ge(q["hidden_copied"], i + 1 + past["hidden_copied"])
                down(pe, slots, 0, 5).then_inc(q["down0"], 1)
                if not last:
                    gather(pe, 1, SEL1[:, 1 - half]).then_inc(q["gathered1"], 1)
                if not last:
                    pe.wait_ge(q["down0_copied"], i + 1 + past["down0_copied"])
                down(pe, slots, 1, 6 if last else 5).then_inc(q["down1"], 1)

            def pe_moe(pe):
                pe_transpose(pe, st)
                pe.wait_ge(s_xT, 4 * (st + 1))
                pe.wait_ge(s_vec, 16 * 10)
                for t in range(TT):
                    for k in range(KT):
                        ins = nc.tensor.matmul(PS[:, 4, t * E:(t + 1) * E], xT[:, k, t * P:(t + 1) * P], WR[:, l, k, :],
                                               start=(k == 0), stop=(k == KT - 1))
                ins.then_inc(q["logits_done"], 1)
                pe.wait_ge(q["shared_loaded"], 48 + past["shared_loaded"])
                g, u, d = wslot(-1)

                def shared_in(w, bank, f):
                    for k in range(KT):
                        ins = nc.tensor.matmul(PS[:, bank, f * T:(f + 1) * T], w[:, k, f * P:(f + 1) * P], xT[:, k, :],
                                               start=(k == 0), stop=(k == KT - 1))
                    return ins

                for f in range(FT):
                    shared_in(g, 5, f)
                pe.wait_ge(q["mask_ready"], 1 + past["mask_ready"])
                nc.tensor.matmul(PS[:, 4, 0:E], before[:, :], MSK[:, 0, :], start=True, stop=True)
                nc.tensor.matmul(PS[:, 4, E:2 * E], ones[:, :], MSK[:, 0, :], start=True, stop=False)
                nc.tensor.matmul(PS[:, 4, E:2 * E], before[:, :], MSK[:, 1, :], start=False, stop=True)
                nc.tensor.matmul(PS[:, 4, 2 * E:3 * E], ones[:, :], MSK[:, 0, :], start=True, stop=False)
                nc.tensor.matmul(PS[:, 4, 2 * E:3 * E], ones[:, :], MSK[:, 1, :], start=False,
                                 stop=True).then_inc(q["rank_done"], 1)
                shared_in(u, 0, 0)
                pe.wait_ge(q["onehot_ready"], 1 + past["onehot_ready"])
                pe.wait_ge(q["x_part"], 3 + past["x_part"])
                gather(pe, 0, SEL1[:, 0]).then_inc(q["gathered0"], 1)
                gather(pe, 1, SEL1[:, 0]).then_inc(q["gathered1"], 1)
                shared_in(u, 0, 1).then_inc(q["shared_gate_up"], 1)
                pe.wait_ge(q["rank_ready"], 1 + past["rank_ready"])
                pe_pair(pe, 0, 0, True, False, 0)
                pe_pair(pe, 1, 1, False, False, 0)
                with pe.Fori(1, PAIRS // 2 - 1) as i:
                    pe_pair(pe, 2 * i, 0, False, False, i)
                    pe_pair(pe, 2 * i + 1, 1, False, False, i)
                pe_pair(pe, PAIRS - 2, 0, False, False, PAIRS // 2 - 1)
                pe_pair(pe, PAIRS - 1, 1, False, True, PAIRS // 2 - 1)
                pe.wait_ge(q["gates_copied"], PAIRS + past["gates_copied"])
                for h in range(2):
                    pe.wait_ge(q[f"down{h}_copied"], PAIRS + past[f"down{h}_copied"])
                    ins = scatter(pe, (h,))
                ins.then_inc(q["scattered"], 1)
                pe.wait_ge(q["count_ready"], 1 + past["count_ready"])
                most = nc.tensor.value_load(cnti[0:1, 2 * l:2 * l + 1], min_val=0, max_val=T)
                with pe.If(most > B):
                    pe_over(pe)
                pe.wait_ge(q["scattered"], PAIRS + past["scattered"])
                pe.sem_inc(s_res, TT)

            def pe_over(pe):
                pe.wait_ge(q["over_dve"], 1)
                nc.tensor.matmul(PS[0:E, 4, 0:NR], before[0:E, 0:E], F1[0:E, 0, :], start=True, stop=False)
                nc.tensor.matmul(PS[0:E, 4, 0:NR], ones[0:E, 0:E], F1[0:E, 1, :], start=False,
                                 stop=True).then_inc(q["over_pe"], 1)
                pe.wait_ge(q["over_dve"], 2)
                nc.tensor.matmul(PS[0:1, 5, 0:NOV], ecol[0:E, :], OS[0:E, 0, :], start=True, stop=True)
                nc.tensor.matmul(PS[0:1, 5, NOV:2 * NOV], ones[0:E, 0:1], OS[0:E, 0, :], start=True, stop=True)
                for t in range(TT):
                    nc.tensor.transpose(PS[0:E, 6, t * P:(t + 1) * P], RKX[:, t, 0:E], ident[:, :])
                    ins = nc.tensor.transpose(PS[0:E, 6, (2 + t) * P:(3 + t) * P], GX[:, t, 0:E], ident[:, :])
                ins.then_inc(q["over_pe"], 1)
                pe.wait_ge(q["over_dve"], 3)
                for t in range(TT):
                    o = t * NOV
                    nc.tensor.matmul(PS[:, 7, o:o + NOV], TR4[0:E, t, :], OS[0:E, 0, :], start=True, stop=False)
                    nc.tensor.matmul(PS[:, 7, o:o + NOV], ones[0:E, :], OS[0:E, 1, :], start=False, stop=True)
                    ins = nc.tensor.matmul(PS[:, 7, (2 + t) * NOV:(3 + t) * NOV], TR4[0:E, 2 + t, :], OS[0:E, 0, :],
                                           start=True, stop=True)
                ins.then_inc(q["over_pe"], 1)
                pe.wait_ge(q["over_list"], 1)
                rounds = nc.tensor.value_load(cnti[0:1, 2 * l + 1:2 * l + 2], min_val=1, max_val=NOV // 2)
                pe.sem_inc(q["over_free"], 1)
                with pe.Fori(0, rounds) as i:
                    pe.wait_ge(q["over_dve"], 5 * i + 5)
                    gather(pe, 0, SEL1[:, 0])
                    gather(pe, 1, SEL1[:, 0]).then_inc(q["over_pe"], 1)
                    pe.wait_ge(q["over_dve"], 5 * i + 6)
                    pe.wait_ge(q["over_loaded"], 96 * i + 96)
                    gate_up(pe, (0, 1)).then_inc(q["over_pe"], 1)
                    pe.wait_ge(q["over_dve"], 5 * i + 7)
                    turn(pe, 0).then_inc(q["over_pe"], 1)
                    pe.wait_ge(q["over_dve"], 5 * i + 8)
                    for h in range(2):
                        ins = down(pe, (0, 1), h, 5 + h)
                    ins.then_inc(q["over_pe"], 1)
                    pe.wait_ge(q["over_dve"], 5 * i + 9)
                    scatter(pe).then_inc(q["over_pe"], 1)
                    pe.wait_ge(q["over_pe"], 5 * i + 8)
                    pe.sem_inc(q["over_free"], 1)

            def silu(sem_):
                nc.scalar.activation(SIL[0:2 * B, :], PS[0:2 * B, 4, 0:FF], ACT.Silu).then_inc(sem_, 1)

            def copy_gathered(eng_copy, half):
                return eng_copy(XG[:, 4 * half:4 * half + 4, :].rearrange("p k b -> p (k b)"), PS[:, 6 + half, 0:8 * B])

            def act_pair(s, i, half, last):
                s.wait_ge(q["gate_up_done"], i + 1 + past["gate_up_done"])
                silu(q["silu_ready"])
                s.wait_ge(q["hidden_copied"], i + 1 + past["hidden_copied"])
                nc.scalar.copy(GT[0:2 * B, :, :].rearrange("p t b -> p (t b)"),
                               PS[0:2 * B, 4, T:2 * T]).then_inc(q["gates_copied"], 1)
                s.wait_ge(q["down0"], i + 1 + past["down0"])
                nc.scalar.copy(Y[0:2 * B, 0:512], PS[0:2 * B, 5, :]).then_inc(q["down0_copied"], 1)
                if not last:
                    s.wait_ge(q["gathered1"], i + 2 + past["gathered1"])
                    copy_gathered(nc.scalar.copy, 1).then_inc(q["gathered1_copied"], 1)

            def act_moe(s):
                part = lambda n: XB[:, n, :, :].rearrange("p t d -> p (t d)")
                act_transpose_copy(s, st)
                s.wait_ge(s_ln, TT * st)
                nc.scalar.copy(part(0), X[:, :, :].rearrange("p t d -> p (t d)")).then_inc(q["x_part"], 1)
                s.wait_ge(q["logits_done"], 1 + past["logits_done"])
                nc.scalar.activation(SCO[:, :, :].rearrange("p t e -> p (t e)"), PS[:, 4, 0:TT * E],
                                     ACT.Sigmoid).then_inc(q["scores_ready"], 1)
                for n in range(2):
                    s.wait_ge(q["x_rest"], n + 1 + past["x_rest"])
                    nc.scalar.copy(part(n + 1), XR).then_inc(q["x_part"], 1)
                s.wait_ge(q["gathered1"], 1 + past["gathered1"])
                copy_gathered(nc.scalar.copy, 1).then_inc(q["gathered1_copied"], 1)
                s.wait_ge(q["shared_gate_up"], 1 + past["shared_gate_up"])
                nc.scalar.activation(HSs[:, :, :].rearrange("p f t -> p (f t)"), PS[:, 5, :],
                                     ACT.Silu).then_inc(q["shared_silu"], 1)
                act_pair(s, 0, 0, False)
                act_pair(s, 1, 1, False)
                with s.Fori(1, PAIRS // 2 - 1) as i:
                    act_pair(s, 2 * i, 0, False)
                    act_pair(s, 2 * i + 1, 1, False)
                act_pair(s, PAIRS - 2, 0, False)
                act_pair(s, PAIRS - 1, 1, True)
                s.wait_ge(q["count_ready"], 1 + past["count_ready"])
                most = nc.scalar.value_load(cnti[0:1, 2 * l:2 * l + 1], min_val=0, max_val=T)
                with s.If(most > B):
                    s.wait_ge(q["over_list"], 1)
                    rounds = nc.scalar.value_load(cnti[0:1, 2 * l + 1:2 * l + 2], min_val=1, max_val=NOV // 2)
                    with s.Fori(0, rounds) as i:
                        s.wait_ge(q["over_pe"], 5 * i + 5)
                        silu(q["over_act"])

            def onehot(v, link, i, buf, sem_, width=E):
                spread = lambda m: m[:, :, ds(2 * i, 2)].rearrange("p t (s o) -> p t s o", o=1).to_broadcast([P, TT, 2, B])
                io = iotab[:, :].rearrange("p (t s b) -> p t s b", t=1, s=1).to_broadcast([P, TT, 2, B])
                link(nc.vector.tensor_tensor(SEL1[:, buf], spread(RKX), io, ALU.is_equal))
                link.sync()
                nc.vector.tensor_tensor(SELG[:, buf], SEL1[:, buf], spread(GX), ALU.mult).then_inc(sem_, 1)

            def hidden(sem_):
                nc.vector.tensor_tensor(HH[0:2 * B, :], SIL[0:2 * B, :], PS[0:2 * B, 4, FF:2 * FF],
                                        ALU.mult).then_inc(sem_, 1)

            def copy_hidden():
                return nc.vector.tensor_copy(HT[:, :, :].rearrange("p f b -> p (f b)"), PS[:, 4, 0:FT * 2 * B])

            def dve_pair(v, link, i, half, more, last):
                v.wait_ge(q["silu_ready"], i + 1 + past["silu_ready"])
                hidden(q["hidden_ready"])
                v.wait_ge(q["turned"], i + 1 + past["turned"])
                copy_hidden().then_inc(q["hidden_copied"], 1)
                if not last:
                    v.wait_ge(q["gathered0"], i + 2 + past["gathered0"])
                    copy_gathered(nc.vector.tensor_copy, 0).then_inc(q["gathered0_copied"], 1)
                if more:
                    onehot(v, link, i + 2, half, q["onehot_ready"])
                v.wait_ge(q["down1"], i + 1 + past["down1"])
                nc.vector.tensor_copy(Y[0:2 * B, 512:1024],
                                      PS[0:2 * B, 6 if last else 5, :]).then_inc(q["down1_copied"], 1)

            def dve_route(v, link):
                pair = lambda m: m[:, :, :].rearrange("p t e -> p (t e)")
                byg = lambda m: m[:, :, :].rearrange("p t (g e) -> p (t g) e", e=GE)
                v.wait_ge(q["scores_ready"], 1 + past["scores_ready"])
                link(nc.vector.tensor_tensor(BIA[:, :, :], SCO[:, :, :], EB[:, l:l + 1, :].to_broadcast([P, TT, E]),
                                             ALU.add))
                link.sync()
                for n in range(TT * NG):
                    link(nc.vector.max(top2[:, n, :], byg(BIA)[:, n, :]))
                link.sync()
                tg = grp[:, :, :].rearrange("p t g -> p (t g)")
                link(nc.vector.tensor_tensor(tg, top2[:, :, 0], top2[:, :, 1], ALU.add))
                link.sync()
                mine = grp[:, :, :].rearrange("p t (g o) -> p t g o", o=1).to_broadcast([P, TT, NG, NG])
                other = grp[:, :, :].rearrange("p t (o g) -> p t o g", o=1).to_broadcast([P, TT, NG, NG])
                tri = tri8[:, :, :].rearrange("p (o g) h -> p o g h", o=1).to_broadcast([P, TT, NG, NG])
                link(nc.vector.tensor_tensor(cmpa[:, :, :, :], other, mine, ALU.is_gt))
                link(nc.vector.tensor_tensor(cmpb[:, :, :, :], other, mine, ALU.is_equal))
                link.sync()
                link(nc.vector.tensor_tensor(cmpb[:, :, :, :], cmpb[:, :, :, :], tri, ALU.mult))
                link.sync()
                link(nc.vector.tensor_tensor(cmpa[:, :, :, :], cmpa[:, :, :, :], cmpb[:, :, :, :], ALU.add))
                link.sync()
                link(nc.vector.tensor_reduce(gcnt[:, :, :], cmpa[:, :, :, :], AX, ALU.add))
                link.sync()
                link(nc.vector.tensor_scalar(gcnt[:, :, :], gcnt[:, :, :], TOPG - 0.5, None, ALU.is_lt))
                link.sync()
                link(nc.vector.tensor_scalar(gpen[:, :, :], gcnt[:, :, :], BIG, -BIG, ALU.mult, ALU.add))
                wide = lambda m: m[:, :, :].rearrange("p t (g o) -> p (t g) o", o=1).to_broadcast([P, TT * NG, GE])
                link(nc.vector.tensor_tensor(byg(BIA), byg(BIA), wide(gcnt), ALU.mult))
                link.sync()
                link(nc.vector.tensor_tensor(byg(BIA), byg(BIA), wide(gpen), ALU.add))
                link.sync()
                for t in range(TT):
                    link(nc.vector.max(top8[:, t, :], BIA[:, t, :]))
                link.sync()
                for t in range(TT):
                    link(nc.vector.match_replace(REP[:, t, :], top8[:, t, :], BIA[:, t, :], -3.0 * BIG))
                link.sync()
                nc.vector.tensor_tensor(MSK[:, :, :], REP[:, :, :], BIA[:, :, :], ALU.not_equal).then_inc(q["mask_ready"], 1)
                v.wait_ge(q["mask_ready"], 1 + past["mask_ready"])
                link(nc.vector.tensor_tensor(SEL[:, :, :], SCO[:, :, :], MSK[:, :, :], ALU.mult))
                link.sync()
                link(nc.vector.tensor_reduce(gsum[:, :], SEL[:, :, :], AX, ALU.add))
                link.sync()
                link(nc.vector.reciprocal(gsum[:, :], gsum[:, :]))
                link.sync()
                for t in range(TT):
                    link(nc.vector.tensor_scalar(GX[:, t, 0:E], SEL[:, t, :], gsum[:, t:t + 1], 2.5, ALU.mult, ALU.mult))
                v.wait_ge(q["rank_done"], 1 + past["rank_done"])
                link(nc.vector.scalar_tensor_tensor(out=RKX[:, :, 0:E],
                                                    in0=PS[:, 4, 0:TT * E].rearrange("p (t e) -> p t e", t=TT), scalar=1.0,
                                                    in1=MSK[:, :, :], op0=ALU.add, op1=ALU.mult))
                link(nc.vector.tensor_reduce(cntf[0:1, 0:1], PS[0:1, 4, 2 * E:3 * E], AX, ALU.max))
                link(nc.vector.tensor_copy(CNT[:, :], PS[:, 4, 2 * E:3 * E]))
                link.sync()
                link(nc.vector.tensor_scalar(RKX[:, :, 0:E], RKX[:, :, 0:E], -1.0, None, ALU.add))
                link(nc.vector.tensor_copy(cnti[0:1, 2 * l:2 * l + 1], cntf[0:1, 0:1]))
                link.sync()
                v.sem_inc(q["rank_ready"], 1)
                v.sem_inc(q["count_ready"], 1)
                onehot(v, link, 0, 0, q["onehot_ready"])
                onehot(v, link, 1, 1, q["onehot_ready"])

            def dve_moe(v, link):
                dve_transpose_copy(v, st)
                dve_route(v, link)
                v.wait_ge(q["gathered0"], 1 + past["gathered0"])
                copy_gathered(nc.vector.tensor_copy, 0).then_inc(q["gathered0_copied"], 1)
                v.wait_ge(q["shared_silu"], 1 + past["shared_silu"])
                nc.vector.tensor_tensor(HS[:, :, :].rearrange("p f t -> p (f t)"),
                                        HSs[:, :, :].rearrange("p f t -> p (f t)"), PS[:, 0, :],
                                        ALU.mult).then_inc(q["shared_hidden"], 1)
                dve_pair(v, link, 0, 0, True, False)
                dve_pair(v, link, 1, 1, True, False)
                with v.Fori(1, PAIRS // 2 - 1) as i:
                    link.enter(i, 1, 2)
                    dve_pair(v, link, 2 * i, 0, True, False)
                    dve_pair(v, link, 2 * i + 1, 1, True, False)
                link.leave(PAIRS // 2 - 2)
                dve_pair(v, link, PAIRS - 2, 0, False, False)
                dve_pair(v, link, PAIRS - 1, 1, False, True)
                most = nc.vector.value_load(cnti[0:1, 2 * l:2 * l + 1], min_val=0, max_val=T)
                with v.If(most > B):
                    dve_over(v, Link(v, q["over_link"]))

            def dve_over(v, link):
                v.wait_ge(q["scattered"], PAIRS + past["scattered"])
                link(nc.vector.tensor_tensor(F2[0:E, :], ident[0:E, 0:E], CNT[0:E, :], ALU.mult))
                link.sync()
                link(nc.vector.tensor_reduce(cntf[0:E, 1:2], F2[0:E, :], AX, ALU.add))
                link.sync()
                link(nc.vector.tensor_scalar(F1[0:E, 0, :], thr[0:E, :], cntf[0:E, 1:2], None, ALU.is_lt))
                link(nc.vector.memset(F1[0:E, 1, 0:1], 0.0))
                link.sync()
                for r in range(1, NR):
                    link(nc.vector.tensor_tensor(F1[0:E, 1, r:r + 1], F1[0:E, 1, r - 1:r], F1[0:E, 0, r - 1:r], ALU.add))
                    link.sync()
                v.sem_inc(q["over_dve"], 1)
                v.wait_ge(q["over_pe"], 1)
                link(nc.vector.tensor_copy(F1[0:E, 2, :], PS[0:E, 4, 0:NR]))
                link.sync()
                wide = lambda m: m.rearrange("p (r o) -> p r o", o=1).to_broadcast([E, NR, NOV])
                link(nc.vector.tensor_tensor(OH[0:E, :, :],
                                             iotap[0:E, :].rearrange("p (o n) -> p o n", o=1).to_broadcast([E, NR, NOV]),
                                             wide(F1[0:E, 2, :]), ALU.is_equal))
                link.sync()
                link(nc.vector.tensor_tensor(OH[0:E, :, :], OH[0:E, :, :], wide(F1[0:E, 0, :]), ALU.mult))
                link.sync()
                link(nc.vector.tensor_reduce(OS[0:E, 0, :], OH[0:E, :, :].rearrange("p r n -> p n r"), AX, ALU.add))
                link.sync()
                link(nc.vector.tensor_tensor(OH[0:E, :, :], OH[0:E, :, :], wide(rbase[0:E, :]), ALU.mult))
                link.sync()
                link(nc.vector.tensor_reduce(OS[0:E, 1, :], OH[0:E, :, :].rearrange("p r n -> p n r"), AX, ALU.add))
                link.sync()
                v.sem_inc(q["over_dve"], 1)
                v.wait_ge(q["over_pe"], 2)
                link(nc.vector.tensor_copy(elist[0:1, :], PS[0:1, 5, 0:NOV]))
                link(nc.vector.tensor_reduce(cntf[0:1, 0:1], PS[0:1, 5, NOV:2 * NOV:2], AX, ALU.add))
                link(nc.vector.tensor_copy(TR4[0:E, :, :].rearrange("p m t -> p (m t)"), PS[0:E, 6, :]))
                link.sync()
                link(nc.vector.tensor_copy(cnti[0:1, 2 * l + 1:2 * l + 2], cntf[0:1, 0:1]))
                link.sync()
                v.sem_inc(q["over_dve"], 1)
                v.wait_ge(q["over_pe"], 3)
                link(nc.vector.tensor_scalar(RKX[:, :, E:E + NOV],
                                             PS[:, 7, 0:2 * NOV].rearrange("p (t n) -> p t n", t=TT), -1.0, None, ALU.add))
                link(nc.vector.tensor_copy(GX[:, :, E:E + NOV],
                                           PS[:, 7, 2 * NOV:4 * NOV].rearrange("p (t n) -> p t n", t=TT)))
                link.sync()
                v.sem_inc(q["over_dve"], 1)
                v.sem_inc(q["over_list"], 1)
                rounds = nc.vector.value_load(cnti[0:1, 2 * l + 1:2 * l + 2], min_val=1, max_val=NOV // 2)
                with v.Fori(0, rounds) as i:
                    link.enter(i, 0, 4)
                    v.wait_ge(q["over_free"], i + 1)
                    onehot(v, link, i + PAIRS, 0, q["over_dve"])
                    v.wait_ge(q["over_pe"], 5 * i + 4)
                    link(copy_gathered(nc.vector.tensor_copy, 0))
                    copy_gathered(nc.vector.tensor_copy, 1).then_inc(q["over_dve"], 1)
                    v.wait_ge(q["over_act"], i + 1)
                    hidden(q["over_dve"])
                    v.wait_ge(q["over_pe"], 5 * i + 6)
                    link(copy_hidden())
                    nc.vector.tensor_copy(GT[0:2 * B, :, :].rearrange("p t b -> p (t b)"),
                                          PS[0:2 * B, 4, T:2 * T]).then_inc(q["over_dve"], 1)
                    v.wait_ge(q["over_pe"], 5 * i + 7)
                    link(nc.vector.tensor_copy(Y[0:2 * B, 0:512], PS[0:2 * B, 5, :]))
                    nc.vector.tensor_copy(Y[0:2 * B, 512:1024], PS[0:2 * B, 6, :]).then_inc(q["over_dve"], 1)
                link.leave(NOV // 2)

            def gp_moe(g):
                part = lambda n: XB[:, n, :, :].rearrange("p t d -> p (t d)")
                for n in range(2):
                    g.wait_ge(q["x_part"], n + 1 + past["x_part"])
                    src = X[:, :, :].rearrange("p t d -> p (t d)") if n == 0 else XR
                    if n:
                        g.wait_ge(q["x_rest"], 1 + past["x_rest"])
                    nc.gpsimd.tensor_tensor(XR, src, part(n), ALU.subtract).then_inc(q["x_rest"], 1)

            return dict(load_expert=load_expert, prefetch=prefetch, loads=loads, pe=pe_moe, gp=gp_moe, act=act_moe, dve=dve_moe)

        moe = [moe_view(l) for l in range(2)]
        out_t = a["out"][0].rearrange("(t p) d -> p t d", p=P)

        with nc.Block() as block:
            @block.sync
            def _(sp):
                sp_mix0(sp)
                moe[0]["loads"](sp)
                sp_mix1(sp)
                moe[1]["loads"](sp)
                for t in range(TT):
                    sp.wait_ge(s_ln, TT * 3 + t + 1)
                    sp.dma_start(out_t[:, t, :], X[:, t, :]).then_inc(s_out, 16)
                sp.wait_ge(s_out, 16 * TT)

            @block.gpsimd
            def _(g):
                constants(g)
                gp_mix0(g)
                moe[0]["gp"](g)
                gp_mix1(g)
                moe[1]["gp"](g)

            @block.scalar
            def _(s):
                act_mix0(s)
                act_ln(s, 0)
                moe[0]["act"](s)
                act_ln(s, 1)
                act_mix1(s)
                act_ln(s, 2)
                moe[1]["act"](s)
                act_ln(s, 3)

            @block.vector
            def _(v):
                link = Link(v, s_dve)
                dve_mix0(v, link)
                layer_norm(v, link, 0)
                moe[0]["dve"](v, link)
                layer_norm(v, link, 1)
                dve_mix1(v, link)
                layer_norm(v, link, 2)
                moe[1]["dve"](v, link)
                layer_norm(v, link, 3)

            @block.tensor
            def _(pe):
                pe_mix0(pe)
                moe[0]["pe"](pe)
                pe_mix1(pe)
                moe[1]["pe"](pe)


_INS = ["x", "ln_mix_g", "ln_mix_b", "ln_ffn_g", "ln_ffn_b", "ab_w_in", "ab_pool_w", "ab_pool_scale", "ab_w_out",
        "rw_mu", "rw_w_r", "rw_w_k", "rw_w_v", "rw_w_w1", "rw_w_w2", "rw_w0", "rw_a1", "rw_a2", "rw_a0",
        "rw_g1", "rw_g2", "rw_k_k", "rw_k_a", "rw_r_k", "rw_lnx_g", "rw_lnx_b", "rw_w_o",
        "moe_w_router", "moe_e_bias", "moe_w_gate", "moe_w_up", "moe_w_down",
        "moe_ws_gate", "moe_ws_up", "moe_ws_down"]


def kernel(**inputs):
    import numpy as _np
    import concourse.bacc as _bacc
    from concourse import mybir as _mybir
    from concourse.bass_utils import run_bass_kernel_spmd as _run

    nc = _bacc.Bacc("TRN2", target_bir_lowering=False, num_devices=1)
    arrays, args = {}, {}
    for name in _INS:
        v = _np.ascontiguousarray(inputs[name])
        arrays[f"in_{name}"] = v
        args[name] = nc.dram_tensor(f"in_{name}", v.shape, _mybir.dt.from_np(v.dtype), kind="ExternalInput").ap()
    args["out"] = nc.dram_tensor("out_x", (1, T, D), F32, kind="ExternalOutput").ap()
    program(nc, args)
    r = _run(nc, [arrays], core_ids=[0])
    return r.results[0]["out_x"]
```
